# Optimizing a Trainium2 kernel written in Bass

```python
import math
import jax, jax.numpy as jnp
from jax import lax
import numpy as np

D_MODEL = 1024
BATCH = 1
SEQ = 256
DEPTH = 2

GRID_W = 64
CTX_LEN = 256
HEAD_DIM = 64
A_HEADS = 4
A_VDIM = 2 * HEAD_DIM
A_WIDTH = A_HEADS * A_VDIM
B_HEADS = 8
B_KV_HEADS = 2
B_REP = B_HEADS // B_KV_HEADS
B_WIDTH = B_HEADS * HEAD_DIM
A_Q_COLS = A_HEADS * 2 * HEAD_DIM
A_K_COLS = A_HEADS * 2 * HEAD_DIM
A_V_COLS = A_WIDTH
B_Q_COLS = B_HEADS * HEAD_DIM
B_K_COLS = B_KV_HEADS * HEAD_DIM
B_V_COLS = B_KV_HEADS * HEAD_DIM
IN_COLS = A_Q_COLS + A_K_COLS + A_V_COLS + B_Q_COLS + B_K_COLS + B_V_COLS
IN_SPLITS = (A_Q_COLS,
             A_Q_COLS + A_K_COLS,
             A_Q_COLS + A_K_COLS + A_V_COLS,
             A_Q_COLS + A_K_COLS + A_V_COLS + B_Q_COLS,
             A_Q_COLS + A_K_COLS + A_V_COLS + B_Q_COLS + B_K_COLS)
MIX_WIDTH = A_WIDTH + B_WIDTH
CONV_WIDTH = 3
MLP_HIDDEN = 4 * D_MODEL
ROPE_THETA = 10000.0
ROPE_FREQS = HEAD_DIM // 4
Q_BLOCK = 128
N_EVEN = (DEPTH + 1) // 2
N_ODD = DEPTH // 2
N_MOD = 6
DEEPNORM_ALPHA = (2 * DEPTH) ** 0.25
DEEPNORM_BETA = (8 * DEPTH) ** -0.25
EPS = 1e-6


def layer_norm(x, g, b):
    xf = x.astype(jnp.float32)
    mu = jnp.mean(xf, axis=-1, keepdims=True)
    var = jnp.mean(jnp.square(xf - mu), axis=-1, keepdims=True)
    return ((xf - mu) * lax.rsqrt(var + EPS) * g + b).astype(x.dtype)

def rms_norm(x, g):
    xf = x.astype(jnp.float32)
    return (xf * lax.rsqrt(jnp.mean(xf * xf, axis=-1, keepdims=True) + EPS) * g).astype(x.dtype)

def modulate(h, shift, scale):
    return h * (1.0 + scale) + shift

def rope_tables(n_tokens):
    rows = n_tokens // GRID_W
    row = jnp.broadcast_to(jnp.arange(rows)[:, None], (rows, GRID_W)).reshape(-1).astype(jnp.float32)
    col = jnp.broadcast_to(jnp.arange(GRID_W)[None, :], (rows, GRID_W)).reshape(-1).astype(jnp.float32)
    inv_freq = ROPE_THETA ** (-jnp.arange(ROPE_FREQS, dtype=jnp.float32) / ROPE_FREQS)
    ang = jnp.stack([row, col], axis=-1)[:, :, None] * inv_freq
    return jnp.cos(ang), jnp.sin(ang)

def apply_rope_2d(x, cos, sin):
    shp = x.shape
    xs = x.astype(jnp.float32).reshape(*shp[:-1], 2, 2, ROPE_FREQS)
    x1, x2 = xs[..., 0, :], xs[..., 1, :]
    n_head_axes = x.ndim - 3
    c = cos.reshape(cos.shape[0], *([1] * n_head_axes), 2, ROPE_FREQS)
    s = sin.reshape(sin.shape[0], *([1] * n_head_axes), 2, ROPE_FREQS)
    o1 = x1 * c - x2 * s
    o2 = x2 * c + x1 * s
    return jnp.stack([o1, o2], axis=-2).reshape(shp).astype(x.dtype)

def diff_attention(q, k, v, lam, lam_init, subln_g):
    s = jnp.einsum('bqhid,bkhid->bhiqk', q, k) * (HEAD_DIM ** -0.5)
    p = jax.nn.softmax(s.astype(jnp.float32), axis=-1)
    attn = (p[:, :, 0] - lam * p[:, :, 1]).astype(v.dtype)
    o = jnp.einsum('bhqk,bkhe->bqhe', attn, v)
    o = rms_norm(o, subln_g) * (1.0 - lam_init)
    return o.reshape(o.shape[0], o.shape[1], A_WIDTH)

def gqa_attention(q, k, v):
    bsz, nq = q.shape[0], q.shape[1]
    q = q.reshape(bsz, nq, B_KV_HEADS, B_REP, HEAD_DIM)
    s = jnp.einsum('bqgrd,bkgd->bgrqk', q, k) * (HEAD_DIM ** -0.5)
    p = jax.nn.softmax(s.astype(jnp.float32), axis=-1).astype(v.dtype)
    o = jnp.einsum('bgrqk,bkgd->bqgrd', p, v)
    return o.reshape(bsz, nq, B_WIDTH)

def even_mixer(h_lat, h_ctx, w_in, w_out, lam_vecs, subln_g, qn_g, kn_g, lam_init, cos, sin, ctx_out):
    bsz, n_lat = h_lat.shape[0], h_lat.shape[1]

    def project(h, use_rope):
        n = h.shape[1]
        z = h @ w_in
        aq, ak, av, bq, bk, bv = jnp.split(z, IN_SPLITS, axis=-1)
        aq = aq.reshape(bsz, n, A_HEADS, 2, HEAD_DIM)
        ak = ak.reshape(bsz, n, A_HEADS, 2, HEAD_DIM)
        av = av.reshape(bsz, n, A_HEADS, A_VDIM)
        bq = rms_norm(bq.reshape(bsz, n, B_HEADS, HEAD_DIM), qn_g)
        bk = rms_norm(bk.reshape(bsz, n, B_KV_HEADS, HEAD_DIM), kn_g)
        bv = bv.reshape(bsz, n, B_KV_HEADS, HEAD_DIM)
        if use_rope:
            aq = apply_rope_2d(aq, cos, sin)
            ak = apply_rope_2d(ak, cos, sin)
            bq = apply_rope_2d(bq, cos, sin)
            bk = apply_rope_2d(bk, cos, sin)
        return aq, ak, av, bq, bk, bv

    lv = lam_vecs.astype(jnp.float32)
    lam = jnp.exp(jnp.sum(lv[0] * lv[1])) - jnp.exp(jnp.sum(lv[2] * lv[3])) + lam_init

    caq, cak, cav, cbq, cbk, cbv = project(h_ctx, False)
    laq, lak, lav, lbq, lbk, lbv = project(h_lat, True)
    ak_all = jnp.concatenate([cak, lak], axis=1)
    av_all = jnp.concatenate([cav, lav], axis=1)
    bk_all = jnp.concatenate([cbk, lbk], axis=1)
    bv_all = jnp.concatenate([cbv, lbv], axis=1)

    nb = n_lat // Q_BLOCK

    def to_blocks(t):
        return jnp.moveaxis(t.reshape(bsz, nb, Q_BLOCK, *t.shape[2:]), 1, 0)

    def block(qs):
        qa, qb = qs
        return jnp.concatenate([diff_attention(qa, ak_all, av_all, lam, lam_init, subln_g),
                                gqa_attention(qb, bk_all, bv_all)], axis=-1)

    o = lax.map(block, (to_blocks(laq), to_blocks(lbq)))
    o = jnp.moveaxis(o, 0, 1).reshape(bsz, n_lat, MIX_WIDTH)
    y_lat = o @ w_out
    y_ctx = None
    if ctx_out:
        oc = jnp.concatenate([diff_attention(caq, cak, cav, lam, lam_init, subln_g),
                              gqa_attention(cbq, cbk, cbv)], axis=-1)
        y_ctx = oc @ w_out
    return y_lat, y_ctx

def conv_mixer(h, w_in, conv_w, conv_b, w_out):
    n = h.shape[1]
    z = h @ w_in
    gate_b, gate_c, xv = jnp.split(z, 3, axis=-1)
    u = gate_c * xv
    up = jnp.pad(u, ((0, 0), (1, 1), (0, 0)))
    y = up[:, :n] * conv_w[0] + up[:, 1:n + 1] * conv_w[1] + up[:, 2:n + 2] * conv_w[2] + conv_b
    return (gate_b * y) @ w_out

def sq_relu_mlp(h, w1, w2):
    return jnp.square(jax.nn.relu(h @ w1)) @ w2

def first_inputs(seed: int = 0) -> dict:
    key = jax.random.key(seed)
    ks = jax.random.split(key, 20)
    f32 = jnp.float32
    nrm = lambda k, shp: jax.random.normal(k, shp, f32)
    d = D_MODEL
    return {
        "x": nrm(ks[0], (BATCH, SEQ, d)),
        "c": nrm(ks[1], (BATCH, d)),
        "ctx": nrm(ks[2], (BATCH, CTX_LEN, d)),
        "c_ctx": nrm(ks[3], (d,)),
        "ada_w": nrm(ks[4], (DEPTH, d, N_MOD * d)) * (0.5 * d ** -0.5),
        "ada_b": nrm(ks[5], (DEPTH, N_MOD * d)) * 0.02,
        "attn_w_in": nrm(ks[6], (N_EVEN, d, IN_COLS)) * d ** -0.5,
        "attn_w_out": nrm(ks[7], (N_EVEN, MIX_WIDTH, d)) * (MIX_WIDTH ** -0.5 * DEEPNORM_BETA),
        "diff_lambda": nrm(ks[8], (N_EVEN, 4, HEAD_DIM)) * 0.1,
        "diff_subln_g": 1.0 + 0.02 * nrm(ks[9], (N_EVEN, A_VDIM)),
        "q_norm_g": 1.0 + 0.02 * nrm(ks[10], (N_EVEN, HEAD_DIM)),
        "k_norm_g": 1.0 + 0.02 * nrm(ks[11], (N_EVEN, HEAD_DIM)),
        "conv_w_in": nrm(ks[12], (N_ODD, d, 3 * d)) * d ** -0.5,
        "conv_w": nrm(ks[13], (N_ODD, CONV_WIDTH, d)) * CONV_WIDTH ** -0.5,
        "conv_b": nrm(ks[14], (N_ODD, d)) * 0.02,
        "conv_w_out": nrm(ks[15], (N_ODD, d, d)) * (d ** -0.5 * DEEPNORM_BETA),
        "mlp_w1": nrm(ks[16], (DEPTH, d, MLP_HIDDEN)) * d ** -0.5,
        "mlp_w2": nrm(ks[17], (DEPTH, MLP_HIDDEN, d)) * (MLP_HIDDEN ** -0.5 * DEEPNORM_BETA),
        "ln_g": 1.0 + 0.02 * nrm(ks[18], (DEPTH, 2, d)),
        "ln_b": 0.02 * nrm(ks[19], (DEPTH, 2, d)),
    }

def first_block(x, c, ctx, c_ctx, ada_w, ada_b, attn_w_in, attn_w_out, diff_lambda, diff_subln_g,
              q_norm_g, k_norm_g, conv_w_in, conv_w, conv_b, conv_w_out, mlp_w1, mlp_w2, ln_g, ln_b):
    n_lat = x.shape[1]
    cos, sin = rope_tables(n_lat)
    c_act = jax.nn.silu(c)
    cc_act = jax.nn.silu(c_ctx)
    x_ctx = ctx
    for l in range(DEPTH):
        even = (l % 2 == 0)
        ctx_out = any(j % 2 == 0 for j in range(l + 1, DEPTH))
        need_ctx = even or ctx_out
        mod = (c_act @ ada_w[l] + ada_b[l])[:, None, :]
        sh1, sc1, g1, sh2, sc2, g2 = jnp.split(mod, N_MOD, axis=-1)
        h = modulate(x, sh1, sc1)
        if need_ctx:
            mod_c = cc_act @ ada_w[l] + ada_b[l]
            csh1, csc1, cg1, csh2, csc2, cg2 = jnp.split(mod_c, N_MOD, axis=-1)
            hc = modulate(x_ctx, csh1, csc1)
        if even:
            e = l // 2
            lam_init = 0.8 - 0.6 * math.exp(-0.3 * l)
            y, yc = even_mixer(h, hc, attn_w_in[e], attn_w_out[e], diff_lambda[e], diff_subln_g[e],
                               q_norm_g[e], k_norm_g[e], lam_init, cos, sin, ctx_out)
        else:
            o = l // 2
            y = conv_mixer(h, conv_w_in[o], conv_w[o], conv_b[o], conv_w_out[o])
            yc = conv_mixer(hc, conv_w_in[o], conv_w[o], conv_b[o], conv_w_out[o]) if ctx_out else None
        x = layer_norm(DEEPNORM_ALPHA * x + g1 * y, ln_g[l, 0], ln_b[l, 0])
        h = modulate(x, sh2, sc2)
        x = layer_norm(DEEPNORM_ALPHA * x + g2 * sq_relu_mlp(h, mlp_w1[l], mlp_w2[l]), ln_g[l, 1], ln_b[l, 1])
        if ctx_out:
            x_ctx = layer_norm(DEEPNORM_ALPHA * x_ctx + cg1 * yc, ln_g[l, 0], ln_b[l, 0])
            hc = modulate(x_ctx, csh2, csc2)
            x_ctx = layer_norm(DEEPNORM_ALPHA * x_ctx + cg2 * sq_relu_mlp(hc, mlp_w1[l], mlp_w2[l]),
                               ln_g[l, 1], ln_b[l, 1])
    return x


DEPTH_2 = 1

RET_HEADS = 8
RET_QK_DIM = 64
RET_V_DIM = 128
RET_CHUNK = 128
ROPE_BASE = 10000.0

MOBA_HEADS = 8
MOBA_HEAD_DIM = 64
MOBA_BLOCK = 256
MOBA_TOPK = 3
MOBA_Q_CHUNK = 32

REL_BUCKETS = 32
REL_MAX_DIST = 2048

PEER_HEADS = 8
PEER_N_KEYS = 128
PEER_N_EXPERTS = PEER_N_KEYS * PEER_N_KEYS
PEER_QUERY_DIM = 256
PEER_TOPK = 16
PEER_TOKEN_CHUNK = 128

NORM_EPS = 1e-6
NEG_INF = -1e30

RET_QK_W = RET_HEADS * RET_QK_DIM
RET_V_W = RET_HEADS * RET_V_DIM
MOBA_W = MOBA_HEADS * MOBA_HEAD_DIM
IN_SIZES = (RET_QK_W, RET_QK_W, RET_V_W, RET_V_W, MOBA_W, MOBA_W, MOBA_W, D_MODEL, D_MODEL)
IN_WIDTH = sum(IN_SIZES)


def rmsnorm(x, g):
    xf = x.astype(jnp.float32)
    y = xf * lax.rsqrt(jnp.mean(xf * xf, axis=-1, keepdims=True) + NORM_EPS)
    return (y * g.astype(jnp.float32)).astype(x.dtype)

def to_heads(t, n_heads):
    b, s, _ = t.shape
    return t.reshape(b, s, n_heads, -1).transpose(0, 2, 1, 3)

def from_heads(t):
    b, h, s, d = t.shape
    return t.transpose(0, 2, 1, 3).reshape(b, s, h * d)

def rotary(x, pos):
    half = x.shape[-1] // 2
    inv = ROPE_BASE ** (-jnp.arange(half, dtype=jnp.float32) / half)
    ang = pos.astype(jnp.float32)[:, None] * inv[None, :]
    cos, sin = jnp.cos(ang), jnp.sin(ang)
    x1, x2 = x[..., :half], x[..., half:]
    return jnp.concatenate([x1 * cos - x2 * sin, x1 * sin + x2 * cos], axis=-1).astype(x.dtype)

def retention(q, k, v):
    B, H, S, dk = q.shape
    dv = v.shape[-1]
    C = RET_CHUNK
    n = S // C
    log_g = jnp.log1p(-jnp.exp2(-5.0 - jnp.arange(H, dtype=jnp.float32)))
    idx = jnp.arange(C, dtype=jnp.float32)
    rel = idx[:, None] - idx[None, :]
    decay_in = jnp.where(rel[None] >= 0, jnp.exp(jnp.maximum(rel, 0.0)[None] * log_g[:, None, None]), 0.0)
    qc = q.reshape(B, H, n, C, dk)
    kc = k.reshape(B, H, n, C, dk)
    vc = v.reshape(B, H, n, C, dv)
    scores = jnp.einsum('bhnid,bhnjd->bhnij', qc, kc) * decay_in[None, :, None]
    o_in = jnp.einsum('bhnij,bhnje->bhnie', scores, vc)
    k_dec = kc * jnp.exp((C - 1 - idx)[None, :] * log_g[:, None])[None, :, None, :, None]
    kv = jnp.einsum('bhncd,bhnce->bhnde', k_dec, vc)
    chunk_decay = jnp.exp(C * log_g)[None, :, None, None]

    def step(state, kv_n):
        return state * chunk_decay + kv_n, state

    state0 = jnp.zeros((B, H, dk, dv), kv.dtype)
    _, prev = lax.scan(step, state0, jnp.moveaxis(kv, 2, 0))
    prev = jnp.moveaxis(prev, 0, 2)
    q_dec = jnp.exp((idx + 1.0)[None, :] * log_g[:, None])
    o_cross = jnp.einsum('bhncd,bhnde->bhnce', qc, prev) * q_dec[None, :, None, :, None]
    o = (o_in + o_cross).reshape(B, H, S, dv).astype(jnp.float32)
    mu = jnp.mean(o, axis=-1, keepdims=True)
    var = jnp.mean(jnp.square(o - mu), axis=-1, keepdims=True)
    return ((o - mu) * lax.rsqrt(var + NORM_EPS)).astype(q.dtype)

def head_rmsnorm(t, g):
    tf = t.astype(jnp.float32)
    y = tf * lax.rsqrt(jnp.mean(tf * tf, axis=-1, keepdims=True) + NORM_EPS)
    return (y * g.astype(jnp.float32)).astype(t.dtype)

def rel_bucket(dist):
    max_exact = REL_BUCKETS // 2
    n = jnp.maximum(dist, 0)
    nf = jnp.maximum(n, 1).astype(jnp.float32)
    large = max_exact + (jnp.log(nf / max_exact) / math.log(REL_MAX_DIST / max_exact)
                         * (REL_BUCKETS - max_exact)).astype(jnp.int32)
    large = jnp.minimum(large, REL_BUCKETS - 1)
    return jnp.where(n < max_exact, n, large)

def moba_attention(q, k, v, rel_bias):
    B, H, S, dh = q.shape
    L = MOBA_BLOCK
    n_blk = -(-S // L)
    s_pad = n_blk * L
    pad = ((0, 0), (0, 0), (0, s_pad - S), (0, 0))
    k_pad = jnp.pad(k, pad)
    v_pad = jnp.pad(v, pad)
    k_blocks = k_pad.reshape(B, H, n_blk, L, dh)
    v_blocks = v_pad.reshape(B, H, n_blk, L, dh)
    k_mean = jnp.mean(k_blocks.astype(jnp.float32), axis=3)
    n_sel = min(MOBA_TOPK, n_blk)
    Qc = MOBA_Q_CHUNK
    n_qc = S // Qc
    q_chunks = jnp.moveaxis(q.reshape(B, H, n_qc, Qc, dh), 2, 0)
    bias_hb = rel_bias.T.astype(jnp.float32)
    b_idx = jnp.arange(B)[:, None, None, None]
    h_idx = jnp.arange(H)[None, :, None, None]
    h_idx5 = jnp.arange(H)[None, :, None, None, None]
    offs = jnp.arange(L)
    blk_ids = jnp.arange(n_blk)

    def one_chunk(args):
        qc, c = args
        q_start = c * Qc
        blk = q_start // L
        qpos = q_start + jnp.arange(Qc)
        gate = jnp.einsum('bhqd,bhnd->bhqn', qc.astype(jnp.float32), k_mean)
        gate = jnp.where(blk_ids < blk, gate, NEG_INF)
        _, sel = lax.top_k(gate, n_sel)
        valid = sel < blk
        k_sel = k_blocks[b_idx, h_idx, sel]
        v_sel = v_blocks[b_idx, h_idx, sel]
        kpos_sel = sel[..., None] * L + offs
        bias_sel = bias_hb[h_idx5, rel_bucket(qpos[None, None, :, None, None] - kpos_sel)]
        logit_sel = jnp.einsum('bhqd,bhqnkd->bhqnk', qc, k_sel).astype(jnp.float32) + bias_sel
        logit_sel = jnp.where(valid[..., None], logit_sel, NEG_INF).reshape(B, H, Qc, n_sel * L)
        k_own = lax.dynamic_slice_in_dim(k_pad, blk * L, L, axis=2)
        v_own = lax.dynamic_slice_in_dim(v_pad, blk * L, L, axis=2)
        dist_own = qpos[:, None] - (blk * L + offs)[None, :]
        bias_own = bias_hb[:, rel_bucket(dist_own)]
        logit_own = jnp.einsum('bhqd,bhkd->bhqk', qc, k_own).astype(jnp.float32) + bias_own[None]
        logit_own = jnp.where(dist_own >= 0, logit_own, NEG_INF)
        p = jax.nn.softmax(jnp.concatenate([logit_sel, logit_own], axis=-1), axis=-1)
        p_sel = p[..., :n_sel * L].reshape(B, H, Qc, n_sel, L).astype(v.dtype)
        p_own = p[..., n_sel * L:].astype(v.dtype)
        return (jnp.einsum('bhqnk,bhqnkd->bhqd', p_sel, v_sel)
                + jnp.einsum('bhqk,bhkd->bhqd', p_own, v_own))

    out = lax.map(one_chunk, (q_chunks, jnp.arange(n_qc)))
    return jnp.moveaxis(out, 0, 2).reshape(B, H, S, dh)

def peer(h, w_q, sub_keys, u_tab, v_tab):
    B, S, D = h.shape
    T = B * S
    ht = h.reshape(T, D)
    half = PEER_QUERY_DIM // 2
    q = (ht @ w_q).reshape(T, PEER_HEADS, 2, half)
    s = jnp.einsum('thcd,hcnd->thcn', q, sub_keys).astype(jnp.float32)
    s1, i1 = lax.top_k(s[:, :, 0], PEER_TOPK)
    s2, i2 = lax.top_k(s[:, :, 1], PEER_TOPK)
    cand_s = (s1[..., :, None] + s2[..., None, :]).reshape(T, PEER_HEADS, PEER_TOPK * PEER_TOPK)
    cand_i = (i1[..., :, None] * PEER_N_KEYS + i2[..., None, :]).reshape(T, PEER_HEADS, PEER_TOPK * PEER_TOPK)
    top_s, pos = lax.top_k(cand_s, PEER_TOPK)
    experts = jnp.take_along_axis(cand_i, pos, axis=-1)
    gates = jax.nn.softmax(top_s, axis=-1).astype(h.dtype)
    Pc = PEER_TOKEN_CHUNK
    n_c = T // Pc

    def one_chunk(args):
        hc, ec, gc = args
        u = u_tab[ec]
        a = jax.nn.gelu(jnp.einsum('td,thkd->thk', hc, u), approximate=False)
        return jnp.einsum('thk,thkd->td', gc * a, v_tab[ec])

    out = lax.map(one_chunk, (ht.reshape(n_c, Pc, D),
                              experts.reshape(n_c, Pc, PEER_HEADS, PEER_TOPK),
                              gates.reshape(n_c, Pc, PEER_HEADS, PEER_TOPK)))
    return out.reshape(B, S, D)

def second_inputs(seed: int = 0) -> dict:
    key = jax.random.key(seed)
    ks = jax.random.split(key, 14)
    f32 = jnp.float32
    nrm = lambda k, shape, scale: jax.random.normal(k, shape, f32) * scale
    return {
        "x": nrm(ks[0], (BATCH, SEQ, D_MODEL), 1.0),
        "mix_norm_g": 1.0 + nrm(ks[1], (DEPTH_2, D_MODEL), 0.1),
        "w_in": nrm(ks[2], (DEPTH_2, D_MODEL, IN_WIDTH), D_MODEL ** -0.5),
        "ret_w_branch": nrm(ks[3], (DEPTH_2, RET_V_W, D_MODEL), RET_V_W ** -0.5),
        "moba_q_gain": 1.0 + nrm(ks[4], (DEPTH_2, MOBA_HEAD_DIM), 0.1),
        "moba_k_gain": 1.0 + nrm(ks[5], (DEPTH_2, MOBA_HEAD_DIM), 0.1),
        "moba_w_branch": nrm(ks[6], (DEPTH_2, MOBA_W, D_MODEL), MOBA_W ** -0.5),
        "rel_bias": nrm(ks[7], (REL_BUCKETS, MOBA_HEADS), 0.5),
        "w_out": nrm(ks[8], (DEPTH_2, D_MODEL, D_MODEL), D_MODEL ** -0.5),
        "ffn_norm_g": 1.0 + nrm(ks[9], (DEPTH_2, D_MODEL), 0.1),
        "peer_w_q": nrm(ks[10], (DEPTH_2, D_MODEL, PEER_HEADS * PEER_QUERY_DIM), D_MODEL ** -0.5),
        "peer_sub_keys": nrm(ks[11], (DEPTH_2, PEER_HEADS, 2, PEER_N_KEYS, PEER_QUERY_DIM // 2), (PEER_QUERY_DIM // 2) ** -0.5),
        "peer_u": nrm(ks[12], (DEPTH_2, PEER_N_EXPERTS, D_MODEL), D_MODEL ** -0.5),
        "peer_v": nrm(ks[13], (DEPTH_2, PEER_N_EXPERTS, D_MODEL), D_MODEL ** -0.5),
    }

def second_block(x, mix_norm_g, w_in, ret_w_branch, moba_q_gain, moba_k_gain, moba_w_branch,
              rel_bias, w_out, ffn_norm_g, peer_w_q, peer_sub_keys, peer_u, peer_v):
    B, S, D = x.shape
    pos = jnp.arange(S)
    offsets = tuple(int(o) for o in np.cumsum(IN_SIZES)[:-1])
    for l in range(DEPTH_2):
        h = rmsnorm(x, mix_norm_g[l])
        proj = h @ w_in[l]
        rq, rk, rv, rg, mq, mk, mv, ga, gb = jnp.split(proj, offsets, axis=-1)
        rq = rotary(to_heads(rq, RET_HEADS), pos)
        rk = rotary(to_heads(rk, RET_HEADS), pos) * (RET_QK_DIM ** -0.5)
        ret = retention(rq, rk, to_heads(rv, RET_HEADS))
        y_a = (from_heads(ret) * jax.nn.silu(rg)) @ ret_w_branch[l]
        mq = head_rmsnorm(to_heads(mq, MOBA_HEADS), moba_q_gain[l]) * (MOBA_HEAD_DIM ** -0.5)
        mk = head_rmsnorm(to_heads(mk, MOBA_HEADS), moba_k_gain[l])
        att = moba_attention(mq, mk, to_heads(mv, MOBA_HEADS), rel_bias)
        y_b = from_heads(att) @ moba_w_branch[l]
        merged = jax.nn.sigmoid(ga) * y_a + jax.nn.sigmoid(gb) * y_b
        x = x + merged @ w_out[l]
        h2 = rmsnorm(x, ffn_norm_g[l])
        x = x + peer(h2, peer_w_q[l], peer_sub_keys[l], peer_u[l], peer_v[l])
    return x


def setup_inputs(seed=0):
    out = dict(first_inputs(seed))
    for name, value in second_inputs(seed + 1).items():
        if name != "x":
            out[name + "_2"] = value
    return out


def reference(
    x, c, ctx, c_ctx, ada_w, ada_b, attn_w_in, attn_w_out, diff_lambda, diff_subln_g, q_norm_g,
    k_norm_g, conv_w_in, conv_w, conv_b, conv_w_out, mlp_w1, mlp_w2, ln_g, ln_b, mix_norm_g_2,
    w_in_2, ret_w_branch_2, moba_q_gain_2, moba_k_gain_2, moba_w_branch_2, rel_bias_2, w_out_2,
    ffn_norm_g_2, peer_w_q_2, peer_sub_keys_2, peer_u_2, peer_v_2,
):
    x = first_block(
        x, c, ctx, c_ctx, ada_w, ada_b, attn_w_in, attn_w_out, diff_lambda, diff_subln_g,
        q_norm_g, k_norm_g, conv_w_in, conv_w, conv_b, conv_w_out, mlp_w1, mlp_w2, ln_g, ln_b,
    )
    return second_block(
        x, mix_norm_g_2, w_in_2, ret_w_branch_2, moba_q_gain_2, moba_k_gain_2, moba_w_branch_2,
        rel_bias_2, w_out_2, ffn_norm_g_2, peer_w_q_2, peer_sub_keys_2, peer_u_2, peer_v_2,
    )


_drawn_inputs = setup_inputs


def setup_inputs(seed=0):
    import zlib

    import numpy as np

    out = dict(_drawn_inputs(seed))
    spreads = {}
    factors = {'diff_lambda': 8.0,
     'diff_subln_g': 8.0,
     'q_norm_g': 8.0,
     'k_norm_g': 8.0,
     'conv_b': 8.0,
     'moba_q_gain_2': 5.832,
     'moba_k_gain_2': 4.59,
     'ffn_norm_g_2': 8.0,
     'peer_w_q_2': 3.982,
     'peer_sub_keys_2': 3.956,
     'peer_u_2': 4.364,
     'peer_v_2': 3.966}
    for name, (base, spread) in spreads.items():
        noise = np.random.default_rng([zlib.crc32(name.encode()), seed]).standard_normal(out[name].shape)
        drawn = base * np.exp(spread * noise) if base else spread * noise
        out[name] = __import__('jax').numpy.asarray(drawn.astype(out[name].dtype))
    for name, factor in factors.items():
        out[name] = (out[name] * factor).astype(out[name].dtype)
    return out
```

```python
from contextlib import ExitStack, contextmanager

import numpy as np

import concourse.bass as bass
from concourse import mybir

F32 = mybir.dt.float32
U32 = mybir.dt.uint32
ALU = mybir.AluOpType
ACT = mybir.ActivationFunctionType
AX_X = mybir.AxisListType.X

P = 128
T = 256
D = 1024
KC = D // P
RING = 8
UNIT = 1024
ALPHA = 4.0 ** 0.25
LAM_INIT = 0.2
EPS = 1e-6
HEAD = 64
SCALE = HEAD ** -0.5
N_EXP = 128
TOPK = 16
HID_TILES = 4 * D // P
MASKED = -1e30
TAKEN = -3.0e38

ADA_UNITS = 48
STAGES = [("ada0", ADA_UNITS), ("ada1", ADA_UNITS), ("attn_in", 18), ("attn_out", 8), ("mlp0", 64),
          ("conv_in", 24), ("conv_out", 8), ("mlp1", 64), ("in2_qk", 16), ("in2_v", 12), ("in2_gates", 24),
          ("ret_out", 8), ("moba_out", 4), ("out2", 8), ("peer_q", 16), ("peer_keys", 2),
          ("peer_u", N_EXP), ("peer_v", N_EXP)]
FIRST_UNIT = {}
N_UNITS = 0
for _name, _n in STAGES:
    FIRST_UNIT[_name] = N_UNITS
    N_UNITS += _n

PARAM = {}
N_PARAM = 0
for _name, _n in (("c", 16), ("ada_b0", 48), ("ada_b1", 48), ("ln_g", 32), ("ln_b", 32), ("mix_g", 8),
                  ("ffn_g", 8), ("conv_w", 24), ("conv_b", 8), ("subln_g", 1), ("qn_g", 1), ("kn_g", 1),
                  ("mq_g", 1), ("mk_g", 1)):
    PARAM[_name] = N_PARAM
    N_PARAM += _n

CONST = {}
N_CONST = 0
for _name, _n in (("ident", P), ("mean_d", P), ("mean_64", P), ("mean_128", P), ("rot_2d", P), ("rot_1d", P),
                  ("iota", P), ("iota16", TOPK), ("cos_2d", T), ("sin_2d", T), ("cos_1d", T), ("sin_1d", T)):
    CONST[_name] = N_CONST
    N_CONST += _n
DIST = 384
DEC = 384

SH1, SC1, G1, SH2, SC2, G2 = range(0, 48, 8)


class Count:

    def __init__(self):
        self.n, self.i, self.per = 0, None, 0

    def add(self, k=1):
        self.n += k
        return self.now()

    def now(self):
        return self.n if self.i is None else self.i * self.per + self.n


@contextmanager
def rolled(eng, trips, counts):
    was = {c: c.n for c, _ in counts}
    with eng.Fori(0, trips) as i:
        for c, per in counts:
            c.i, c.per = i, per
        yield i
        for c, per in counts:
            assert c.n - was[c] == per, (c.n, was[c], per)
    for c, per in counts:
        c.i, c.n = None, was[c] + per * trips


def build(nc, stream, x_t, ctx_t, params, consts, decay, lam_in, rel_bias, onehot, dist_mask, bias_rows, out):
    with ExitStack() as ctx:
        def sb(name, shape, dt=F32):
            return ctx.enter_context(nc.sbuf_tensor(name, shape, dt))

        def sem(name):
            return ctx.enter_context(nc.semaphore(name))

        ring = sb("ring", [P, RING, UNIT])
        arena = sb("arena", [P, N_EXP * T])
        late = sb("late", [P, 4096])
        resid = sb("resid", [P, KC, T])
        h = sb("h", [P, KC, T])
        par = sb("par", [P, N_PARAM])
        cst = sb("cst", [P, N_CONST])
        mod = [sb(f"mod{l}", [P, 48, 2]) for l in range(2)]
        cact = sb("cact", [P, KC, 2])
        small = sb("small", [P, 160])

        def param(name, k=0, n=1):
            a = PARAM[name] + k
            return par[:, a:a + n]

        def const(name, n=P):
            return cst[:, CONST[name]:CONST[name] + n]

        def area(at, *shape):
            size = int(np.prod(shape))
            a = arena[:, at:at + size]
            if len(shape) == 2:
                a = a.rearrange("p (a b) -> p a b", b=shape[1])
            if len(shape) == 3:
                a = a.rearrange("p (a b c) -> p a b c", b=shape[1], c=shape[2])
            return a

        branch = area(19456, KC, T)
        z = area(21504, KC, T)
        sq = area(23552, KC, T)
        zc = area(25600, KC, T)
        rope_a = area(27648, 2, T)
        rope_b = area(28160, 2, T)
        hid = area(28672, 2, T)
        hid2 = area(29184, 2, T)
        vare = area(29696, 2, 512)
        rstd = area(30720, 2, 512)
        hcat = area(0, KC, 2 * T)
        zq = area(4096, 8, T)
        zk = area(6144, 5, 2 * T)
        av = area(8704, 4, 512)
        bv = area(10752, 4, P)
        pexp = area(11264, 4, 512)
        attn = area(13312, 2, 512)
        attn_t = area(14336, 2, 4, T)
        o_a = area(16384, 4, T)
        mix = area(17408, 8, T)
        conv_z = area(0, 24, T)
        conv_u = area(6144, KC, T + 2)
        conv_y = area(8208, KC, T)
        zz = area(0, 40, T)
        rv = area(10240, 2, D)
        mv = area(12288, 2, 512)
        dec = area(13312, 8, DEC)
        ret = area(16384, 8, T)
        att = area(18432, 4, T)
        sdec = area(31744, 2, DEC)
        m_s = area(27648, 2, T)
        m_exp = area(28160, 2, T)
        m_attn = area(28672, 2, T)
        m_attn_t = area(11264, 2, 2, T)
        y_a, y_b = area(0, KC, T), area(2048, KC, T)
        merged = area(10240, KC, T)
        qp = area(0, 16, T)
        act_e = area(0, N_EXP, T)
        QUARTER = 3 * N_EXP * T // 4
        sco = area(QUARTER, 2, 16, P)
        cand = area(QUARTER + 4096, 8, TOPK * TOPK)
        hot = area(QUARTER + 6144, P, TOPK)
        mod_row = late[:, 2048:3072].rearrange("p (b n) -> p b n", b=2)
        bias = late[:, 0:2048].rearrange("p (h k) -> p h k", h=8)
        rowbuf = late[:, 3072:3072 + DIST]
        relb = late[:, 3456:3464]
        lamb = late[:, 3464:3720].rearrange("p (a n) -> p a n", a=4)
        lamw = late[:, 3720:3848].rearrange("p (a n) -> p a n", a=2)
        dmask = late[:, 2048:2048 + DIST]
        oneh = late[:, 2432:2432 + DIST]
        i1_t, i2_t, gate_t = late[:, 0:256], late[:, 256:512], late[:, 512:768]
        hot1 = late[:, 768:1792].rearrange("p (b t n) -> p b t n", b=2, t=4)
        hot2 = late[:, 1792:2816].rearrange("p (b t n) -> p b t n", b=2, t=4)
        top_v = late[:, 2816:3072].rearrange("p (h c k) -> p h c k", h=8, c=2)
        top_i = late[:, 3072:3328].rearrange("p (h c k) -> p h c k", h=8, c=2)
        top_iu = late[:, 3328:3584].bitcast(U32).rearrange("p (h k) -> p h k", h=16)
        best_v = late[:, 3584:3712].rearrange("p (h k) -> p h k", h=8)
        best_u = late[:, 3712:3840].bitcast(U32)
        pick_u = late[:, 3840:3968].bitcast(U32)
        pick = late[:, 3968:4096]
        found = [cst[:, CONST["cos_2d"] + 384 * i:CONST["cos_2d"] + 384 * (i + 1)].rearrange("p (a n) -> p a n", a=3) for i in range(2)]

        i2_now = cst[:, CONST["cos_2d"] + 768:CONST["cos_2d"] + 776].rearrange("p (b t) -> p b t", b=2)
        nmax, sums, inv = small[:, 0:32], small[:, 32:64], small[:, 64:96]
        lam2, nlam, gsub = small[:, 96:98], small[:, 98:99], small[:, 99:100]
        mqg = small[:, 100:101]
        sc1p = small[:, 104:120].rearrange("p (k c) -> p k c", c=2)
        gs, bs = small[:, 120:128], small[:, 128:136]
        ga_, ba_ = small[:, 136:144], small[:, 144:152]
        exps = small[:, 152:160]

        ps = ctx.enter_context(nc.psum_tensor("ps", [P, 8, 512], F32))

        landed = [sem(f"landed{s}") for s in range(RING)]
        units_begun = sem("units_begun")
        full = [sem(f"full{b}") for b in range(8)]
        emptied = [sem(f"emptied{b}") for b in range(8)]
        inputs = sem("inputs")
        bias_in = sem("bias_in")
        cact_ready = sem("cact_ready")
        h_dve = sem("h_dve")
        h_act = sem("h_act")
        dve_step = sem("dve_step")
        act_step = sem("act_step")
        squared = sem("squared")
        var_ready = sem("var_ready")
        std_ready = sem("std_ready")
        centred = sem("centred")
        normed = sem("normed")
        summed = sem("summed")
        roped = sem("roped")
        qk_ready = sem("qk_ready")
        nmax_ready = sem("nmax_ready")
        exp_ready = sem("exp_ready")
        attn_ready = sem("attn_ready")
        mix_ready = sem("mix_ready")
        o_ready = sem("o_ready")
        hid_ready = sem("hid_ready")
        lam_sum = sem("lam_sum")
        mod_cols = sem("mod_cols")
        row_ready = sem("row_ready")
        row_out = sem("row_out")
        dec_in = sem("dec_in")
        block1_done = sem("block1_done")
        sdec_ready = sem("sdec_ready")
        topk_done = sem("topk_done")
        half_found = sem("half_found")
        hot1_ready = sem("hot1_ready")
        hot2_ready = sem("hot2_ready")
        gated = sem("gated")
        final = sem("final")
        stored = sem("stored")
        pool_step = sem("pool_step")
        i2_copied = sem("i2_copied")
        gate_exp = sem("gate_exp")

        mark = {}

        block = ctx.enter_context(nc.Block())

        @block.tensor
        def _(pe):
            fills = [Count() for _ in range(8)]
            n_h = Count()
            n_centred, n_squared, n_summed = Count(), Count(), Count()

            def start_fill(b):
                if fills[b].i is not None:
                    assert fills[b].n > 0
                if fills[b].n:
                    pe.wait_ge(emptied[b], fills[b].now())

            def unit(u, i=None, rounds=1):
                s = u % RING
                value = 16 * (u // RING + 1)
                pe.wait_ge(landed[s], value if i is None else i * (16 * rounds) + value)
                return ring[:, s, :]

            def k_tile(u, rhs, bank, i=None, rounds=1):
                w = unit(u, i, rounds)
                start_fill(bank)
                for kc in range(KC):
                    r = rhs(kc)
                    n = r.shape[-1]
                    m = pe.matmul(ps[:, bank, 0:n], w[:, kc * P:(kc + 1) * P], r, start=kc == 0, stop=kc == KC - 1)
                    if kc == 0:
                        m.then_inc(units_begun, 1)
                m.then_inc(full[bank], 1)
                fills[bank].add()

            def ones_sum(name, src, bank, n):
                start_fill(bank)
                for k in range(n):
                    r = src(k)
                    m = pe.matmul(ps[:, bank, 0:r.shape[-1]], const(name), r, start=k == 0, stop=k == n - 1)
                m.then_inc(full[bank], 1)
                fills[bank].add()

            def one(bank, lhs, rhs, shape):
                start_fill(bank)
                pe.matmul(shape, lhs, rhs, start=True, stop=True).then_inc(full[bank], 1)
                fills[bank].add()

            def wait_h():
                pe.wait_ge(h_dve, n_h.add())
                pe.wait_ge(h_act, n_h.now())

            pe.wait_ge(inputs, 16 * 8)
            one(7, relb[0:32, 0:8], oneh[0:32, :], ps[0:8, 7, 0:DIST])

            pe.wait_ge(cact_ready, 1)
            def ada_rows(u, i=None):
                for g in range(2):
                    start_fill(4 + g)
                    for k4 in range(4):
                        w = unit(u + 4 * g + k4, i)
                        for k2 in range(2):
                            kc = 2 * k4 + k2
                            m = pe.matmul(ps[0:2, 4 + g, :], cact[:, kc, :], w[:, k2 * 512:(k2 + 1) * 512],
                                          start=kc == 0, stop=kc == KC - 1)
                            if k2 == 0:
                                m.then_inc(units_begun, 1)
                    m.then_inc(full[4 + g], 1)
                    fills[4 + g].add()
                for g in range(2):
                    pe.wait_ge(emptied[4 + g], fills[4 + g].now())
                    start_fill(6 + g)
                    for q in range(4):
                        m = pe.matmul(ps[:, 6 + g, 2 * q:2 * q + 2], mod_row[0:2, g, q * P:(q + 1) * P],
                                      const("ident")[0:2, 0:2], start=True, stop=True)
                    m.then_inc(full[6 + g], 1)
                    fills[6 + g].add()

            ada_rows(FIRST_UNIT["ada0"])
            with rolled(pe, ADA_UNITS // 8 - 1, [(fills[b], 1) for b in (4, 5, 6, 7)]) as i:
                ada_rows(FIRST_UNIT["ada0"] + 8, i)
            with rolled(pe, ADA_UNITS // 8, [(fills[b], 1) for b in (4, 5, 6, 7)]) as i:
                ada_rows(FIRST_UNIT["ada1"], i)

            def projections(src, wide):
                u = FIRST_UNIT["attn_in"]
                tile = 0
                for _ in range(8):
                    k_tile(u, lambda kc: hcat[:, kc, T:2 * T], 4 + tile % 2)
                    u, tile = u + 1, tile + 1
                for _ in range(4):
                    k_tile(u, lambda kc: hcat[:, kc, :], 4 + tile % 2)
                    u, tile = u + 1, tile + 1
                v_units(u, 4, lambda kc, tt: hcat[:, kc, tt * P:(tt + 1) * P], 4)
                u += 4
                k_tile(u, lambda kc: hcat[:, kc, :], 4 + tile % 2)
                w = unit(u + 1)
                start_fill(6)
                for tt in range(4):
                    for kc in range(KC):
                        m = pe.matmul(ps[:, 6, tt * P:(tt + 1) * P], hcat[:, kc, tt * P:(tt + 1) * P],
                                      w[:, kc * P:(kc + 1) * P], start=kc == 0, stop=kc == KC - 1)
                        if tt == 0 and kc == 0:
                            m.then_inc(units_begun, 1)
                m.then_inc(full[6], 1)
                fills[6].add()

            def v_units(u, n_units, lhs, n_tok):
                for tt in range(n_tok):
                    start_fill(tt)
                for k4 in range(4):
                    w = unit(u + k4)
                    for k2 in range(2):
                        kc = 2 * k4 + k2
                        for tt in range(n_tok):
                            m = pe.matmul(ps[:, tt, :], lhs(kc, tt), w[:, k2 * 512:(k2 + 1) * 512],
                                          start=kc == 0, stop=kc == KC - 1)
                            if k2 == 0 and tt == 0:
                                m.then_inc(units_begun, 1)
                            elif kc == KC - 1:
                                m.then_inc(full[tt], 1)
                for tt in range(n_tok):
                    fills[tt].add()

            n_attn, n_qk = Count(), Count()

            def attention(n_maps, scores, keys_of, at_t, values, heads_per_fill):
                for m in range(n_maps + 1):
                    if m < n_maps:
                        scores(m)
                    if m >= 1:
                        k = m - 1
                        b = 4 + k % 2
                        pe.wait_ge(attn_ready, n_attn.add())
                        start_fill(b)
                        for kt in range(keys_of(k)):
                            t = pe.transpose(ps[:, b, kt * P:(kt + 1) * P], at_t(k, kt), const("ident"))
                        t.then_inc(full[b], 1)
                        fills[b].add()
                        if k % 2 == 1:
                            pe.wait_ge(emptied[4], fills[4].now())
                            pe.wait_ge(emptied[5], fills[5].now())
                            values(k // 2)

            wait_h()
            projections(None, None)
            pe.wait_ge(emptied[4], fills[4].now())
            pe.wait_ge(emptied[5], fills[5].now())
            for f in range(2):
                one(6 + f, const("rot_2d"), zq[:, 2 * f:2 * f + 2, :], ps[:, 6 + f, :])
            for f in range(2):
                one(6 + f, const("rot_2d"), zk[:, 2 * f:2 * f + 2, T:2 * T], ps[:, 6 + f, :])
            pe.wait_ge(squared, n_squared.add(2))
            for f in range(2):
                one(6 + f, const("mean_64"), sq[:, 2 * f:2 * f + 2, :], ps[:, 6 + f, :])
            one(6, const("mean_64"), sq[:, 4:6, :], ps[:, 6, :])
            pe.wait_ge(roped, 1)
            for f in range(2):
                one(7 - f, const("rot_2d"), zq[:, 4 + 2 * f:6 + 2 * f, :], ps[:, 7 - f, :])
            one(7, const("rot_2d"), zk[:, 4, T:2 * T], ps[:, 7, 0:T])
            pe.wait_ge(qk_ready, n_qk.add())

            def scores_a(m):
                hd, qt = divmod(m, 2)
                for i in range(2):
                    r = slice(HEAD * i, HEAD * (i + 1))
                    b = 2 * (m % 2) + i
                    one(b, zq[r, hd, qt * P:(qt + 1) * P], zk[r, hd, :], ps[:, b, :])

            def values_a(hd):
                b = 6 + hd % 2
                start_fill(b)
                for kt in range(4):
                    m = pe.matmul(ps[:, b, 0:T], av[:, kt, hd * P:(hd + 1) * P], attn_t[:, hd % 2, kt, :],
                                  start=kt == 0, stop=kt == 3)
                m.then_inc(full[b], 1)
                fills[b].add()

            attention(8, scores_a, lambda k: 4, lambda k, kt: attn[:, k % 2, kt * P:(kt + 1) * P], values_a, 1)

            def scores_b(m):
                hd, qt = divmod(m, 2)
                jt, g = divmod(hd, 2)
                r = slice(HEAD * g, HEAD * (g + 1))
                one(m % 4, zq[r, 4 + jt, qt * P:(qt + 1) * P], zk[r, 4, :], ps[:, m % 4, :])

            def values_b(hd):
                jt, g = divmod(hd, 2)
                b = 6 + jt % 2
                if g == 0:
                    start_fill(b)
                for kt in range(4):
                    m = pe.matmul(ps[HEAD * g:HEAD * (g + 1), b, 0:T], bv[:, kt, HEAD * g:HEAD * (g + 1)],
                                  attn_t[:, hd % 2, kt, :], start=kt == 0, stop=kt == 3)
                if g == 1:
                    m.then_inc(full[b], 1)
                    fills[b].add()

            attention(16, scores_b, lambda k: 4, lambda k, kt: attn[:, k % 2, kt * P:(kt + 1) * P], values_b, 2)
            pe.wait_ge(squared, n_squared.add())
            for f in range(2):
                one(6 + f, const("mean_128"), sq[:, 2 * f:2 * f + 2, :], ps[:, 6 + f, :])
            pe.wait_ge(mix_ready, 1)

            def out_tiles(stage, src, mark_name):
                for n in range(KC):
                    k_tile(FIRST_UNIT[stage] + n, lambda kc: src[:, kc, :], 4 + n % 2)
                mark[mark_name] = (fills[4].n, fills[5].n)

            out_tiles("attn_out", mix, "attn_out")

            def layer_norm():
                pe.wait_ge(summed, n_summed.add())
                ones_sum("mean_d", lambda k: z[:, k, :], 6, KC)
                pe.wait_ge(squared, n_squared.add())
                ones_sum("mean_d", lambda k: sq[:, k, :], 7, KC)

            n_hid = Count()

            def mlp(l):
                u0 = FIRST_UNIT[f"mlp{l}"]

                def up(j_static, u, i=None):
                    k_tile(u, lambda kc: h[:, kc, :], 4 + j_static % 2, i)

                def down(j_static, u, i=None, first=False, last=False):
                    w = unit(u, i)
                    pe.wait_ge(hid_ready, n_hid.add())
                    if first:
                        for b in range(4):
                            start_fill(b)
                    for n in range(KC):
                        m = pe.matmul(ps[:, n // 2, (n % 2) * T:(n % 2 + 1) * T], w[:, n * P:(n + 1) * P],
                                      hid2[:, j_static % 2, :], start=first and n % 2 == 0, stop=last,
                                      skip_group_check=True)
                        if n == 0:
                            m.then_inc(units_begun, 1)
                        elif last and n % 2 == 1:
                            m.then_inc(full[n // 2], 1)
                    if last:
                        for b in range(4):
                            fills[b].add()

                up(0, u0)
                up(1, u0 + 1)
                down(0, u0 + 2, first=True)
                with rolled(pe, 7, [(fills[4], 2), (fills[5], 2), (n_hid, 4)]) as i:
                    for j in range(1, 5):
                        up(j + 1, u0 + 1 + 2 * j, i)
                        down(j, u0 + 2 + 2 * j, i)
                for j in (29, 30):
                    up(j + 1, u0 + 1 + 2 * j)
                    down(j, u0 + 2 + 2 * j)
                down(31, u0 + 63, last=True)

            layer_norm()
            wait_h()
            mlp(0)
            layer_norm()
            wait_h()
            with rolled(pe, 3, [(fills[4], 4), (fills[5], 4)]) as i:
                for n in range(8):
                    k_tile(FIRST_UNIT["conv_in"] + n, lambda kc: h[:, kc, :], 4 + n % 2, i)
            mark["conv_gb"] = (fills[4].n, fills[5].n)
            pe.wait_ge(mix_ready, 2)
            out_tiles("conv_out", conv_y, "conv_out")
            layer_norm()
            wait_h()
            mlp(1)
            layer_norm()

            def rms_norm():
                pe.wait_ge(squared, n_squared.add())
                ones_sum("mean_d", lambda k: sq[:, k, :], 6, KC)

            rms_norm()
            wait_h()
            with rolled(pe, 2, [(fills[4], 4), (fills[5], 4)]) as i:
                for n in range(8):
                    k_tile(FIRST_UNIT["in2_qk"] + n, lambda kc: h[:, kc, :], 4 + n % 2, i)
            u = FIRST_UNIT["in2_v"]
            for _ in range(3):
                v_units(u, 4, lambda kc, tt: h[:, kc, tt * P:(tt + 1) * P], 2)
                u += 4
            pe.wait_ge(emptied[4], fills[4].now())
            pe.wait_ge(emptied[5], fills[5].now())
            pe.wait_ge(squared, n_squared.add())
            for f in range(4):
                one(6 + f % 2, const("mean_64"), sq[:, 2 * f:2 * f + 2, :], ps[:, 6 + f % 2, :])
            for f in range(4):
                one(6 + f % 2, const("rot_1d"), zz[:, 2 * f:2 * f + 2, :], ps[:, 6 + f % 2, :])
            with rolled(pe, 3, [(fills[4], 4), (fills[5], 4)]) as i:
                for n in range(8):
                    k_tile(FIRST_UNIT["in2_gates"] + n, lambda kc: h[:, kc, :], 4 + n % 2, i)
            mark["gates"] = (fills[4].n, fills[5].n)
            pe.wait_ge(qk_ready, n_qk.add())
            for hd in range(9):
                if hd < 8:
                    r = slice(HEAD * (hd % 2), HEAD * (hd % 2 + 1))
                    b = hd % 4
                    start_fill(b)
                    pe.matmul(ps[:, b, 0:T], zz[r, 4 + hd // 2, 0:P], zz[r, hd // 2, :], start=True, stop=True)
                    pe.matmul(ps[:, b, T:T + P], zz[r, 4 + hd // 2, P:T], zz[r, hd // 2, P:T],
                              start=True, stop=True).then_inc(full[b], 1)
                    fills[b].add()
                if hd >= 1:
                    k = hd - 1
                    b = 6 + k % 2
                    pe.wait_ge(sdec_ready, k + 1)
                    start_fill(b)
                    pe.matmul(ps[:, b, 0:T], rv[:, 0, k * P:(k + 1) * P], sdec[:, k % 2, 0:T], start=True, stop=False,
                              skip_group_check=True)
                    pe.matmul(ps[:, b, P:T], rv[:, 1, k * P:(k + 1) * P], sdec[:, k % 2, T:T + P], start=False,
                              stop=True, skip_group_check=True).then_inc(full[b], 1)
                    fills[b].add()
            pe.wait_ge(o_ready, 1)
            for f in range(4):
                one(6 + f % 2, const("mean_128"), ret[:, 2 * f:2 * f + 2, :], ps[:, 6 + f % 2, :])
            pe.wait_ge(squared, n_squared.add())
            for f in range(4):
                one(6 + f % 2, const("mean_128"), sq[:, 2 * f:2 * f + 2, :], ps[:, 6 + f % 2, :])

            def scores_m(m):
                hd, qt = divmod(m, 2)
                r = slice(HEAD * (hd % 2), HEAD * (hd % 2 + 1))
                nk = P * (qt + 1)
                one(m % 4, zz[r, 8 + hd // 2, qt * P:(qt + 1) * P], zz[r, 12 + hd // 2, 0:nk], ps[:, m % 4, 0:nk])

            def values_m(hd):
                jt, g = divmod(hd, 2)
                b = 6 + jt % 2
                if g == 0:
                    start_fill(b)
                r = slice(HEAD * g, HEAD * (g + 1))
                pe.matmul(ps[r, b, 0:T], mv[:, 0, hd * HEAD:(hd + 1) * HEAD], m_attn_t[:, hd % 2, 0, :],
                          start=True, stop=False, skip_group_check=True)
                m = pe.matmul(ps[r, b, P:T], mv[:, 1, hd * HEAD:(hd + 1) * HEAD], m_attn_t[:, hd % 2, 1, P:T],
                              start=False, stop=True, skip_group_check=True)
                if g == 1:
                    m.then_inc(full[b], 1)
                    fills[b].add()

            attention(16, scores_m, lambda k: k % 2 + 1, lambda k, kt: m_attn[:, k % 2, kt * P:(kt + 1) * P],
                      values_m, 2)
            pe.wait_ge(mix_ready, 3)
            out_tiles("ret_out", ret, "ret_out")
            pe.wait_ge(mix_ready, 4)
            for n in range(4):
                w = unit(FIRST_UNIT["moba_out"] + n)
                for half in range(2):
                    b = 4 + half
                    start_fill(b)
                    for kc in range(4):
                        m = pe.matmul(ps[:, b, 0:T], w[:, kc * T + half * P:kc * T + (half + 1) * P], att[:, kc, :],
                                      start=kc == 0, stop=kc == 3)
                        if half == 0 and kc == 0:
                            m.then_inc(units_begun, 1)
                    m.then_inc(full[b], 1)
                    fills[b].add()
            mark["moba_out"] = (fills[4].n, fills[5].n)
            pe.wait_ge(mix_ready, 5)
            out_tiles("out2", merged, "out2")
            rms_norm()
            wait_h()
            with rolled(pe, 2, [(fills[4], 4), (fills[5], 4)]) as i:
                for n in range(8):
                    k_tile(FIRST_UNIT["peer_q"] + n, lambda kc: h[:, kc, :], 4 + n % 2, i)
            pe.wait_ge(emptied[4], fills[4].now())
            pe.wait_ge(emptied[5], fills[5].now())
            for un in range(2):
                w = unit(FIRST_UNIT["peer_keys"] + un)
                for tt in range(2):
                    for g4 in range(2):
                        b = 2 * tt + g4
                        start_fill(b)
                        for q in range(4):
                            hc = 8 * un + 4 * g4 + q
                            m = pe.matmul(ps[:, b, q * P:(q + 1) * P], qp[:, hc, tt * P:(tt + 1) * P],
                                          w[:, (hc % 8) * P:(hc % 8 + 1) * P], start=True, stop=True)
                            if tt == 0 and g4 == 0 and q == 0:
                                m.then_inc(units_begun, 1)
                        m.then_inc(full[b], 1)
                        fills[b].add()
            with rolled(pe, N_EXP // 8, [(fills[4], 4), (fills[5], 4)]) as i:
                for n in range(8):
                    k_tile(FIRST_UNIT["peer_u"] + n, lambda kc: h[:, kc, :], 4 + n % 2, i)
            mark["peer_u"] = (fills[4].n, fills[5].n)
            mark["hot"] = (fills[0].n, fills[1].n)
            pe.wait_ge(half_found, 2)
            for a in range(3):
                start_fill(6 + a % 2)
                for tt in range(2):
                    m = pe.transpose(ps[:, 6 + a % 2, tt * P:(tt + 1) * P], found[tt][:, a, :], const("ident"))
                m.then_inc(full[6 + a % 2], 1)
                fills[6 + a % 2].add()
            n_hot = Count()
            with rolled(pe, T // 8, [(fills[0], 1), (fills[1], 1), (n_hot, 2)]) as i:
                for b in range(2):
                    pe.wait_ge(hot1_ready, n_hot.add())
                    pe.wait_ge(hot2_ready, n_hot.now())
                    start_fill(b)
                    for t in range(4):
                        m = pe.matmul(ps[:, b, t * P:(t + 1) * P], hot1[:, b, t, :], hot2[:, b, t, :],
                                      start=True, stop=True)
                    m.then_inc(full[b], 1)
                    fills[b].add()
            pe.wait_ge(gated, 1)

            def expert_rows(u, e, i=None, first=False, last=False):
                w = unit(u, i)
                for n in range(KC):
                    m = pe.matmul(ps[:, n // 2, (n % 2) * T:(n % 2 + 1) * T], w[:, n * P:(n + 1) * P],
                                  act_e[:, e, :], start=first and n % 2 == 0, stop=last, skip_group_check=True)
                    if n == 0:
                        m.then_inc(units_begun, 1)
                    elif last and n % 2 == 1:
                        m.then_inc(full[n // 2], 1)

            u0 = FIRST_UNIT["peer_v"]
            for b in range(4):
                start_fill(b)
            for e in range(8):
                expert_rows(u0 + e, e, first=e == 0)
            with rolled(pe, N_EXP // 8 - 2, []) as i:
                for e in range(8):
                    expert_rows(u0 + 8 + e, i * 8 + 8 + e, i)
            for e in range(N_EXP - 8, N_EXP):
                expert_rows(u0 + e, e, last=e == N_EXP - 1)

        @block.scalar
        def _(act):
            drains = {4: Count(), 5: Count()}
            steps = Count()

            for dst, src in ((par[:, :], params), (cst[:, :], consts), (resid[:, :, :], x_t), (z, ctx_t),
                             (lamb, lam_in), (relb[0:32, :], rel_bias), (oneh[0:32, :], onehot),
                             (dmask[0:8, :], dist_mask)):
                act.dma_start(dst, src).then_inc(inputs, 16)
            act.wait_ge(inputs, 16 * 8)
            act.activation(cact[:, :, :], param("c", 0, 16).rearrange("p (k c) -> p k c", c=2),
                           ACT.Silu).then_inc(cact_ready, 1)
            act.wait_ge(lam_sum, 1)
            act.activation(lam2, lam2, ACT.Exp).then_inc(act_step, 1)
            act.wait_ge(row_ready, 1)
            act.dma_start(bias_rows, rowbuf[0:8, :].unsqueeze(1).broadcast_to([8, P, DIST])).then_inc(row_out, 16)
            act.wait_ge(row_out, 16)
            toeplitz = bass.AP(bias_rows.tensor, bias_rows.offset + P - 1, [[DIST - 1, P], [P * DIST, 8], [1, T]])
            act.dma_start(bias, toeplitz).then_inc(bias_in, 16)

            def drain(b, dst, func=ACT.Copy, n=T, **kw):
                act.wait_ge(full[b], drains[b].add())
                act.activation(dst, ps[:, b, 0:n], func, **kw).then_inc(emptied[b], 1)

            for l in range(2):
                with rolled(act, ADA_UNITS // 8, [(drains[4], 1), (drains[5], 1)]):
                    for g in range(2):
                        act.wait_ge(full[4 + g], drains[4 + g].add())
                        act.activation(mod_row[0:2, g, :], ps[0:2, 4 + g, :], ACT.Copy).then_inc(emptied[4 + g], 1)

            n_norm, n_var = Count(), Count()

            def roots(n, k=1):
                for _ in range(k):
                    act.wait_ge(var_ready, n_var.add())
                    s = (n_var.n - 1) % 2
                    act.activation(vare[:, s, 0:n], vare[:, s, 0:n], ACT.Sqrt).then_inc(std_ready, 1)

            act.wait_ge(mod_cols, 1)
            for kc in range(KC):
                m = act.activation(hcat[:, kc, 0:T], z[:, kc, :], ACT.Identity, scale=sc1p[:, kc, 1:2],
                                   bias=mod[0][:, SH1 + kc, 1:2])
            m.then_inc(h_act, 1)
            for n in range(8):
                drain(4 + n % 2, zq[:, n, :])
            for n in range(5):
                drain(4 + n % 2, zk[:, n, :], n=2 * T)
            act.wait_ge(emptied[4], drains[4].now())
            act.activation(sq[:, 0:4, :], zq[:, 4:8, :], ACT.Square).then_inc(squared, 1)
            act.activation(sq[:, 4:6, :].rearrange("p a b -> p (a b)"), zk[:, 4, :], ACT.Square).then_inc(squared, 1)
            roots(512, 3)

            n_nmax = Count()

            def attention(n_maps, exp_of, evac_of):
                for m in range(n_maps + 1):
                    if m < n_maps:
                        act.wait_ge(nmax_ready, n_nmax.add())
                        exp_of(m)
                    if m >= 1:
                        k = m - 1
                        b = 4 + k % 2
                        act.wait_ge(full[b], drains[b].add())
                        evac_of(k, b)

            def exp_a(m):
                for i in range(2):
                    c = 2 * (m % 2) + i
                    act.activation(pexp[:, c, :], ps[:, c, :], ACT.Exp, bias=nmax[:, c:c + 1], scale=SCALE,
                                   accum_out=sums[:, c:c + 1]).then_inc(exp_ready, 1)

            def exp_b(m):
                c = m % 4
                act.activation(pexp[:, c, :], ps[:, c, :], ACT.Exp, bias=nmax[:, c:c + 1], scale=SCALE,
                               accum_out=sums[:, c:c + 1]).then_inc(exp_ready, 1)

            def evac_ab(k, b):
                hd, qt = divmod(k, 2)
                act.activation(attn_t[:, hd % 2, :, qt * P:(qt + 1) * P],
                               ps[:, b, :].rearrange("p (a b) -> p a b", a=4), ACT.Copy).then_inc(emptied[b], 1)

            attention(8, exp_a, evac_ab)
            attention(16, exp_b, evac_ab)
            act.wait_ge(o_ready, 1)
            act.activation(sq[:, 0:4, :], o_a, ACT.Square).then_inc(squared, 1)
            roots(512, 2)
            for n in range(KC):
                drain(4 + n % 2, branch[:, n, :], ACT.Identity, scale=mod[0][:, G1 + n, 0:1])

            n_centred = Count()

            def norm_square(n=T, k=1):
                act.wait_ge(centred, n_centred.add())
                act.activation(sq, zc, ACT.Square).then_inc(squared, 1)
                roots(n, k)

            def half_h(scale, bias_):
                act.wait_ge(normed, n_norm.add())
                for kc in range(4, KC):
                    kw = {} if bias_ is None else {"bias": bias_[:, kc:kc + 1]}
                    m = act.activation(h[:, kc, :], zc[:, kc, :], ACT.Identity, scale=scale[:, kc:kc + 1], **kw)
                m.then_inc(h_act, 1)

            def mlp():
                def hidden(j):
                    b = 4 + j % 2
                    act.wait_ge(full[b], drains[b].add())
                    act.activation(hid[:, j % 2, :], ps[:, b, 0:T], ACT.Relu).then_inc(emptied[b], 1)
                    act.wait_ge(emptied[b], drains[b].now())
                    act.activation(hid2[:, j % 2, :], hid[:, j % 2, :], ACT.Square).then_inc(hid_ready, 1)

                with rolled(act, HID_TILES // 4, [(drains[4], 2), (drains[5], 2)]):
                    for j in range(4):
                        hidden(j)

            norm_square()
            half_h(gs, bs)
            mlp()
            norm_square()
            half_h(gs, bs)
            with rolled(act, 3, [(drains[4], 4), (drains[5], 4)]) as i:
                for n in range(8):
                    drain(4 + n % 2, conv_z[:, i * 8 + n, :])
            for n in range(KC):
                drain(4 + n % 2, branch[:, n, :], ACT.Identity, scale=mod[1][:, G1 + n, 0:1])
            norm_square()
            half_h(gs, bs)
            mlp()
            norm_square()

            act.wait_ge(block1_done, 1)
            act.dma_start(dec, decay).then_inc(dec_in, 16)
            act.activation(sq, resid[:, :, :], ACT.Square).then_inc(squared, 1)
            roots(T)
            half_h(param("mix_g", 0, 8), None)
            with rolled(act, 2, [(drains[4], 4), (drains[5], 4)]) as i:
                for n in range(8):
                    drain(4 + n % 2, zz[:, i * 8 + n, :])
            act.wait_ge(emptied[5], drains[5].now())
            act.activation(sq, zz[:, 8:16, :], ACT.Square).then_inc(squared, 1)
            roots(512, 4)
            for n in range(8):
                drain(4 + n % 2, zz[:, 16 + n, :], ACT.Silu)
            with rolled(act, 2, [(drains[4], 4), (drains[5], 4)]) as i:
                for n in range(8):
                    drain(4 + n % 2, zz[:, i * 8 + 24 + n, :], ACT.Sigmoid)
            norm_square(512, 4)

            def exp_m(m):
                hd, qt = divmod(m, 2)
                nk = P * (qt + 1)
                c = m % 2
                act.activation(m_exp[:, c, 0:nk], m_s[:, c, 0:nk], ACT.Exp, bias=nmax[:, c:c + 1],
                               accum_out=sums[:, c:c + 1]).then_inc(exp_ready, 1)

            def evac_m(k, b):
                hd, qt = divmod(k, 2)
                nt = qt + 1
                act.activation(m_attn_t[:, hd % 2, 0:nt, qt * P:(qt + 1) * P],
                               ps[:, b, 0:nt * P].rearrange("p (a b) -> p a b", a=nt), ACT.Copy).then_inc(emptied[b], 1)

            attention(16, exp_m, evac_m)
            for n in range(KC):
                drain(4 + n % 2, y_a[:, n, :])
            for n in range(KC):
                drain(4 + n % 2, y_b[:, n, :])
            for n in range(KC):
                drain(4 + n % 2, branch[:, n, :])
            act.wait_ge(block1_done, 2)
            act.activation(sq, resid[:, :, :], ACT.Square).then_inc(squared, 1)
            roots(T)
            half_h(param("ffn_g", 0, 8), None)
            with rolled(act, 2, [(drains[4], 4), (drains[5], 4)]) as i:
                for n in range(8):
                    drain(4 + n % 2, qp[:, i * 8 + n, :])
            with rolled(act, 12, [(drains[4], 4), (drains[5], 4)]) as i:
                for n in range(8):
                    drain(4 + n % 2, act_e[:, i * 8 + n, :], ACT.Gelu)
            act.wait_ge(topk_done, 1)
            for tt in range(2):
                act.activation(found[tt][:, 2, :], found[tt][:, 2, :], ACT.Exp).then_inc(gate_exp, 1)
            with rolled(act, 4, [(drains[4], 4), (drains[5], 4)]) as i:
                for n in range(8):
                    drain(4 + n % 2, act_e[:, i * 8 + 96 + n, :], ACT.Gelu)
            act.wait_ge(final, 1)
            act.dma_start(out, resid[:, :, :]).then_inc(stored, 16)
            act.wait_ge(stored, 16)

        @block.vector
        def _(dve):
            steps = Count()
            reads = {b: Count() for b in (0, 1, 2, 3, 6, 7)}

            def step(ins):
                ins.then_inc(dve_step, 1)
                steps.add()

            def settle():
                dve.wait_ge(dve_step, steps.now())

            def filled(b):
                dve.wait_ge(full[b], reads[b].add())

            def spread(a, n):
                return a.unsqueeze(1).broadcast_to([P, n, a.shape[-1]])

            n_rstd = Count()

            dve.wait_ge(inputs, 16 * 8)
            step(dve.tensor_tensor(lamw, lamb[:, 0:4:2, :], lamb[:, 1:4:2, :], ALU.mult))
            settle()
            dve.tensor_reduce(lam2, lamw, AX_X, ALU.add).then_inc(lam_sum, 1)
            filled(7)
            step(dve.tensor_copy(rowbuf[0:8, :], ps[0:8, 7, 0:DIST]))
            settle()
            dve.tensor_tensor(rowbuf[0:8, :], rowbuf[0:8, :], dmask[0:8, :], ALU.add).then_inc(row_ready, 1)
            dve.wait_ge(row_ready, 1)
            dve.sem_inc(emptied[7], 1)
            step(dve.tensor_scalar(gsub, param("subln_g"), 1.0 - LAM_INIT, None, ALU.mult))
            step(dve.tensor_scalar(mqg, param("mq_g"), SCALE, None, ALU.mult))
            dve.wait_ge(act_step, 1)
            step(dve.tensor_tensor(nlam, lam2[:, 1:2], lam2[:, 0:1], ALU.subtract))
            settle()
            step(dve.tensor_scalar(nlam, nlam, -LAM_INIT, None, ALU.add))

            for l in range(2):
                with rolled(dve, ADA_UNITS // 8, [(reads[6], 1), (reads[7], 1)]) as i:
                    for g in range(2):
                        filled(6 + g)
                        at = i * 8 + 4 * g
                        dve.tensor_tensor(mod[l][:, bass.ds(at, 4), :],
                                          ps[:, 6 + g, 0:8].rearrange("p (a b) -> p a b", b=2),
                                          par[:, bass.ds(PARAM[f"ada_b{l}"] + at, 4)].unsqueeze(2)
                                          .broadcast_to([P, 4, 2]), ALU.add).then_inc(emptied[6 + g], 1)
            dve.wait_ge(emptied[7], reads[7].now())
            dve.tensor_scalar(sc1p, mod[0][:, SC1:SC1 + 8, :], 1.0, None, ALU.add).then_inc(mod_cols, 1)
            dve.wait_ge(mod_cols, 1)
            for kc in range(KC):
                m = dve.tensor_scalar(hcat[:, kc, T:2 * T], resid[:, kc, :], sc1p[:, kc, 0:1],
                                      mod[0][:, SH1 + kc, 0:1], ALU.mult, ALU.add)
            m.then_inc(h_dve, 1)
            dve.wait_ge(h_dve, 1)
            step(dve.tensor_scalar(resid[:, :, :], resid[:, :, :], ALPHA, None, ALU.mult))

            for tt in range(4):
                filled(tt)
                dve.tensor_copy(av[:, tt, :], ps[:, tt, :]).then_inc(emptied[tt], 1)
            filled(6)
            dve.tensor_copy(bv.rearrange("p a b -> p (a b)"), ps[:, 6, :]).then_inc(emptied[6], 1)

            def rope(b, zs, n, cos, sin):
                filled(b)
                ra, rb = rope_a[:, 0:n, :], rope_b[:, 0:n, :]
                dve.tensor_tensor(ra, ps[:, b, 0:n * T].rearrange("p (a b) -> p a b", a=n), spread(const(sin, T), n),
                                  ALU.mult).then_inc(emptied[b], 1)
                step(dve.tensor_tensor(rb, zs, spread(const(cos, T), n), ALU.mult))
                settle()
                step(dve.tensor_tensor(zs, ra, rb, ALU.add))
                settle()

            def variance(b, n=512):
                k = n_rstd.add()
                filled(b)
                dve.tensor_scalar(vare[:, (k - 1) % 2, 0:n], ps[:, b, 0:n], EPS, None, ALU.add).then_inc(var_ready, 1)
                dve.wait_ge(var_ready, k)
                dve.sem_inc(emptied[b], 1)
                return k

            def inverse_root(k, n=512):
                s = (k - 1) % 2
                dve.wait_ge(std_ready, k)
                step(dve.reciprocal(rstd[:, s, 0:n], vare[:, s, 0:n]))
                settle()
                return rstd[:, s, 0:n]

            def scaled_by_roots(banks, apply):
                ks = []
                for f in range(len(banks) + 1):
                    if f < len(banks):
                        ks.append(variance(banks[f]))
                    if f >= 1:
                        apply(f - 1, inverse_root(ks[f - 1]))

            for f in range(2):
                rope(6 + f, zq[:, 2 * f:2 * f + 2, :], 2, "cos_2d", "sin_2d")
            for f in range(2):
                rope(6 + f, zk[:, 2 * f:2 * f + 2, T:2 * T], 2, "cos_2d", "sin_2d")
            flat_q = zq.rearrange("p a b -> p (a b)")
            normed_b = ((flat_q[:, 1024:1536], "qn_g"), (flat_q[:, 1536:2048], "qn_g"), (zk[:, 4, :], "kn_g"))

            def norm_bqk(f, inverse):
                dst, g = normed_b[f]
                step(dve.scalar_tensor_tensor(out=dst, in0=dst, scalar=param(g), in1=inverse, op0=ALU.mult,
                                              op1=ALU.mult))

            scaled_by_roots((6, 7, 6), norm_bqk)
            settle()
            dve.sem_inc(roped, 1)
            rope(7, zq[:, 4:6, :], 2, "cos_2d", "sin_2d")
            rope(6, zq[:, 6:8, :], 2, "cos_2d", "sin_2d")
            rope(7, zk[:, 4:5, T:2 * T], 1, "cos_2d", "sin_2d")
            dve.sem_inc(qk_ready, 1)

            n_exp = Count()

            def attention(n_maps, max_of, norm_of, values_of):
                for m in range(n_maps + 1):
                    if m < n_maps:
                        max_of(m)
                    if m >= 1:
                        norm_of(m - 1)
                        if m >= 4 and m % 2 == 0:
                            values_of(m // 2 - 2)
                values_of(n_maps // 2 - 1)

            def max_a(m):
                c = 2 * (m % 2)
                for i in range(2):
                    filled(c + i)
                    step(dve.tensor_reduce(nmax[:, c + i:c + i + 1], ps[:, c + i, :], AX_X, ALU.max, negate=True))
                settle()
                dve.tensor_scalar(nmax[:, c:c + 2], nmax[:, c:c + 2], SCALE, None, ALU.mult).then_inc(nmax_ready, 1)

            def norm_a(m):
                c = 2 * (m % 2)
                dve.wait_ge(exp_ready, n_exp.add(2))
                for i in range(2):
                    dve.sem_inc(emptied[c + i], 1)
                step(dve.reciprocal(inv[:, c:c + 2], sums[:, c:c + 2]))
                settle()
                step(dve.tensor_tensor(inv[:, c + 1:c + 2], inv[:, c + 1:c + 2], nlam, ALU.mult))
                step(dve.tensor_scalar(pexp[:, c, :], pexp[:, c, :], inv[:, c:c + 1], None, ALU.mult))
                settle()
                dve.scalar_tensor_tensor(out=attn[:, m % 2, :], in0=pexp[:, c + 1, :], scalar=inv[:, c + 1:c + 2],
                                         in1=pexp[:, c, :], op0=ALU.mult, op1=ALU.add).then_inc(attn_ready, 1)

            def values_a(hd):
                b = 6 + hd % 2
                filled(b)
                dve.tensor_copy(o_a[:, hd, :], ps[:, b, 0:T]).then_inc(emptied[b], 1)

            def max_b(m):
                c = m % 4
                filled(c)
                step(dve.tensor_reduce(nmax[:, c:c + 1], ps[:, c, :], AX_X, ALU.max, negate=True))
                settle()
                dve.tensor_scalar(nmax[:, c:c + 1], nmax[:, c:c + 1], SCALE, None, ALU.mult).then_inc(nmax_ready, 1)

            def norm_b(m):
                c = m % 4
                dve.wait_ge(exp_ready, n_exp.add())
                dve.sem_inc(emptied[c], 1)
                step(dve.reciprocal(inv[:, c:c + 1], sums[:, c:c + 1]))
                settle()
                dve.tensor_scalar(attn[:, m % 2, :], pexp[:, c, :], inv[:, c:c + 1], None,
                                  ALU.mult).then_inc(attn_ready, 1)

            def values_b(hd):
                if hd % 2 == 0:
                    return
                jt = hd // 2
                filled(6 + jt % 2)
                dve.tensor_copy(mix[:, 4 + jt, :], ps[:, 6 + jt % 2, 0:T]).then_inc(emptied[6 + jt % 2], 1)

            attention(8, max_a, norm_a, values_a)
            dve.wait_ge(emptied[7], reads[7].n)
            dve.sem_inc(o_ready, 1)
            attention(16, max_b, norm_b, values_b)
            flat_o, flat_m = o_a.rearrange("p a b -> p (a b)"), mix.rearrange("p a b -> p (a b)")

            def norm_o(f, inverse):
                c = slice(512 * f, 512 * (f + 1))
                step(dve.scalar_tensor_tensor(out=flat_m[:, c], in0=flat_o[:, c], scalar=gsub, in1=inverse,
                                              op0=ALU.mult, op1=ALU.mult))

            scaled_by_roots((6, 7), norm_o)
            settle()
            dve.sem_inc(mix_ready, 1)

            def wait_branch(name):
                dve.wait_ge(emptied[4], mark[name][0])
                dve.wait_ge(emptied[5], mark[name][1])

            def fold(ln, md, sc, sh):
                g, b = param("ln_g", 8 * ln, 8), param("ln_b", 8 * ln, 8)
                dve.wait_ge(h_act, n_hact.now())
                step(dve.tensor_scalar(ga_, g, ALPHA, None, ALU.mult))
                step(dve.tensor_scalar(ba_, b, ALPHA, None, ALU.mult))
                step(dve.tensor_scalar(exps, mod[md][:, sc:sc + 8, 0], 1.0, None, ALU.add))
                settle()
                step(dve.tensor_tensor(gs, g, exps, ALU.mult))
                step(dve.tensor_tensor(bs, b, exps, ALU.mult))
                settle()
                step(dve.tensor_tensor(bs, bs, mod[md][:, sh:sh + 8, 0], ALU.add))

            def half_h(scale, bias_):
                for kc in range(4):
                    if bias_ is None:
                        m = dve.tensor_scalar(h[:, kc, :], zc[:, kc, :], scale[:, kc:kc + 1], None, ALU.mult)
                    else:
                        m = dve.tensor_scalar(h[:, kc, :], zc[:, kc, :], scale[:, kc:kc + 1], bias_[:, kc:kc + 1],
                                              ALU.mult, ALU.add)
                m.then_inc(h_dve, 1)

            def centre():
                filled(6)
                dve.tensor_tensor(zc, z, spread(ps[:, 6, 0:T], KC), ALU.subtract).then_inc(centred, 1)

            n_cent, n_hact = Count(), Count()
            n_hact.add()

            def layer_norm(to_h):
                centre()
                dve.wait_ge(centred, n_cent.add())
                dve.sem_inc(emptied[6], 1)
                k = variance(7, T)
                dve.tensor_tensor(zc, zc, spread(inverse_root(k, T), KC), ALU.mult).then_inc(
                    normed if to_h else dve_step, 1)
                if to_h:
                    dve.wait_ge(normed, n_normed.add())
                    half_h(gs, bs)
                    n_hact.add()
                    for kc in range(KC):
                        step(dve.tensor_scalar(resid[:, kc, :], zc[:, kc, :], ga_[:, kc:kc + 1], ba_[:, kc:kc + 1],
                                               ALU.mult, ALU.add))
                    settle()
                else:
                    steps.add()
                    settle()

            n_normed = Count()

            def mixer_norm(l, name):
                fold(2 * l, l, SC2, SH2)
                wait_branch(name)
                settle()
                dve.tensor_tensor(z, branch, resid[:, :, :], ALU.add).then_inc(summed, 1)
                layer_norm(True)

            def mlp_norm(l):
                if l == 0:
                    fold(1, 1, SC1, SH1)
                    settle()
                for n in range(KC):
                    b = n // 2
                    if n % 2 == 0:
                        filled(b)
                    m = dve.scalar_tensor_tensor(out=z[:, n, :], in0=ps[:, b, (n % 2) * T:(n % 2 + 1) * T],
                                                 scalar=mod[l][:, G2 + n, 0:1], in1=resid[:, n, :],
                                                 op0=ALU.mult, op1=ALU.add)
                    if n == KC - 1:
                        m.then_inc(summed, 1)
                    elif n % 2 == 1:
                        m.then_inc(emptied[b], 1)
                dve.wait_ge(summed, 2 * l + 2)
                dve.sem_inc(emptied[3], 1)
                layer_norm(l == 0)

            mixer_norm(0, "attn_out")
            mlp_norm(0)
            step(dve.memset(conv_u[:, :, 0:1], 0.0))
            step(dve.memset(conv_u[:, :, T + 1:T + 2], 0.0))
            dve.wait_ge(emptied[4], mark["conv_gb"][0] - 4)
            dve.wait_ge(emptied[5], mark["conv_gb"][1] - 4)
            step(dve.tensor_tensor(conv_u[:, :, 1:T + 1], conv_z[:, 0:8, :], conv_z[:, 8:16, :], ALU.mult))
            settle()
            for kc in range(KC):
                step(dve.tensor_scalar(conv_y[:, kc, :], conv_u[:, kc, 0:T], param("conv_w", kc), param("conv_b", kc),
                                       ALU.mult, ALU.add))
            for tap in (1, 2):
                settle()
                for kc in range(KC):
                    step(dve.scalar_tensor_tensor(out=conv_y[:, kc, :], in0=conv_u[:, kc, tap:tap + T],
                                                  scalar=param("conv_w", 8 * tap + kc), in1=conv_y[:, kc, :],
                                                  op0=ALU.mult, op1=ALU.add))
            settle()
            wait_branch("conv_gb")
            dve.tensor_tensor(conv_y, conv_y, conv_z[:, 16:24, :], ALU.mult).then_inc(mix_ready, 1)
            mixer_norm(1, "conv_out")
            mlp_norm(1)
            for kc in range(KC):
                m = dve.tensor_scalar(resid[:, kc, :], zc[:, kc, :], param("ln_g", 24 + kc), param("ln_b", 24 + kc),
                                      ALU.mult, ALU.add)
            m.then_inc(block1_done, 1)

            n_b1 = Count()

            def rms_norm(g):
                dve.wait_ge(block1_done, n_b1.add())
                k = variance(6, T)
                dve.tensor_tensor(zc, resid[:, :, :], spread(inverse_root(k, T), KC), ALU.mult).then_inc(normed, 1)
                dve.wait_ge(normed, n_normed.add())
                half_h(param(g, 0, 8), None)

            rms_norm("mix_g")
            for v in range(3):
                for tt in range(2):
                    dst = rv[:, tt, 512 * v:512 * (v + 1)] if v < 2 else mv[:, tt, :]
                    filled(tt)
                    dve.tensor_copy(dst, ps[:, tt, :]).then_inc(emptied[tt], 1)
            flat_z = zz.rearrange("p a b -> p (a b)")

            def norm_mqk(f, inverse):
                dst = flat_z[:, 2048 + 512 * f:2048 + 512 * (f + 1)]
                step(dve.scalar_tensor_tensor(out=dst, in0=dst, scalar=mqg if f < 2 else param("mk_g"), in1=inverse,
                                              op0=ALU.mult, op1=ALU.mult))

            scaled_by_roots((6, 7, 6, 7), norm_mqk)
            for f in range(4):
                rope(6 + f % 2, zz[:, 2 * f:2 * f + 2, :], 2, "cos_1d", "sin_1d")
            dve.sem_inc(qk_ready, 1)
            dve.wait_ge(dec_in, 16)

            def ret_copy(hd):
                b = 6 + hd % 2
                filled(b)
                dve.tensor_copy(ret[:, hd, :], ps[:, b, 0:T]).then_inc(emptied[b], 1)

            for hd in range(8):
                b = hd % 4
                filled(b)
                dve.tensor_tensor(sdec[:, hd % 2, :], ps[:, b, 0:DEC], dec[:, hd, :], ALU.mult).then_inc(sdec_ready, 1)
                dve.wait_ge(sdec_ready, hd + 1)
                dve.sem_inc(emptied[b], 1)
                if hd >= 1:
                    ret_copy(hd - 1)
            ret_copy(7)
            dve.wait_ge(emptied[7], reads[7].n)
            dve.sem_inc(o_ready, 1)
            flat_r, flat_c = ret.rearrange("p a b -> p (a b)"), zc.rearrange("p a b -> p (a b)")
            for f in range(4):
                filled(6 + f % 2)
                c = slice(512 * f, 512 * (f + 1))
                dve.tensor_tensor(flat_c[:, c], flat_r[:, c], ps[:, 6 + f % 2, :], ALU.subtract).then_inc(
                    emptied[6 + f % 2], 1)
            dve.wait_ge(emptied[7], reads[7].n)
            dve.sem_inc(centred, 1)
            n_cent.add()
            wait_branch("gates")

            def norm_ret(f, inverse):
                c = slice(512 * f, 512 * (f + 1))
                step(dve.tensor_tensor(flat_c[:, c], flat_c[:, c], inverse, ALU.mult))
                settle()
                step(dve.tensor_tensor(flat_r[:, c], flat_c[:, c], flat_z[:, 4096 + 512 * f:4096 + 512 * (f + 1)],
                                       ALU.mult))

            scaled_by_roots((6, 7, 6, 7), norm_ret)
            settle()
            dve.sem_inc(mix_ready, 1)

            dve.wait_ge(bias_in, 16)

            def max_m(m):
                hd, qt = divmod(m, 2)
                nk = P * (qt + 1)
                filled(m % 4)
                dve.tensor_tensor(m_s[:, m % 2, 0:nk], ps[:, m % 4, 0:nk], bias[:, hd, T - nk:T],
                                  ALU.add).then_inc(emptied[m % 4], 1)
                dve.wait_ge(emptied[m % 4], reads[m % 4].n)
                dve.tensor_reduce(nmax[:, m % 2:m % 2 + 1], m_s[:, m % 2, 0:nk], AX_X, ALU.max,
                                  negate=True).then_inc(nmax_ready, 1)

            def norm_m(m):
                nk = P * (m % 2 + 1)
                c = m % 2
                dve.wait_ge(exp_ready, n_exp.add())
                step(dve.reciprocal(inv[:, c:c + 1], sums[:, c:c + 1]))
                settle()
                dve.tensor_scalar(m_attn[:, c, 0:nk], m_exp[:, c, 0:nk], inv[:, c:c + 1], None,
                                  ALU.mult).then_inc(attn_ready, 1)

            def values_m(hd):
                if hd % 2 == 0:
                    return
                jt = hd // 2
                filled(6 + jt % 2)
                m = dve.tensor_copy(att[:, jt, :], ps[:, 6 + jt % 2, 0:T])
                m.then_inc(emptied[6 + jt % 2], 1)

            attention(16, max_m, norm_m, values_m)
            dve.wait_ge(emptied[7], reads[7].n)
            dve.sem_inc(mix_ready, 1)
            wait_branch("ret_out")
            step(dve.tensor_tensor(y_a, y_a, zz[:, 24:32, :], ALU.mult))
            wait_branch("moba_out")
            step(dve.tensor_tensor(y_b, y_b, zz[:, 32:40, :], ALU.mult))
            settle()
            dve.tensor_tensor(merged, y_a, y_b, ALU.add).then_inc(mix_ready, 1)
            wait_branch("out2")
            dve.tensor_tensor(resid[:, :, :], resid[:, :, :], branch, ALU.add).then_inc(block1_done, 1)
            rms_norm("ffn_g")

            for un in range(2):
                for tt in range(2):
                    for g4 in range(2):
                        b = 2 * tt + g4
                        filled(b)
                        hc = 8 * un + 4 * g4
                        dve.tensor_copy(sco[:, tt, hc:hc + 4, :].rearrange("p a b -> p (a b)"),
                                        ps[:, b, :]).then_inc(emptied[b], 1)
            for b in range(4):
                dve.wait_ge(emptied[b], reads[b].n)

            def top16(vals, idx, src, n):
                for r in range(n):
                    step(dve.max(vals(r)[:, 0:8], src(r)))
                settle()
                for r in range(n):
                    step(dve.max_index(idx(r)[:, 0:8], vals(r)[:, 0:8], src(r)))
                settle()
                for r in range(n):
                    step(dve.match_replace(src(r), vals(r)[:, 0:8], src(r), TAKEN))
                settle()
                for r in range(n):
                    step(dve.max(vals(r)[:, 8:16], src(r)))
                settle()
                for r in range(n):
                    step(dve.max_index(idx(r)[:, 8:16], vals(r)[:, 8:16], src(r)))
                settle()

            v16 = top_v.rearrange("p h c k -> p (h c) k")
            i16 = top_i.rearrange("p h c k -> p (h c) k")
            bu = best_u.rearrange("p (h k) -> p h k", h=8)
            hot4 = hot.rearrange("p (h k) a -> p h k a", h=8)
            cand4 = cand.rearrange("p h (a b) -> p h a b", a=TOPK)
            for tt in range(2):
                top16(lambda r: v16[:, r, :], lambda r: top_iu[:, r, :], lambda r: sco[:, tt, r, :], 16)
                step(dve.tensor_copy(i16, top_iu))
                for hd in range(8):
                    step(dve.tensor_tensor(cand4[:, hd], top_v[:, hd, 0, :].unsqueeze(2).broadcast_to([P, TOPK, TOPK]),
                                           top_v[:, hd, 1, :].unsqueeze(1).broadcast_to([P, TOPK, TOPK]), ALU.add))
                settle()
                top16(lambda r: best_v[:, r, :], lambda r: bu[:, r, :], lambda r: cand[:, r, :], 8)
                for c, (op, by) in enumerate(((ALU.logical_shift_right, 4), (ALU.bitwise_and, 15))):
                    step(dve.tensor_scalar(pick_u, best_u, by, None, op))
                    settle()
                    step(dve.tensor_copy(pick, pick_u))
                    settle()
                    step(dve.tensor_tensor(hot, pick.unsqueeze(2).broadcast_to([P, P, TOPK]),
                                           spread(const("iota16", TOPK), P), ALU.is_equal))
                    settle()
                    for hd in range(8):
                        step(dve.tensor_tensor(hot4[:, hd], hot4[:, hd], spread(top_i[:, hd, c, :], TOPK), ALU.mult))
                    settle()
                    step(dve.tensor_reduce(found[tt][:, c, :], hot, AX_X, ALU.add))
                    settle()
                gates = found[tt][:, 2, :].rearrange("p (h k) -> p h k", h=8)
                step(dve.tensor_tensor(gates, best_v, best_v[:, :, 0:1].broadcast_to([P, 8, TOPK]), ALU.subtract))
            settle()
            dve.sem_inc(topk_done, 1)
            for tt in range(2):
                gates = found[tt][:, 2, :].rearrange("p (h k) -> p h k", h=8)
                dve.wait_ge(gate_exp, tt + 1)
                step(dve.tensor_reduce(exps, gates, AX_X, ALU.add))
                settle()
                step(dve.reciprocal(exps, exps))
                settle()
                dve.tensor_tensor(gates, gates, exps.unsqueeze(2).broadcast_to([P, 8, TOPK]),
                                  ALU.mult).then_inc(half_found, 1)
                dve.wait_ge(half_found, tt + 1)
            for a, dst in enumerate((i1_t, i2_t, gate_t)):
                filled(6 + a % 2)
                m = dve.tensor_copy(dst, ps[:, 6 + a % 2, 0:T])
                m.then_inc(emptied[6 + a % 2], 1)
            for b in (6, 7):
                dve.wait_ge(emptied[b], reads[b].n)
            dve.sem_inc(topk_done, 1)

            def one_hots(b, t0):
                for t in range(4):
                    m = dve.tensor_scalar(hot1[:, b, t, :], const("iota"), i1_t[:, bass.ds(t0 + t, 1)],
                                          gate_t[:, bass.ds(t0 + t, 1)], ALU.is_equal, ALU.mult)
                m.then_inc(hot1_ready, 1)

            def gate(b, t0):
                filled(b)
                a = act_e[:, :, bass.ds(t0, 4)]
                dve.tensor_tensor(a, a, ps[:, b, :].rearrange("p (t e) -> p e t", t=4), ALU.mult).then_inc(emptied[b], 1)

            dve.wait_ge(emptied[4], mark["peer_u"][0])
            dve.wait_ge(emptied[5], mark["peer_u"][1])
            one_hots(0, 0)
            with rolled(dve, T // 8 - 1, [(reads[0], 1), (reads[1], 1)]) as i:
                one_hots(1, i * 8 + 4)
                gate(0, i * 8)
                one_hots(0, i * 8 + 8)
                gate(1, i * 8 + 4)
            one_hots(1, T - 4)
            gate(0, T - 8)
            gate(1, T - 4)
            dve.wait_ge(emptied[1], reads[1].n)
            dve.sem_inc(gated, 1)
            for b in range(4):
                filled(b)
                m = dve.tensor_tensor(resid[:, 2 * b:2 * b + 2, :], resid[:, 2 * b:2 * b + 2, :],
                                      ps[:, b, :].rearrange("p (a b) -> p a b", a=2), ALU.add)
            m.then_inc(final, 1)

        @block.gpsimd
        def _(pool):
            pool.wait_ge(topk_done, 2)
            with pool.Fori(0, T // 8) as i:
                for b in range(2):
                    pool.wait_ge(full[b], i + mark["hot"][b])
                    pool.tensor_copy(i2_now[:, b, :], i2_t[:, bass.ds(i * 8 + 4 * b, 4)]).then_inc(pool_step, 1)
                    pool.wait_ge(pool_step, i * 2 + (1 + b))
                    pool.sem_inc(i2_copied, 1)
                    for t in range(4):
                        m = pool.tensor_scalar(hot2[:, b, t, :], const("iota"), i2_now[:, b, t:t + 1], None,
                                               ALU.is_equal)
                    m.then_inc(hot2_ready, 1)

        @block.sync
        def _(sp):
            def load(v, s):
                sp.dma_start(ring[:, s, :], stream[v]).then_inc(landed[s], 16)

            for s in range(RING):
                load(s, s)
            with sp.Fori(1, N_UNITS // RING) as r:
                for s in range(RING):
                    sp.wait_ge(units_begun, r * RING + (s + 2 - RING))
                    load(r * RING + s, s)
            for v in range(N_UNITS // RING * RING, N_UNITS):
                sp.wait_ge(units_begun, v + 2 - RING)
                load(v, v % RING)


def _constants():
    c = np.zeros((P, N_CONST), np.float32)

    def put(name, a):
        c[:, CONST[name]:CONST[name] + a.shape[1]] = a

    put("ident", np.eye(P))
    put("mean_d", np.full((P, P), 1.0 / D))
    put("mean_64", np.kron(np.eye(2), np.full((HEAD, HEAD), 1.0 / HEAD)))
    put("mean_128", np.full((P, P), 1.0 / P))
    f = np.arange(HEAD)

    def rotation(half):
        r = np.zeros((HEAD, HEAD))
        first = f % (2 * half) < half
        r[f[first], f[first] + half] = -1.0
        r[f[~first], f[~first] - half] = 1.0
        return np.kron(np.eye(2), r).T

    put("rot_2d", rotation(HEAD // 4))
    put("rot_1d", rotation(HEAD // 2))
    put("iota", np.tile(np.arange(P), (P, 1)))
    put("iota16", np.tile(np.arange(TOPK), (P, 1)))
    t = np.arange(T)
    nf = HEAD // 4
    inv_freq = np.float32(10000.0) ** (-np.arange(nf, dtype=np.float32) / nf)
    where = np.stack([t // 64, t % 64]).astype(np.float32)
    ang = (where[f // 32] * inv_freq[f % nf][:, None]).astype(np.float32)
    put("cos_2d", np.tile(np.cos(ang), (2, 1)))
    put("sin_2d", np.tile(np.sin(ang), (2, 1)))
    half = HEAD // 2
    inv = np.float32(10000.0) ** (-np.arange(half, dtype=np.float32) / half)
    ang = (t[None].astype(np.float32) * inv[f % half][:, None]).astype(np.float32)
    put("cos_1d", np.tile(np.cos(ang), (2, 1)))
    put("sin_1d", np.tile(np.sin(ang), (2, 1)))
    return c


def _decay():
    log_g = np.log1p(-np.exp2(-5.0 - np.arange(8)))
    rel = np.arange(T)[None, :] - np.arange(P)[:, None]
    d = np.where(rel[:, None, :] >= 0, np.exp(np.maximum(rel, 0)[:, None, :] * log_g[None, :, None]), 0.0) * SCALE
    return np.concatenate([d, d[:, :, 0:P]], axis=2).astype(np.float32)


def _distances():
    import math
    dist = 255 - np.arange(DIST)
    n = np.maximum(dist, 0)
    nf = np.maximum(n, 1).astype(np.float32)
    large = 16 + (np.log(nf / np.float32(16)) / np.float32(math.log(2048 / 16)) * np.float32(16)).astype(np.int32)
    bucket = np.where(n < 16, n, np.minimum(large, 31))
    onehot = (np.arange(32)[:, None] == bucket[None]).astype(np.float32)
    mask = np.where(dist < 0, np.float32(MASKED), np.float32(0.0))
    return onehot, np.tile(mask, (8, 1)).astype(np.float32)


def _units(a):
    def tiles(w):
        return w.reshape(KC, P, -1, P).transpose(2, 1, 0, 3).reshape(-1, P, UNIT)

    def wide(w):
        return w.reshape(4, 2, P, -1, 512).transpose(3, 0, 2, 1, 4).reshape(-1, P, UNIT)

    def mlp(w1, w2):
        up, down = tiles(w1), w2.reshape(HID_TILES, P, UNIT)
        body = np.stack([up[1:], down[:-1]], axis=1).reshape(-1, P, UNIT)
        return [up[:1], body, down[-1:]]

    w = a["attn_w_in"][0]
    aq, ak, v, bq, bk, bvw = np.split(w, [512, 1024, 1536, 2048, 2176], axis=1)
    bq = bq.reshape(D, 2, 4, HEAD).transpose(0, 2, 1, 3).reshape(D, 512)
    wo = a["attn_w_out"][0]
    wo_b = wo[512:].reshape(2, 4, HEAD, D).transpose(1, 0, 2, 3).reshape(512, D)
    w2 = a["w_in_2"][0]
    rq, rk, rvw, rg, mq, mk, mvw, ga, gb = np.split(w2, np.cumsum([512, 512, 1024, 1024, 512, 512, 512, 1024]), axis=1)
    gate_b, gate_c, xv = np.split(a["conv_w_in"][0], 3, axis=1)
    keys = a["peer_sub_keys_2"][0].reshape(16, N_EXP, P)
    u = a["peer_u_2"][0].reshape(N_EXP, N_EXP, KC, P)
    return [
        wide(a["ada_w"][0]), wide(a["ada_w"][1]),
        tiles(aq), tiles(bq), tiles(ak), wide(v), tiles(bk), tiles(bvw),
        tiles(np.concatenate([wo[:512], wo_b])), *mlp(a["mlp_w1"][0], a["mlp_w2"][0]),
        tiles(gate_c), tiles(xv), tiles(gate_b), tiles(a["conv_w_out"][0]), *mlp(a["mlp_w1"][1], a["mlp_w2"][1]),
        tiles(rq), tiles(rk), tiles(mq), tiles(mk), wide(rvw), wide(mvw), tiles(rg), tiles(ga), tiles(gb),
        tiles(a["ret_w_branch_2"][0]),
        a["moba_w_branch_2"][0].reshape(4, P, 4, 2 * P).transpose(2, 1, 0, 3).reshape(-1, P, UNIT),
        tiles(a["w_out_2"][0]), tiles(a["peer_w_q_2"][0]),
        keys.transpose(2, 0, 1).reshape(P, 2, UNIT).transpose(1, 0, 2),
        u.transpose(1, 3, 2, 0).reshape(N_EXP, P, UNIT),
        a["peer_v_2"][0].reshape(N_EXP, N_EXP, UNIT).transpose(1, 0, 2),
    ]


def _params(a):
    def cols(v):
        return np.ascontiguousarray(v).reshape(-1, P).T

    twice = lambda v: np.tile(v.reshape(-1), 2).reshape(P, 1)
    c = np.stack([a["c"][0], a["c_ctx"]], axis=-1).reshape(KC, P, 2).transpose(1, 0, 2).reshape(P, 16)
    parts = [c, cols(a["ada_b"][0]), cols(a["ada_b"][1]), cols(a["ln_g"]), cols(a["ln_b"]), cols(a["mix_norm_g_2"]),
             cols(a["ffn_norm_g_2"]), cols(a["conv_w"]), cols(a["conv_b"]), a["diff_subln_g"].reshape(P, 1),
             twice(a["q_norm_g"]), twice(a["k_norm_g"]), twice(a["moba_q_gain_2"]), twice(a["moba_k_gain_2"])]
    return np.ascontiguousarray(np.concatenate(parts, axis=1))


def kernel(**inputs):
    import concourse.bacc as bacc
    from concourse.bass_utils import run_bass_kernel_spmd

    a = {k: np.asarray(v) for k, v in inputs.items()}
    parts = _units(a)
    stream = np.empty((N_UNITS, P, UNIT), np.float32)
    at = 0
    for p in parts:
        stream[at:at + len(p)] = p
        at += len(p)
    assert at == N_UNITS

    def features(v):
        return np.ascontiguousarray(v.reshape(T, KC, P).transpose(2, 1, 0))

    onehot, dist_mask = _distances()
    arrays = {
        "stream": stream, "x_t": features(a["x"]), "ctx_t": features(a["ctx"]), "params": _params(a),
        "consts": _constants(), "decay": _decay(),
        "lam_in": np.ascontiguousarray(np.broadcast_to(a["diff_lambda"], (P, 4, HEAD))),
        "rel_bias": np.ascontiguousarray(a["rel_bias_2"]), "onehot": onehot, "dist_mask": dist_mask,
    }
    nc = bacc.Bacc("TRN2", target_bir_lowering=False, num_devices=1)
    args = [nc.dram_tensor(n, v.shape, F32, kind="ExternalInput").ap() for n, v in arrays.items()]
    bias_rows = nc.dram_tensor("bias_rows", (8, P, DIST), F32).ap()
    out = nc.dram_tensor("out", (P, KC, T), F32, kind="ExternalOutput").ap()
    build(nc, *args, bias_rows, out)
    r = run_bass_kernel_spmd(nc, [arrays], core_ids=[0])
    y = r.results[0]["out"]
    return np.ascontiguousarray(y.transpose(2, 1, 0)).reshape(1, T, D)
```

```python
from contextlib import ExitStack, contextmanager

import numpy as np

import concourse.bass as bass
from concourse import mybir

F32 = mybir.dt.float32
F32R = mybir.dt.float32r
U32 = mybir.dt.uint32
ALU = mybir.AluOpType
ACT = mybir.ActivationFunctionType
AX_X = mybir.AxisListType.X

P = 128
T = 256
D = 1024
KC = D // P
RING = 4
TRIP = 8
UNIT = 1024
ALPHA = 4.0 ** 0.25
LAM_INIT = 0.2
EPS = 1e-6
HEAD = 64
SCALE = HEAD ** -0.5
N_EXP = 128
TOPK = 16
HID_TILES = 4 * D // P
MASKED = -1e30
TAKEN = -3.0e38

ADA_UNITS = 48
STAGES = [("ada0", ADA_UNITS), ("ada1", ADA_UNITS), ("attn_in", 18), ("attn_out", 8), ("mlp0", 64),
          ("conv_in", 24), ("conv_out", 8), ("mlp1", 64), ("in2_qk", 16), ("in2_v", 12), ("in2_gates", 24),
          ("ret_out", 8), ("moba_out", 4), ("out2", 8), ("peer_q", 16), ("peer_keys", 2),
          ("peer_u", N_EXP), ("peer_v", N_EXP)]
FIRST_UNIT = {}
N_UNITS = 0
for _name, _n in STAGES:
    FIRST_UNIT[_name] = N_UNITS
    N_UNITS += _n
SPLIT_STAGES = ("mlp0", "conv_in", "mlp1", "in2_qk", "in2_v", "in2_gates", "peer_q", "peer_u", "peer_v")
IS_SPLIT = [_name in SPLIT_STAGES for _name, _n in STAGES for _ in range(_n)]
SPLIT_NO = np.cumsum(IS_SPLIT).tolist()
SPLIT_IN_SLOT = [sum(IS_SPLIT[v] for v in range(_u % RING, _u + 1, RING)) for _u in range(N_UNITS)]

PARAM = {}
N_PARAM = 0
for _name, _n in (("c", 16), ("ada_b0", 48), ("ada_b1", 48), ("ln_g", 32), ("ln_b", 32), ("mix_g", 8),
                  ("ffn_g", 8), ("conv_w", 24), ("conv_b", 8), ("subln_g", 1), ("qn_g", 1), ("kn_g", 1),
                  ("mq_g", 1), ("mk_g", 1)):
    PARAM[_name] = N_PARAM
    N_PARAM += _n

CONST = {}
N_CONST = 0
for _name, _n in (("ident", P), ("mean_d", P), ("mean_64", P), ("mean_128", P), ("rot_2d", P), ("rot_1d", P),
                  ("iota", P), ("iota16", TOPK), ("cos_2d", T), ("sin_2d", T), ("cos_1d", T), ("sin_1d", T)):
    CONST[_name] = N_CONST
    N_CONST += _n
DIST = 384
DEC = 384

SH1, SC1, G1, SH2, SC2, G2 = range(0, 48, 8)


class Count:

    def __init__(self):
        self.n, self.i, self.per = 0, None, 0

    def add(self, k=1):
        self.n += k
        return self.now()

    def now(self):
        return self.n if self.i is None else self.i * self.per + self.n


@contextmanager
def rolled(eng, trips, counts):
    was = {c: c.n for c, _ in counts}
    with eng.Fori(0, trips) as i:
        for c, per in counts:
            c.i, c.per = i, per
        yield i
        for c, per in counts:
            assert c.n - was[c] == per, (c.n, was[c], per)
    for c, per in counts:
        c.i, c.n = None, was[c] + per * trips


def build(nc, stream, x_t, ctx_t, params, consts, decay, lam_in, rel_bias, onehot, dist_mask, bias_rows, out):
    with ExitStack() as ctx:
        at = {}

        def sb(name, shape, dt=F32):
            t = ctx.enter_context(nc.sbuf_tensor(name, shape, dt))
            at[name] = nc.sbuf_base - 4 * int(np.prod(shape[1:]))
            return t

        def rounded(name, like, shape):
            return nc.alloc_sbuf_tensor_at(name, shape, F32R, offset=at[like])

        def sem(name):
            return ctx.enter_context(nc.semaphore(name))

        ring = sb("ring", [P, RING, UNIT])
        ring_hi = sb("ring_hi", [P, RING, UNIT], F32R)
        arena = sb("arena", [P, N_EXP * T])
        late = sb("late", [P, 4096])
        resid = sb("resid", [P, KC, T])
        h = sb("h", [P, KC, T])
        par = sb("par", [P, N_PARAM])
        cst = sb("cst", [P, N_CONST])
        mod = [sb(f"mod{l}", [P, 48, 2]) for l in range(2)]
        cact = sb("cact", [P, KC, 2])
        small = sb("small", [P, 160])

        ring_lo = rounded("ring_lo", "ring", [P, RING, UNIT])
        arena_r = rounded("arena_r", "arena", [P, 21504])
        late_r = rounded("late_r", "late", [P, 2048])
        h_lo = rounded("h_lo", "h", [P, KC, T])

        def param(name, k=0, n=1):
            a = PARAM[name] + k
            return par[:, a:a + n]

        def const(name, n=P):
            return cst[:, CONST[name]:CONST[name] + n]

        def area(at, *shape):
            size = int(np.prod(shape))
            a = arena[:, at:at + size]
            if len(shape) == 2:
                a = a.rearrange("p (a b) -> p a b", b=shape[1])
            if len(shape) == 3:
                a = a.rearrange("p (a b c) -> p a b c", b=shape[1], c=shape[2])
            return a

        branch = area(19456, KC, T)
        z = area(21504, KC, T)
        sq = area(23552, KC, T)
        zc = area(25600, KC, T)
        rope_a = area(27648, 2, T)
        rope_b = area(28160, 2, T)
        hid = area(28672, 2, T)
        hid2 = area(29184, 2, T)
        vare = area(29696, 2, 512)
        rstd = area(30720, 2, 512)
        h_hi_1 = arena_r[:, 10752:12800].rearrange("p (a b) -> p a b", a=KC)
        h_hi_2 = arena_r[:, 19456:21504].rearrange("p (a b) -> p a b", a=KC)
        h_hi_3 = late_r[:, :].rearrange("p (a b) -> p a b", a=KC)
        hid_hi = arena_r[:, 12800:13312].rearrange("p (a b) -> p a b", a=2)
        hid_lo = arena_r[:, 13312:13824].rearrange("p (a b) -> p a b", a=2)
        hcat = area(0, KC, 2 * T)
        zq = area(4096, 8, T)
        zk = area(6144, 5, 2 * T)
        av = area(8704, 4, 512)
        bv = area(10752, 4, P)
        pexp = area(11264, 4, 512)
        attn = area(13312, 2, 512)
        attn_t = area(14336, 2, 4, T)
        o_a = area(16384, 4, T)
        mix = area(17408, 8, T)
        conv_z = area(0, 24, T)
        conv_u = area(6144, KC, T + 2)
        conv_y = area(8208, KC, T)
        zz = area(0, 40, T)
        rv = area(10240, 2, D)
        mv = area(12288, 2, 512)
        dec = area(13312, 8, DEC)
        ret = area(16384, 8, T)
        att = area(18432, 4, T)
        sdec = area(31744, 2, DEC)
        m_s = area(27648, 2, T)
        m_exp = area(28160, 2, T)
        m_attn = area(28672, 2, T)
        m_attn_t = area(11264, 2, 2, T)
        y_a, y_b = area(0, KC, T), area(2048, KC, T)
        merged = area(10240, KC, T)
        qp = area(0, 16, T)
        act_e = area(0, N_EXP, T)
        QUARTER = 3 * N_EXP * T // 4
        sco = area(QUARTER, 2, 16, P)
        cand = area(QUARTER + 4096, 8, TOPK * TOPK)
        hot = area(QUARTER + 6144, P, TOPK)
        mod_row = late[:, 2048:3072].rearrange("p (b n) -> p b n", b=2)
        bias = late[:, 0:2048].rearrange("p (h k) -> p h k", h=8)
        rowbuf = late[:, 3072:3072 + DIST]
        relb = late[:, 3456:3464]
        lamb = late[:, 3464:3720].rearrange("p (a n) -> p a n", a=4)
        lamw = late[:, 3720:3848].rearrange("p (a n) -> p a n", a=2)
        dmask = late[:, 2048:2048 + DIST]
        oneh = late[:, 2432:2432 + DIST]
        e_hi = late_r[:, 0:1024].rearrange("p (s t) -> p s t", s=4)
        e_lo = late_r[:, 1024:2048].rearrange("p (s t) -> p s t", s=4)
        i1_t, i2_t, gate_t = late[:, 0:256], late[:, 256:512], late[:, 512:768]
        hot1 = late[:, 768:1792].rearrange("p (b t n) -> p b t n", b=2, t=4)
        hot2 = late[:, 1792:2816].rearrange("p (b t n) -> p b t n", b=2, t=4)
        top_v = late[:, 2816:3072].rearrange("p (h c k) -> p h c k", h=8, c=2)
        top_i = late[:, 3072:3328].rearrange("p (h c k) -> p h c k", h=8, c=2)
        top_iu = late[:, 3328:3584].bitcast(U32).rearrange("p (h k) -> p h k", h=16)
        best_v = late[:, 3584:3712].rearrange("p (h k) -> p h k", h=8)
        best_u = late[:, 3712:3840].bitcast(U32)
        pick_u = late[:, 3840:3968].bitcast(U32)
        pick = late[:, 3968:4096]
        found = [cst[:, CONST["cos_2d"] + 384 * i:CONST["cos_2d"] + 384 * (i + 1)].rearrange("p (a n) -> p a n", a=3) for i in range(2)]

        i2_now = cst[:, CONST["cos_2d"] + 768:CONST["cos_2d"] + 776].rearrange("p (b t) -> p b t", b=2)
        nmax, sums, inv = small[:, 0:32], small[:, 32:64], small[:, 64:96]
        lam2, nlam, gsub = small[:, 96:98], small[:, 98:99], small[:, 99:100]
        mqg = small[:, 100:101]
        sc1p = small[:, 104:120].rearrange("p (k c) -> p k c", c=2)
        gs, bs = small[:, 120:128], small[:, 128:136]
        ga_, ba_ = small[:, 136:144], small[:, 144:152]
        exps = small[:, 152:160]

        ps = ctx.enter_context(nc.psum_tensor("ps", [P, 8, 512], F32))

        landed = [sem(f"landed{s}") for s in range(RING)]
        hi_ready = sem("hi_ready")
        lo_ready = [sem(f"lo_ready{s}") for s in range(RING)]
        units_begun = sem("units_begun")
        full = [sem(f"full{b}") for b in range(8)]
        emptied = [sem(f"emptied{b}") for b in range(8)]
        inputs = sem("inputs")
        bias_in = sem("bias_in")
        cact_ready = sem("cact_ready")
        h_dve = sem("h_dve")
        h_act = sem("h_act")
        h_lo_ready = sem("h_lo_ready")
        h_own = sem("h_own")
        dve_step = sem("dve_step")
        act_step = sem("act_step")
        squared = sem("squared")
        var_ready = sem("var_ready")
        std_ready = sem("std_ready")
        centred = sem("centred")
        normed = sem("normed")
        summed = sem("summed")
        roped = sem("roped")
        qk_ready = sem("qk_ready")
        nmax_ready = sem("nmax_ready")
        exp_ready = sem("exp_ready")
        attn_ready = sem("attn_ready")
        mix_ready = sem("mix_ready")
        o_ready = sem("o_ready")
        hid_ready = sem("hid_ready")
        hid_hi_ready = sem("hid_hi_ready")
        hid_lo_ready = sem("hid_lo_ready")
        e_hi_ready = sem("e_hi_ready")
        e_lo_ready = sem("e_lo_ready")
        lam_sum = sem("lam_sum")
        mod_cols = sem("mod_cols")
        row_ready = sem("row_ready")
        row_out = sem("row_out")
        dec_in = sem("dec_in")
        block1_done = sem("block1_done")
        sdec_ready = sem("sdec_ready")
        topk_done = sem("topk_done")
        half_found = sem("half_found")
        hot1_ready = sem("hot1_ready")
        hot2_ready = sem("hot2_ready")
        gated = sem("gated")
        final = sem("final")
        stored = sem("stored")
        pool_step = sem("pool_step")
        i2_copied = sem("i2_copied")
        gate_exp = sem("gate_exp")

        mark = {}

        def at_trip(i, per, value):
            return value if i is None else i * per + value

        def unit_hi(act, u, i=None):
            s = u % RING
            act.wait_ge(landed[s], at_trip(i, 16 * TRIP // RING, 16 * (u // RING + 1)))
            act.activation(ring_hi[:, s, :], ring[:, s, :], ACT.Copy).then_inc(hi_ready, 1)

        def unit_lo(eng, u, i=None):
            s = u % RING
            eng.wait_ge(hi_ready, at_trip(i, TRIP, SPLIT_NO[u]))
            eng.tensor_tensor(ring_lo[:, s, :], ring[:, s, :], ring_hi[:, s, :],
                              ALU.subtract).then_inc(lo_ready[s], 1)

        block = ctx.enter_context(nc.Block())

        @block.tensor
        def _(pe):
            fills = [Count() for _ in range(8)]
            n_h, n_h_lo = Count(), Count()
            n_centred, n_squared, n_summed = Count(), Count(), Count()

            def start_fill(b):
                if fills[b].i is not None:
                    assert fills[b].n > 0
                if fills[b].n:
                    pe.wait_ge(emptied[b], fills[b].now())

            def unit(u, i=None):
                s = u % RING
                pe.wait_ge(landed[s], at_trip(i, 16 * TRIP // RING, 16 * (u // RING + 1)))
                return ring[:, s, :]

            def split_unit(u, i=None):
                pe.wait_ge(hi_ready, at_trip(i, TRIP, SPLIT_NO[u]))
                return ring_hi[:, u % RING, :], ring_lo[:, u % RING, :]

            def wait_unit_lo(u, i=None):
                pe.wait_ge(lo_ready[u % RING], at_trip(i, TRIP // RING, SPLIT_IN_SLOT[u]))

            def k_tile(u, rhs, bank, i=None):
                w = unit(u, i)
                start_fill(bank)
                for kc in range(KC):
                    r = rhs(kc)
                    n = r.shape[-1]
                    m = pe.matmul(ps[:, bank, 0:n], w[:, kc * P:(kc + 1) * P], r, start=kc == 0, stop=kc == KC - 1)
                    if kc == 0:
                        m.then_inc(units_begun, 1)
                m.then_inc(full[bank], 1)
                fills[bank].add()

            def h_tile(u, h_hi, bank, i=None, first=False):
                w_hi, w_lo = split_unit(u, i)
                start_fill(bank)
                for w, x in ((w_hi, h_hi), (w_hi, h_lo), (w_lo, h_hi)):
                    if first and x is h_lo:
                        pe.wait_ge(h_lo_ready, n_h_lo.now())
                    if w is w_lo:
                        wait_unit_lo(u, i)
                    for kc in range(KC):
                        begin = w is w_hi and x is h_hi and kc == 0
                        m = pe.matmul(ps[:, bank, 0:T], w[:, kc * P:(kc + 1) * P], x[:, kc, :], start=begin,
                                      stop=w is w_lo and kc == KC - 1)
                        if begin:
                            m.then_inc(units_begun, 1)
                m.then_inc(full[bank], 1)
                fills[bank].add()

            def ones_sum(name, src, bank, n):
                start_fill(bank)
                for k in range(n):
                    r = src(k)
                    m = pe.matmul(ps[:, bank, 0:r.shape[-1]], const(name), r, start=k == 0, stop=k == n - 1)
                m.then_inc(full[bank], 1)
                fills[bank].add()

            def one(bank, lhs, rhs, shape):
                start_fill(bank)
                pe.matmul(shape, lhs, rhs, start=True, stop=True).then_inc(full[bank], 1)
                fills[bank].add()

            def wait_h():
                pe.wait_ge(h_dve, n_h.add())
                pe.wait_ge(h_act, n_h.now())
                n_h_lo.n = n_h.n - 1

            pe.wait_ge(inputs, 16 * 8)
            one(7, relb[0:32, 0:8], oneh[0:32, :], ps[0:8, 7, 0:DIST])

            pe.wait_ge(cact_ready, 1)
            def ada_rows(u, i=None):
                for g in range(2):
                    start_fill(4 + g)
                    for k4 in range(4):
                        w = unit(u + 4 * g + k4, i)
                        for k2 in range(2):
                            kc = 2 * k4 + k2
                            m = pe.matmul(ps[0:2, 4 + g, :], cact[:, kc, :], w[:, k2 * 512:(k2 + 1) * 512],
                                          start=kc == 0, stop=kc == KC - 1)
                            if k2 == 0:
                                m.then_inc(units_begun, 1)
                    m.then_inc(full[4 + g], 1)
                    fills[4 + g].add()
                for g in range(2):
                    pe.wait_ge(emptied[4 + g], fills[4 + g].now())
                    start_fill(6 + g)
                    for q in range(4):
                        m = pe.matmul(ps[:, 6 + g, 2 * q:2 * q + 2], mod_row[0:2, g, q * P:(q + 1) * P],
                                      const("ident")[0:2, 0:2], start=True, stop=True)
                    m.then_inc(full[6 + g], 1)
                    fills[6 + g].add()

            ada_rows(FIRST_UNIT["ada0"])
            with rolled(pe, ADA_UNITS // 8 - 1, [(fills[b], 1) for b in (4, 5, 6, 7)]) as i:
                ada_rows(FIRST_UNIT["ada0"] + 8, i)
            with rolled(pe, ADA_UNITS // 8, [(fills[b], 1) for b in (4, 5, 6, 7)]) as i:
                ada_rows(FIRST_UNIT["ada1"], i)

            def projections(src, wide):
                u = FIRST_UNIT["attn_in"]
                tile = 0
                for _ in range(8):
                    k_tile(u, lambda kc: hcat[:, kc, T:2 * T], 4 + tile % 2)
                    u, tile = u + 1, tile + 1
                for _ in range(4):
                    k_tile(u, lambda kc: hcat[:, kc, :], 4 + tile % 2)
                    u, tile = u + 1, tile + 1
                v_units(u, 4, lambda kc, tt: hcat[:, kc, tt * P:(tt + 1) * P], 4)
                u += 4
                k_tile(u, lambda kc: hcat[:, kc, :], 4 + tile % 2)
                w = unit(u + 1)
                start_fill(6)
                for tt in range(4):
                    for kc in range(KC):
                        m = pe.matmul(ps[:, 6, tt * P:(tt + 1) * P], hcat[:, kc, tt * P:(tt + 1) * P],
                                      w[:, kc * P:(kc + 1) * P], start=kc == 0, stop=kc == KC - 1)
                        if tt == 0 and kc == 0:
                            m.then_inc(units_begun, 1)
                m.then_inc(full[6], 1)
                fills[6].add()

            def v_units(u, n_units, lhs, n_tok):
                for tt in range(n_tok):
                    start_fill(tt)
                for k4 in range(4):
                    w = unit(u + k4)
                    for k2 in range(2):
                        kc = 2 * k4 + k2
                        for tt in range(n_tok):
                            m = pe.matmul(ps[:, tt, :], lhs(kc, tt), w[:, k2 * 512:(k2 + 1) * 512],
                                          start=kc == 0, stop=kc == KC - 1)
                            if k2 == 0 and tt == 0:
                                m.then_inc(units_begun, 1)
                            elif kc == KC - 1:
                                m.then_inc(full[tt], 1)
                for tt in range(n_tok):
                    fills[tt].add()

            def h_v_units(u, h_hi):
                for tt in range(2):
                    start_fill(tt)
                for k4 in range(4):
                    w_hi, w_lo = split_unit(u + k4)
                    for w, x in ((w_hi, h_hi), (w_hi, h_lo), (w_lo, h_hi)):
                        if w is w_lo:
                            wait_unit_lo(u + k4)
                        for k2 in range(2):
                            kc = 2 * k4 + k2
                            for tt in range(2):
                                begin = w is w_hi and x is h_hi
                                m = pe.matmul(ps[:, tt, :], x[:, kc, tt * P:(tt + 1) * P],
                                              w[:, k2 * 512:(k2 + 1) * 512], start=begin and kc == 0,
                                              stop=w is w_lo and kc == KC - 1)
                                if begin and k2 == 0 and tt == 0:
                                    m.then_inc(units_begun, 1)
                                elif w is w_lo and kc == KC - 1:
                                    m.then_inc(full[tt], 1)
                for tt in range(2):
                    fills[tt].add()

            n_attn, n_qk = Count(), Count()

            def attention(n_maps, scores, keys_of, at_t, values, heads_per_fill):
                for m in range(n_maps + 1):
                    if m < n_maps:
                        scores(m)
                    if m >= 1:
                        k = m - 1
                        b = 4 + k % 2
                        pe.wait_ge(attn_ready, n_attn.add())
                        start_fill(b)
                        for kt in range(keys_of(k)):
                            t = pe.transpose(ps[:, b, kt * P:(kt + 1) * P], at_t(k, kt), const("ident"))
                        t.then_inc(full[b], 1)
                        fills[b].add()
                        if k % 2 == 1:
                            pe.wait_ge(emptied[4], fills[4].now())
                            pe.wait_ge(emptied[5], fills[5].now())
                            values(k // 2)

            wait_h()
            projections(None, None)
            pe.wait_ge(emptied[4], fills[4].now())
            pe.wait_ge(emptied[5], fills[5].now())
            for f in range(2):
                one(6 + f, const("rot_2d"), zq[:, 2 * f:2 * f + 2, :], ps[:, 6 + f, :])
            for f in range(2):
                one(6 + f, const("rot_2d"), zk[:, 2 * f:2 * f + 2, T:2 * T], ps[:, 6 + f, :])
            pe.wait_ge(squared, n_squared.add(2))
            for f in range(2):
                one(6 + f, const("mean_64"), sq[:, 2 * f:2 * f + 2, :], ps[:, 6 + f, :])
            one(6, const("mean_64"), sq[:, 4:6, :], ps[:, 6, :])
            pe.wait_ge(roped, 1)
            for f in range(2):
                one(7 - f, const("rot_2d"), zq[:, 4 + 2 * f:6 + 2 * f, :], ps[:, 7 - f, :])
            one(7, const("rot_2d"), zk[:, 4, T:2 * T], ps[:, 7, 0:T])
            pe.wait_ge(qk_ready, n_qk.add())

            def scores_a(m):
                hd, qt = divmod(m, 2)
                for i in range(2):
                    r = slice(HEAD * i, HEAD * (i + 1))
                    b = 2 * (m % 2) + i
                    one(b, zq[r, hd, qt * P:(qt + 1) * P], zk[r, hd, :], ps[:, b, :])

            def values_a(hd):
                b = 6 + hd % 2
                start_fill(b)
                for kt in range(4):
                    m = pe.matmul(ps[:, b, 0:T], av[:, kt, hd * P:(hd + 1) * P], attn_t[:, hd % 2, kt, :],
                                  start=kt == 0, stop=kt == 3)
                m.then_inc(full[b], 1)
                fills[b].add()

            attention(8, scores_a, lambda k: 4, lambda k, kt: attn[:, k % 2, kt * P:(kt + 1) * P], values_a, 1)

            def scores_b(m):
                hd, qt = divmod(m, 2)
                jt, g = divmod(hd, 2)
                r = slice(HEAD * g, HEAD * (g + 1))
                one(m % 4, zq[r, 4 + jt, qt * P:(qt + 1) * P], zk[r, 4, :], ps[:, m % 4, :])

            def values_b(hd):
                jt, g = divmod(hd, 2)
                b = 6 + jt % 2
                if g == 0:
                    start_fill(b)
                for kt in range(4):
                    m = pe.matmul(ps[HEAD * g:HEAD * (g + 1), b, 0:T], bv[:, kt, HEAD * g:HEAD * (g + 1)],
                                  attn_t[:, hd % 2, kt, :], start=kt == 0, stop=kt == 3)
                if g == 1:
                    m.then_inc(full[b], 1)
                    fills[b].add()

            attention(16, scores_b, lambda k: 4, lambda k, kt: attn[:, k % 2, kt * P:(kt + 1) * P], values_b, 2)
            pe.wait_ge(squared, n_squared.add())
            for f in range(2):
                one(6 + f, const("mean_128"), sq[:, 2 * f:2 * f + 2, :], ps[:, 6 + f, :])
            pe.wait_ge(mix_ready, 1)

            def out_tiles(stage, src, mark_name):
                for n in range(KC):
                    k_tile(FIRST_UNIT[stage] + n, lambda kc: src[:, kc, :], 4 + n % 2)
                mark[mark_name] = (fills[4].n, fills[5].n)

            out_tiles("attn_out", mix, "attn_out")

            def layer_norm():
                pe.wait_ge(summed, n_summed.add())
                ones_sum("mean_d", lambda k: z[:, k, :], 6, KC)
                pe.wait_ge(squared, n_squared.add())
                ones_sum("mean_d", lambda k: sq[:, k, :], 7, KC)

            n_hid = Count()

            def rows_in(u, i, w_hi, w_lo, x_hi, x_lo, x_lo_ready, x_no, first, last):
                for w, x in ((w_hi, x_hi), (w_lo, x_hi), (w_hi, x_lo)):
                    if w is w_lo:
                        wait_unit_lo(u, i)
                    if x is x_lo:
                        pe.wait_ge(x_lo_ready, x_no)
                    begin, end = w is w_hi and x is x_hi, last and x is x_lo
                    for n in range(KC):
                        m = pe.matmul(ps[:, n // 2, (n % 2) * T:(n % 2 + 1) * T], w[:, n * P:(n + 1) * P], x,
                                      start=first and begin and n % 2 == 0, stop=end, skip_group_check=True)
                        if begin and n == 0:
                            m.then_inc(units_begun, 1)
                        elif end and n % 2 == 1:
                            m.then_inc(full[n // 2], 1)

            def mlp(l):
                u0 = FIRST_UNIT[f"mlp{l}"]

                def up(j_static, u, i=None, first=False):
                    h_tile(u, h_hi_1, 4 + j_static % 2, i, first)

                def down(j_static, u, i=None, first=False, last=False):
                    w_hi, w_lo = split_unit(u, i)
                    j = j_static % 2
                    pe.wait_ge(hid_hi_ready, n_hid.add())
                    if first:
                        for b in range(4):
                            start_fill(b)
                    rows_in(u, i, w_hi, w_lo, hid_hi[:, j, :], hid_lo[:, j, :], hid_lo_ready, n_hid.now(), first, last)
                    if last:
                        for b in range(4):
                            fills[b].add()

                up(0, u0, first=True)
                up(1, u0 + 1)
                down(0, u0 + 2, first=True)
                with rolled(pe, 7, [(fills[4], 2), (fills[5], 2), (n_hid, 4)]) as i:
                    for j in range(1, 5):
                        up(j + 1, u0 + 1 + 2 * j, i)
                        down(j, u0 + 2 + 2 * j, i)
                for j in (29, 30):
                    up(j + 1, u0 + 1 + 2 * j)
                    down(j, u0 + 2 + 2 * j)
                down(31, u0 + 63, last=True)

            layer_norm()
            wait_h()
            mlp(0)
            layer_norm()
            wait_h()
            with rolled(pe, 3, [(fills[4], 4), (fills[5], 4)]) as i:
                for n in range(8):
                    h_tile(FIRST_UNIT["conv_in"] + n, h_hi_1, 4 + n % 2, i, n == 0)
            mark["conv_gb"] = (fills[4].n, fills[5].n)
            pe.wait_ge(mix_ready, 2)
            out_tiles("conv_out", conv_y, "conv_out")
            layer_norm()
            wait_h()
            mlp(1)
            layer_norm()

            def rms_norm():
                pe.wait_ge(squared, n_squared.add())
                ones_sum("mean_d", lambda k: sq[:, k, :], 6, KC)

            rms_norm()
            wait_h()
            with rolled(pe, 2, [(fills[4], 4), (fills[5], 4)]) as i:
                for n in range(8):
                    h_tile(FIRST_UNIT["in2_qk"] + n, h_hi_2, 4 + n % 2, i, n == 0)
            u = FIRST_UNIT["in2_v"]
            for _ in range(3):
                h_v_units(u, h_hi_2)
                u += 4
            pe.wait_ge(emptied[4], fills[4].now())
            pe.wait_ge(emptied[5], fills[5].now())
            pe.wait_ge(squared, n_squared.add())
            for f in range(4):
                one(6 + f % 2, const("mean_64"), sq[:, 2 * f:2 * f + 2, :], ps[:, 6 + f % 2, :])
            for f in range(4):
                one(6 + f % 2, const("rot_1d"), zz[:, 2 * f:2 * f + 2, :], ps[:, 6 + f % 2, :])
            with rolled(pe, 3, [(fills[4], 4), (fills[5], 4)]) as i:
                for n in range(8):
                    h_tile(FIRST_UNIT["in2_gates"] + n, h_hi_2, 4 + n % 2, i)
            mark["gates"] = (fills[4].n, fills[5].n)
            pe.wait_ge(qk_ready, n_qk.add())
            for hd in range(9):
                if hd < 8:
                    r = slice(HEAD * (hd % 2), HEAD * (hd % 2 + 1))
                    b = hd % 4
                    start_fill(b)
                    pe.matmul(ps[:, b, 0:T], zz[r, 4 + hd // 2, 0:P], zz[r, hd // 2, :], start=True, stop=True)
                    pe.matmul(ps[:, b, T:T + P], zz[r, 4 + hd // 2, P:T], zz[r, hd // 2, P:T],
                              start=True, stop=True).then_inc(full[b], 1)
                    fills[b].add()
                if hd >= 1:
                    k = hd - 1
                    b = 6 + k % 2
                    pe.wait_ge(sdec_ready, k + 1)
                    start_fill(b)
                    pe.matmul(ps[:, b, 0:T], rv[:, 0, k * P:(k + 1) * P], sdec[:, k % 2, 0:T], start=True, stop=False,
                              skip_group_check=True)
                    pe.matmul(ps[:, b, P:T], rv[:, 1, k * P:(k + 1) * P], sdec[:, k % 2, T:T + P], start=False,
                              stop=True, skip_group_check=True).then_inc(full[b], 1)
                    fills[b].add()
            pe.wait_ge(o_ready, 1)
            for f in range(4):
                one(6 + f % 2, const("mean_128"), ret[:, 2 * f:2 * f + 2, :], ps[:, 6 + f % 2, :])
            pe.wait_ge(squared, n_squared.add())
            for f in range(4):
                one(6 + f % 2, const("mean_128"), sq[:, 2 * f:2 * f + 2, :], ps[:, 6 + f % 2, :])

            def scores_m(m):
                hd, qt = divmod(m, 2)
                r = slice(HEAD * (hd % 2), HEAD * (hd % 2 + 1))
                nk = P * (qt + 1)
                one(m % 4, zz[r, 8 + hd // 2, qt * P:(qt + 1) * P], zz[r, 12 + hd // 2, 0:nk], ps[:, m % 4, 0:nk])

            def values_m(hd):
                jt, g = divmod(hd, 2)
                b = 6 + jt % 2
                if g == 0:
                    start_fill(b)
                r = slice(HEAD * g, HEAD * (g + 1))
                pe.matmul(ps[r, b, 0:T], mv[:, 0, hd * HEAD:(hd + 1) * HEAD], m_attn_t[:, hd % 2, 0, :],
                          start=True, stop=False, skip_group_check=True)
                m = pe.matmul(ps[r, b, P:T], mv[:, 1, hd * HEAD:(hd + 1) * HEAD], m_attn_t[:, hd % 2, 1, P:T],
                              start=False, stop=True, skip_group_check=True)
                if g == 1:
                    m.then_inc(full[b], 1)
                    fills[b].add()

            attention(16, scores_m, lambda k: k % 2 + 1, lambda k, kt: m_attn[:, k % 2, kt * P:(kt + 1) * P],
                      values_m, 2)
            pe.wait_ge(mix_ready, 3)
            out_tiles("ret_out", ret, "ret_out")
            pe.wait_ge(mix_ready, 4)
            for n in range(4):
                w = unit(FIRST_UNIT["moba_out"] + n)
                for half in range(2):
                    b = 4 + half
                    start_fill(b)
                    for kc in range(4):
                        m = pe.matmul(ps[:, b, 0:T], w[:, kc * T + half * P:kc * T + (half + 1) * P], att[:, kc, :],
                                      start=kc == 0, stop=kc == 3)
                        if half == 0 and kc == 0:
                            m.then_inc(units_begun, 1)
                    m.then_inc(full[b], 1)
                    fills[b].add()
            mark["moba_out"] = (fills[4].n, fills[5].n)
            pe.wait_ge(mix_ready, 5)
            out_tiles("out2", merged, "out2")
            rms_norm()
            wait_h()
            with rolled(pe, 2, [(fills[4], 4), (fills[5], 4)]) as i:
                for n in range(8):
                    h_tile(FIRST_UNIT["peer_q"] + n, h_hi_3, 4 + n % 2, i, n == 0)
            pe.wait_ge(emptied[4], fills[4].now())
            pe.wait_ge(emptied[5], fills[5].now())
            for un in range(2):
                w = unit(FIRST_UNIT["peer_keys"] + un)
                for tt in range(2):
                    for g4 in range(2):
                        b = 2 * tt + g4
                        start_fill(b)
                        for q in range(4):
                            hc = 8 * un + 4 * g4 + q
                            m = pe.matmul(ps[:, b, q * P:(q + 1) * P], qp[:, hc, tt * P:(tt + 1) * P],
                                          w[:, (hc % 8) * P:(hc % 8 + 1) * P], start=True, stop=True)
                            if tt == 0 and g4 == 0 and q == 0:
                                m.then_inc(units_begun, 1)
                        m.then_inc(full[b], 1)
                        fills[b].add()
            with rolled(pe, N_EXP // 8, [(fills[4], 4), (fills[5], 4)]) as i:
                for n in range(8):
                    h_tile(FIRST_UNIT["peer_u"] + n, h_hi_3, 4 + n % 2, i)
            mark["peer_u"] = (fills[4].n, fills[5].n)
            mark["hot"] = (fills[0].n, fills[1].n)
            pe.wait_ge(half_found, 2)
            for a in range(3):
                start_fill(6 + a % 2)
                for tt in range(2):
                    m = pe.transpose(ps[:, 6 + a % 2, tt * P:(tt + 1) * P], found[tt][:, a, :], const("ident"))
                m.then_inc(full[6 + a % 2], 1)
                fills[6 + a % 2].add()
            n_hot = Count()
            with rolled(pe, T // 8, [(fills[0], 1), (fills[1], 1), (n_hot, 2)]) as i:
                for b in range(2):
                    pe.wait_ge(hot1_ready, n_hot.add())
                    pe.wait_ge(hot2_ready, n_hot.now())
                    start_fill(b)
                    for t in range(4):
                        m = pe.matmul(ps[:, b, t * P:(t + 1) * P], hot1[:, b, t, :], hot2[:, b, t, :],
                                      start=True, stop=True)
                    m.then_inc(full[b], 1)
                    fills[b].add()
            pe.wait_ge(gated, 1)

            def expert_rows(e, i=None, first=False, last=False):
                u = FIRST_UNIT["peer_v"] + e
                w_hi, w_lo = split_unit(u, i)
                pe.wait_ge(e_hi_ready, at_trip(i, TRIP, e + 1))
                rows_in(u, i, w_hi, w_lo, e_hi[:, e % 4, :], e_lo[:, e % 4, :], e_lo_ready, at_trip(i, TRIP, e + 1),
                        first, last)

            for b in range(4):
                start_fill(b)
            for e in range(8):
                expert_rows(e, first=e == 0)
            with rolled(pe, N_EXP // 8 - 2, []) as i:
                for e in range(8):
                    expert_rows(8 + e, i)
            for e in range(N_EXP - 8, N_EXP):
                expert_rows(e, last=e == N_EXP - 1)

        @block.scalar
        def _(act):
            drains = {4: Count(), 5: Count()}
            steps = Count()

            for dst, src in ((par[:, :], params), (cst[:, :], consts), (resid[:, :, :], x_t), (z, ctx_t),
                             (lamb, lam_in), (relb[0:32, :], rel_bias), (oneh[0:32, :], onehot),
                             (dmask[0:8, :], dist_mask)):
                act.dma_start(dst, src).then_inc(inputs, 16)
            act.wait_ge(inputs, 16 * 8)
            act.activation(cact[:, :, :], param("c", 0, 16).rearrange("p (k c) -> p k c", c=2),
                           ACT.Silu).then_inc(cact_ready, 1)
            act.wait_ge(lam_sum, 1)
            act.activation(lam2, lam2, ACT.Exp).then_inc(act_step, 1)
            act.wait_ge(row_ready, 1)
            act.dma_start(bias_rows, rowbuf[0:8, :].unsqueeze(1).broadcast_to([8, P, DIST])).then_inc(row_out, 16)
            act.wait_ge(row_out, 16)
            toeplitz = bass.AP(bias_rows.tensor, bias_rows.offset + P - 1, [[DIST - 1, P], [P * DIST, 8], [1, T]])
            act.dma_start(bias, toeplitz).then_inc(bias_in, 16)

            def drain(b, dst, func=ACT.Copy, n=T, **kw):
                act.wait_ge(full[b], drains[b].add())
                act.activation(dst, ps[:, b, 0:n], func, **kw).then_inc(emptied[b], 1)

            for l in range(2):
                with rolled(act, ADA_UNITS // 8, [(drains[4], 1), (drains[5], 1)]):
                    for g in range(2):
                        act.wait_ge(full[4 + g], drains[4 + g].add())
                        act.activation(mod_row[0:2, g, :], ps[0:2, 4 + g, :], ACT.Copy).then_inc(emptied[4 + g], 1)

            n_norm, n_var, n_act_step = Count(), Count(), Count()
            n_act_step.add()

            def roots(n, k=1):
                for _ in range(k):
                    act.wait_ge(var_ready, n_var.add())
                    s = (n_var.n - 1) % 2
                    act.activation(vare[:, s, 0:n], vare[:, s, 0:n], ACT.Sqrt).then_inc(std_ready, 1)

            act.wait_ge(mod_cols, 1)
            for kc in range(KC):
                m = act.activation(hcat[:, kc, 0:T], z[:, kc, :], ACT.Identity, scale=sc1p[:, kc, 1:2],
                                   bias=mod[0][:, SH1 + kc, 1:2])
            m.then_inc(h_act, 1)
            for n in range(8):
                drain(4 + n % 2, zq[:, n, :])
            for n in range(5):
                drain(4 + n % 2, zk[:, n, :], n=2 * T)
            act.wait_ge(emptied[4], drains[4].now())
            act.activation(sq[:, 0:4, :], zq[:, 4:8, :], ACT.Square).then_inc(squared, 1)
            act.activation(sq[:, 4:6, :].rearrange("p a b -> p (a b)"), zk[:, 4, :], ACT.Square).then_inc(squared, 1)
            roots(512, 3)

            n_nmax = Count()

            def attention(n_maps, exp_of, evac_of):
                for m in range(n_maps + 1):
                    if m < n_maps:
                        act.wait_ge(nmax_ready, n_nmax.add())
                        exp_of(m)
                    if m >= 1:
                        k = m - 1
                        b = 4 + k % 2
                        act.wait_ge(full[b], drains[b].add())
                        evac_of(k, b)

            def exp_a(m):
                for i in range(2):
                    c = 2 * (m % 2) + i
                    act.activation(pexp[:, c, :], ps[:, c, :], ACT.Exp, bias=nmax[:, c:c + 1], scale=SCALE,
                                   accum_out=sums[:, c:c + 1]).then_inc(exp_ready, 1)

            def exp_b(m):
                c = m % 4
                act.activation(pexp[:, c, :], ps[:, c, :], ACT.Exp, bias=nmax[:, c:c + 1], scale=SCALE,
                               accum_out=sums[:, c:c + 1]).then_inc(exp_ready, 1)

            def evac_ab(k, b):
                hd, qt = divmod(k, 2)
                act.activation(attn_t[:, hd % 2, :, qt * P:(qt + 1) * P],
                               ps[:, b, :].rearrange("p (a b) -> p a b", a=4), ACT.Copy).then_inc(emptied[b], 1)

            attention(8, exp_a, evac_ab)
            attention(16, exp_b, evac_ab)
            act.wait_ge(o_ready, 1)
            act.activation(sq[:, 0:4, :], o_a, ACT.Square).then_inc(squared, 1)
            roots(512, 2)
            for n in range(KC):
                drain(4 + n % 2, branch[:, n, :], ACT.Identity, scale=mod[0][:, G1 + n, 0:1])

            n_centred = Count()

            def norm_square(n=T, k=1):
                act.wait_ge(centred, n_centred.add())
                act.activation(sq, zc, ACT.Square).then_inc(squared, 1)
                roots(n, k)

            def half_h(scale, bias_, h_hi):
                act.wait_ge(normed, n_norm.add())
                for kc in range(4, KC):
                    kw = {} if bias_ is None else {"bias": bias_[:, kc:kc + 1]}
                    m = act.activation(h[:, kc, :], zc[:, kc, :], ACT.Identity, scale=scale[:, kc:kc + 1], **kw)
                m.then_inc(act_step, 1)
                act.wait_ge(act_step, n_act_step.add())
                act.activation(h_hi[:, 4:8, :], h[:, 4:8, :], ACT.Copy).then_inc(h_act, 1)

            def mlp(l):
                u0 = FIRST_UNIT[f"mlp{l}"]

                def hidden(j):
                    b = 4 + j % 2
                    act.wait_ge(full[b], drains[b].add())
                    act.activation(hid[:, j % 2, :], ps[:, b, 0:T], ACT.Relu).then_inc(emptied[b], 1)
                    act.wait_ge(emptied[b], drains[b].now())
                    act.activation(hid2[:, j % 2, :], hid[:, j % 2, :], ACT.Square).then_inc(hid_ready, 1)

                with rolled(act, HID_TILES // 4, [(drains[4], 2), (drains[5], 2)]) as i:
                    for j in range(4):
                        hidden(j)
                        unit_hi(act, u0 + 2 * j + 2, i)
                        unit_hi(act, u0 + 2 * j + 3, i)

            def first_hi(stage):
                for n in range(2):
                    unit_hi(act, FIRST_UNIT[stage] + n)

            def split_and_drain(stage, n, dst, func=ACT.Copy, i=None, ahead=True):
                if ahead:
                    unit_hi(act, FIRST_UNIT[stage] + n + 2, i)
                drain(4 + n % 2, dst, func)

            first_hi("mlp0")
            norm_square()
            half_h(gs, bs, h_hi_1)
            mlp(0)
            norm_square()
            half_h(gs, bs, h_hi_1)
            with rolled(act, 2, [(drains[4], 4), (drains[5], 4)]) as i:
                for n in range(8):
                    split_and_drain("conv_in", n, conv_z[:, i * 8 + n, :], i=i)
            for n in range(16, 24):
                split_and_drain("conv_in", n, conv_z[:, n, :], ahead=n < 22)
            for n in range(KC):
                drain(4 + n % 2, branch[:, n, :], ACT.Identity, scale=mod[1][:, G1 + n, 0:1])
            first_hi("mlp1")
            norm_square()
            half_h(gs, bs, h_hi_1)
            mlp(1)
            norm_square()

            act.wait_ge(block1_done, 1)
            act.dma_start(dec, decay).then_inc(dec_in, 16)
            act.activation(sq, resid[:, :, :], ACT.Square).then_inc(squared, 1)
            roots(T)
            half_h(param("mix_g", 0, 8), None, h_hi_2)
            with rolled(act, 2, [(drains[4], 4), (drains[5], 4)]) as i:
                for n in range(8):
                    split_and_drain("in2_qk", n, zz[:, i * 8 + n, :], i=i)
            act.wait_ge(emptied[5], drains[5].now())
            act.activation(sq, zz[:, 8:16, :], ACT.Square).then_inc(squared, 1)
            for n in range(2, 12):
                unit_hi(act, FIRST_UNIT["in2_v"] + n)
            first_hi("in2_gates")
            roots(512, 4)
            for n in range(8):
                split_and_drain("in2_gates", n, zz[:, 16 + n, :], ACT.Silu)
            with rolled(act, 1, [(drains[4], 4), (drains[5], 4)]) as i:
                for n in range(8):
                    split_and_drain("in2_gates", 8 + n, zz[:, i * 8 + 24 + n, :], ACT.Sigmoid, i=i)
            for n in range(16, 24):
                split_and_drain("in2_gates", n, zz[:, 16 + n, :], ACT.Sigmoid, ahead=n < 22)
            norm_square(512, 4)

            def exp_m(m):
                hd, qt = divmod(m, 2)
                nk = P * (qt + 1)
                c = m % 2
                act.activation(m_exp[:, c, 0:nk], m_s[:, c, 0:nk], ACT.Exp, bias=nmax[:, c:c + 1],
                               accum_out=sums[:, c:c + 1]).then_inc(exp_ready, 1)

            def evac_m(k, b):
                hd, qt = divmod(k, 2)
                nt = qt + 1
                act.activation(m_attn_t[:, hd % 2, 0:nt, qt * P:(qt + 1) * P],
                               ps[:, b, 0:nt * P].rearrange("p (a b) -> p a b", a=nt), ACT.Copy).then_inc(emptied[b], 1)

            attention(16, exp_m, evac_m)
            for n in range(KC):
                drain(4 + n % 2, y_a[:, n, :])
            for n in range(KC):
                drain(4 + n % 2, y_b[:, n, :])
            for n in range(KC):
                drain(4 + n % 2, branch[:, n, :])
            first_hi("peer_q")
            act.wait_ge(block1_done, 2)
            act.activation(sq, resid[:, :, :], ACT.Square).then_inc(squared, 1)
            roots(T)
            half_h(param("ffn_g", 0, 8), None, h_hi_3)
            with rolled(act, 1, [(drains[4], 4), (drains[5], 4)]) as i:
                for n in range(8):
                    split_and_drain("peer_q", n, qp[:, i * 8 + n, :], i=i)
            for n in range(8, 16):
                split_and_drain("peer_q", n, qp[:, n, :], ahead=n < 14)
            first_hi("peer_u")
            with rolled(act, 12, [(drains[4], 4), (drains[5], 4)]) as i:
                for n in range(8):
                    split_and_drain("peer_u", n, act_e[:, i * 8 + n, :], ACT.Gelu, i=i)
            act.wait_ge(topk_done, 1)
            for tt in range(2):
                act.activation(found[tt][:, 2, :], found[tt][:, 2, :], ACT.Exp).then_inc(gate_exp, 1)
            with rolled(act, 4, [(drains[4], 4), (drains[5], 4)]) as i:
                for n in range(8):
                    split_and_drain("peer_u", 96 + n, act_e[:, i * 8 + 96 + n, :], ACT.Gelu, i=i)
            unit_hi(act, FIRST_UNIT["peer_v"] + 2)
            act.wait_ge(gated, 1)

            def expert_hi(e, i=None, row=None):
                if e >= 3:
                    unit_hi(act, FIRST_UNIT["peer_v"] + e, i)
                act.activation(e_hi[:, e % 4, :], act_e[:, e if row is None else row, :], ACT.Copy).then_inc(e_hi_ready, 1)

            for e in range(8):
                expert_hi(e)
            with rolled(act, N_EXP // 8 - 1, []) as i:
                for e in range(8):
                    expert_hi(8 + e, i, i * 8 + 8 + e)
            act.wait_ge(final, 1)
            act.dma_start(out, resid[:, :, :]).then_inc(stored, 16)
            act.wait_ge(stored, 16)

        @block.vector
        def _(dve):
            steps = Count()
            reads = {b: Count() for b in (0, 1, 2, 3, 6, 7)}

            def step(ins):
                ins.then_inc(dve_step, 1)
                steps.add()

            def settle():
                dve.wait_ge(dve_step, steps.now())

            def filled(b):
                dve.wait_ge(full[b], reads[b].add())

            def spread(a, n):
                return a.unsqueeze(1).broadcast_to([P, n, a.shape[-1]])

            n_rstd = Count()

            dve.wait_ge(inputs, 16 * 8)
            step(dve.tensor_tensor(lamw, lamb[:, 0:4:2, :], lamb[:, 1:4:2, :], ALU.mult))
            settle()
            dve.tensor_reduce(lam2, lamw, AX_X, ALU.add).then_inc(lam_sum, 1)
            filled(7)
            step(dve.tensor_copy(rowbuf[0:8, :], ps[0:8, 7, 0:DIST]))
            settle()
            dve.tensor_tensor(rowbuf[0:8, :], rowbuf[0:8, :], dmask[0:8, :], ALU.add).then_inc(row_ready, 1)
            dve.wait_ge(row_ready, 1)
            dve.sem_inc(emptied[7], 1)
            step(dve.tensor_scalar(gsub, param("subln_g"), 1.0 - LAM_INIT, None, ALU.mult))
            step(dve.tensor_scalar(mqg, param("mq_g"), SCALE, None, ALU.mult))
            dve.wait_ge(act_step, 1)
            step(dve.tensor_tensor(nlam, lam2[:, 1:2], lam2[:, 0:1], ALU.subtract))
            settle()
            step(dve.tensor_scalar(nlam, nlam, -LAM_INIT, None, ALU.add))

            for l in range(2):
                with rolled(dve, ADA_UNITS // 8, [(reads[6], 1), (reads[7], 1)]) as i:
                    for g in range(2):
                        filled(6 + g)
                        at = i * 8 + 4 * g
                        dve.tensor_tensor(mod[l][:, bass.ds(at, 4), :],
                                          ps[:, 6 + g, 0:8].rearrange("p (a b) -> p a b", b=2),
                                          par[:, bass.ds(PARAM[f"ada_b{l}"] + at, 4)].unsqueeze(2)
                                          .broadcast_to([P, 4, 2]), ALU.add).then_inc(emptied[6 + g], 1)
            dve.wait_ge(emptied[7], reads[7].now())
            dve.tensor_scalar(sc1p, mod[0][:, SC1:SC1 + 8, :], 1.0, None, ALU.add).then_inc(mod_cols, 1)
            dve.wait_ge(mod_cols, 1)
            for kc in range(KC):
                m = dve.tensor_scalar(hcat[:, kc, T:2 * T], resid[:, kc, :], sc1p[:, kc, 0:1],
                                      mod[0][:, SH1 + kc, 0:1], ALU.mult, ALU.add)
            m.then_inc(h_dve, 1)
            dve.wait_ge(h_dve, 1)
            step(dve.tensor_scalar(resid[:, :, :], resid[:, :, :], ALPHA, None, ALU.mult))

            for tt in range(4):
                filled(tt)
                dve.tensor_copy(av[:, tt, :], ps[:, tt, :]).then_inc(emptied[tt], 1)
            filled(6)
            dve.tensor_copy(bv.rearrange("p a b -> p (a b)"), ps[:, 6, :]).then_inc(emptied[6], 1)

            def rope(b, zs, n, cos, sin):
                filled(b)
                ra, rb = rope_a[:, 0:n, :], rope_b[:, 0:n, :]
                dve.tensor_tensor(ra, ps[:, b, 0:n * T].rearrange("p (a b) -> p a b", a=n), spread(const(sin, T), n),
                                  ALU.mult).then_inc(emptied[b], 1)
                step(dve.tensor_tensor(rb, zs, spread(const(cos, T), n), ALU.mult))
                settle()
                step(dve.tensor_tensor(zs, ra, rb, ALU.add))
                settle()

            def variance(b, n=512):
                k = n_rstd.add()
                filled(b)
                dve.tensor_scalar(vare[:, (k - 1) % 2, 0:n], ps[:, b, 0:n], EPS, None, ALU.add).then_inc(var_ready, 1)
                dve.wait_ge(var_ready, k)
                dve.sem_inc(emptied[b], 1)
                return k

            def inverse_root(k, n=512):
                s = (k - 1) % 2
                dve.wait_ge(std_ready, k)
                step(dve.reciprocal(rstd[:, s, 0:n], vare[:, s, 0:n]))
                settle()
                return rstd[:, s, 0:n]

            def scaled_by_roots(banks, apply):
                ks = []
                for f in range(len(banks) + 1):
                    if f < len(banks):
                        ks.append(variance(banks[f]))
                    if f >= 1:
                        apply(f - 1, inverse_root(ks[f - 1]))

            for f in range(2):
                rope(6 + f, zq[:, 2 * f:2 * f + 2, :], 2, "cos_2d", "sin_2d")
            for f in range(2):
                rope(6 + f, zk[:, 2 * f:2 * f + 2, T:2 * T], 2, "cos_2d", "sin_2d")
            flat_q = zq.rearrange("p a b -> p (a b)")
            normed_b = ((flat_q[:, 1024:1536], "qn_g"), (flat_q[:, 1536:2048], "qn_g"), (zk[:, 4, :], "kn_g"))

            def norm_bqk(f, inverse):
                dst, g = normed_b[f]
                step(dve.scalar_tensor_tensor(out=dst, in0=dst, scalar=param(g), in1=inverse, op0=ALU.mult,
                                              op1=ALU.mult))

            scaled_by_roots((6, 7, 6), norm_bqk)
            settle()
            dve.sem_inc(roped, 1)
            rope(7, zq[:, 4:6, :], 2, "cos_2d", "sin_2d")
            rope(6, zq[:, 6:8, :], 2, "cos_2d", "sin_2d")
            rope(7, zk[:, 4:5, T:2 * T], 1, "cos_2d", "sin_2d")
            dve.sem_inc(qk_ready, 1)

            n_exp = Count()

            def attention(n_maps, max_of, norm_of, values_of):
                for m in range(n_maps + 1):
                    if m < n_maps:
                        max_of(m)
                    if m >= 1:
                        norm_of(m - 1)
                        if m >= 4 and m % 2 == 0:
                            values_of(m // 2 - 2)
                values_of(n_maps // 2 - 1)

            def max_a(m):
                c = 2 * (m % 2)
                for i in range(2):
                    filled(c + i)
                    step(dve.tensor_reduce(nmax[:, c + i:c + i + 1], ps[:, c + i, :], AX_X, ALU.max, negate=True))
                settle()
                dve.tensor_scalar(nmax[:, c:c + 2], nmax[:, c:c + 2], SCALE, None, ALU.mult).then_inc(nmax_ready, 1)

            def norm_a(m):
                c = 2 * (m % 2)
                dve.wait_ge(exp_ready, n_exp.add(2))
                for i in range(2):
                    dve.sem_inc(emptied[c + i], 1)
                step(dve.reciprocal(inv[:, c:c + 2], sums[:, c:c + 2]))
                settle()
                step(dve.tensor_tensor(inv[:, c + 1:c + 2], inv[:, c + 1:c + 2], nlam, ALU.mult))
                step(dve.tensor_scalar(pexp[:, c, :], pexp[:, c, :], inv[:, c:c + 1], None, ALU.mult))
                settle()
                dve.scalar_tensor_tensor(out=attn[:, m % 2, :], in0=pexp[:, c + 1, :], scalar=inv[:, c + 1:c + 2],
                                         in1=pexp[:, c, :], op0=ALU.mult, op1=ALU.add).then_inc(attn_ready, 1)

            def values_a(hd):
                b = 6 + hd % 2
                filled(b)
                dve.tensor_copy(o_a[:, hd, :], ps[:, b, 0:T]).then_inc(emptied[b], 1)

            def max_b(m):
                c = m % 4
                filled(c)
                step(dve.tensor_reduce(nmax[:, c:c + 1], ps[:, c, :], AX_X, ALU.max, negate=True))
                settle()
                dve.tensor_scalar(nmax[:, c:c + 1], nmax[:, c:c + 1], SCALE, None, ALU.mult).then_inc(nmax_ready, 1)

            def norm_b(m):
                c = m % 4
                dve.wait_ge(exp_ready, n_exp.add())
                dve.sem_inc(emptied[c], 1)
                step(dve.reciprocal(inv[:, c:c + 1], sums[:, c:c + 1]))
                settle()
                dve.tensor_scalar(attn[:, m % 2, :], pexp[:, c, :], inv[:, c:c + 1], None,
                                  ALU.mult).then_inc(attn_ready, 1)

            def values_b(hd):
                if hd % 2 == 0:
                    return
                jt = hd // 2
                filled(6 + jt % 2)
                dve.tensor_copy(mix[:, 4 + jt, :], ps[:, 6 + jt % 2, 0:T]).then_inc(emptied[6 + jt % 2], 1)

            attention(8, max_a, norm_a, values_a)
            dve.wait_ge(emptied[7], reads[7].n)
            dve.sem_inc(o_ready, 1)
            attention(16, max_b, norm_b, values_b)
            flat_o, flat_m = o_a.rearrange("p a b -> p (a b)"), mix.rearrange("p a b -> p (a b)")

            def norm_o(f, inverse):
                c = slice(512 * f, 512 * (f + 1))
                step(dve.scalar_tensor_tensor(out=flat_m[:, c], in0=flat_o[:, c], scalar=gsub, in1=inverse,
                                              op0=ALU.mult, op1=ALU.mult))

            scaled_by_roots((6, 7), norm_o)
            settle()
            dve.sem_inc(mix_ready, 1)

            def wait_branch(name):
                dve.wait_ge(emptied[4], mark[name][0])
                dve.wait_ge(emptied[5], mark[name][1])

            def fold(ln, md, sc, sh):
                g, b = param("ln_g", 8 * ln, 8), param("ln_b", 8 * ln, 8)
                dve.wait_ge(h_act, n_hact.now())
                step(dve.tensor_scalar(ga_, g, ALPHA, None, ALU.mult))
                step(dve.tensor_scalar(ba_, b, ALPHA, None, ALU.mult))
                step(dve.tensor_scalar(exps, mod[md][:, sc:sc + 8, 0], 1.0, None, ALU.add))
                settle()
                step(dve.tensor_tensor(gs, g, exps, ALU.mult))
                step(dve.tensor_tensor(bs, b, exps, ALU.mult))
                settle()
                step(dve.tensor_tensor(bs, bs, mod[md][:, sh:sh + 8, 0], ALU.add))

            def half_h(scale, bias_, h_hi):
                for kc in range(4):
                    if bias_ is None:
                        m = dve.tensor_scalar(h[:, kc, :], zc[:, kc, :], scale[:, kc:kc + 1], None, ALU.mult)
                    else:
                        m = dve.tensor_scalar(h[:, kc, :], zc[:, kc, :], scale[:, kc:kc + 1], bias_[:, kc:kc + 1],
                                              ALU.mult, ALU.add)
                m.then_inc(h_own, 1)
                dve.wait_ge(h_own, n_h_own.add())
                dve.tensor_copy(h_hi[:, 0:4, :], h[:, 0:4, :]).then_inc(h_dve, 1)
                dve.wait_ge(h_dve, n_h_own.n + 1)
                dve.tensor_tensor(h_lo[:, 0:4, :], h[:, 0:4, :], h_hi[:, 0:4, :], ALU.subtract)
                dve.wait_ge(h_act, n_hact.add())
                dve.tensor_tensor(h_lo[:, 4:8, :], h[:, 4:8, :], h_hi[:, 4:8, :],
                                  ALU.subtract).then_inc(h_lo_ready, 1)

            def centre():
                filled(6)
                dve.tensor_tensor(zc, z, spread(ps[:, 6, 0:T], KC), ALU.subtract).then_inc(centred, 1)

            n_cent, n_hact, n_h_own = Count(), Count(), Count()
            n_hact.add()

            def layer_norm(to_h):
                centre()
                dve.wait_ge(centred, n_cent.add())
                dve.sem_inc(emptied[6], 1)
                k = variance(7, T)
                dve.tensor_tensor(zc, zc, spread(inverse_root(k, T), KC), ALU.mult).then_inc(
                    normed if to_h else dve_step, 1)
                if to_h:
                    dve.wait_ge(normed, n_normed.add())
                    half_h(gs, bs, h_hi_1)
                    for kc in range(KC):
                        step(dve.tensor_scalar(resid[:, kc, :], zc[:, kc, :], ga_[:, kc:kc + 1], ba_[:, kc:kc + 1],
                                               ALU.mult, ALU.add))
                    settle()
                else:
                    steps.add()
                    settle()

            n_normed = Count()

            def mixer_norm(l, name):
                fold(2 * l, l, SC2, SH2)
                wait_branch(name)
                settle()
                dve.tensor_tensor(z, branch, resid[:, :, :], ALU.add).then_inc(summed, 1)
                layer_norm(True)

            def mlp_norm(l):
                if l == 0:
                    fold(1, 1, SC1, SH1)
                    settle()
                for n in range(KC):
                    b = n // 2
                    if n % 2 == 0:
                        filled(b)
                    m = dve.scalar_tensor_tensor(out=z[:, n, :], in0=ps[:, b, (n % 2) * T:(n % 2 + 1) * T],
                                                 scalar=mod[l][:, G2 + n, 0:1], in1=resid[:, n, :],
                                                 op0=ALU.mult, op1=ALU.add)
                    if n == KC - 1:
                        m.then_inc(summed, 1)
                    elif n % 2 == 1:
                        m.then_inc(emptied[b], 1)
                dve.wait_ge(summed, 2 * l + 2)
                dve.sem_inc(emptied[3], 1)
                layer_norm(l == 0)

            n_hid = Count()

            def split_hidden(u0):
                def hidden(j):
                    dve.wait_ge(hid_ready, n_hid.add())
                    dve.tensor_copy(hid_hi[:, j % 2, :], hid2[:, j % 2, :]).then_inc(hid_hi_ready, 1)
                    dve.wait_ge(hid_hi_ready, n_hid.now())
                    dve.tensor_tensor(hid_lo[:, j % 2, :], hid2[:, j % 2, :], hid_hi[:, j % 2, :],
                                      ALU.subtract).then_inc(hid_lo_ready, 1)

                unit_lo(dve, u0)
                with rolled(dve, 7, [(n_hid, 4)]) as i:
                    for j in range(4):
                        hidden(j)
                        unit_lo(dve, u0 + 2 * j + 2, i)
                for j in range(28, 32):
                    hidden(j)
                    if j < 31:
                        unit_lo(dve, u0 + 2 * j + 2)

            mixer_norm(0, "attn_out")
            split_hidden(FIRST_UNIT["mlp0"])
            mlp_norm(0)
            step(dve.memset(conv_u[:, :, 0:1], 0.0))
            step(dve.memset(conv_u[:, :, T + 1:T + 2], 0.0))
            dve.wait_ge(emptied[4], mark["conv_gb"][0] - 4)
            dve.wait_ge(emptied[5], mark["conv_gb"][1] - 4)
            step(dve.tensor_tensor(conv_u[:, :, 1:T + 1], conv_z[:, 0:8, :], conv_z[:, 8:16, :], ALU.mult))
            settle()
            for kc in range(KC):
                step(dve.tensor_scalar(conv_y[:, kc, :], conv_u[:, kc, 0:T], param("conv_w", kc), param("conv_b", kc),
                                       ALU.mult, ALU.add))
            for tap in (1, 2):
                settle()
                for kc in range(KC):
                    step(dve.scalar_tensor_tensor(out=conv_y[:, kc, :], in0=conv_u[:, kc, tap:tap + T],
                                                  scalar=param("conv_w", 8 * tap + kc), in1=conv_y[:, kc, :],
                                                  op0=ALU.mult, op1=ALU.add))
            settle()
            wait_branch("conv_gb")
            dve.tensor_tensor(conv_y, conv_y, conv_z[:, 16:24, :], ALU.mult).then_inc(mix_ready, 1)
            mixer_norm(1, "conv_out")
            split_hidden(FIRST_UNIT["mlp1"])
            mlp_norm(1)
            for kc in range(KC):
                m = dve.tensor_scalar(resid[:, kc, :], zc[:, kc, :], param("ln_g", 24 + kc), param("ln_b", 24 + kc),
                                      ALU.mult, ALU.add)
            m.then_inc(block1_done, 1)

            n_b1 = Count()

            def rms_norm(g, h_hi):
                dve.wait_ge(block1_done, n_b1.add())
                k = variance(6, T)
                dve.tensor_tensor(zc, resid[:, :, :], spread(inverse_root(k, T), KC), ALU.mult).then_inc(normed, 1)
                dve.wait_ge(normed, n_normed.add())
                half_h(param(g, 0, 8), None, h_hi)

            rms_norm("mix_g", h_hi_2)
            for v in range(3):
                for tt in range(2):
                    dst = rv[:, tt, 512 * v:512 * (v + 1)] if v < 2 else mv[:, tt, :]
                    filled(tt)
                    dve.tensor_copy(dst, ps[:, tt, :]).then_inc(emptied[tt], 1)
            flat_z = zz.rearrange("p a b -> p (a b)")

            def norm_mqk(f, inverse):
                dst = flat_z[:, 2048 + 512 * f:2048 + 512 * (f + 1)]
                step(dve.scalar_tensor_tensor(out=dst, in0=dst, scalar=mqg if f < 2 else param("mk_g"), in1=inverse,
                                              op0=ALU.mult, op1=ALU.mult))

            scaled_by_roots((6, 7, 6, 7), norm_mqk)
            for f in range(4):
                rope(6 + f % 2, zz[:, 2 * f:2 * f + 2, :], 2, "cos_1d", "sin_1d")
            dve.sem_inc(qk_ready, 1)
            dve.wait_ge(dec_in, 16)

            def ret_copy(hd):
                b = 6 + hd % 2
                filled(b)
                dve.tensor_copy(ret[:, hd, :], ps[:, b, 0:T]).then_inc(emptied[b], 1)

            for hd in range(8):
                b = hd % 4
                filled(b)
                dve.tensor_tensor(sdec[:, hd % 2, :], ps[:, b, 0:DEC], dec[:, hd, :], ALU.mult).then_inc(sdec_ready, 1)
                dve.wait_ge(sdec_ready, hd + 1)
                dve.sem_inc(emptied[b], 1)
                if hd >= 1:
                    ret_copy(hd - 1)
            ret_copy(7)
            dve.wait_ge(emptied[7], reads[7].n)
            dve.sem_inc(o_ready, 1)
            flat_r, flat_c = ret.rearrange("p a b -> p (a b)"), zc.rearrange("p a b -> p (a b)")
            for f in range(4):
                filled(6 + f % 2)
                c = slice(512 * f, 512 * (f + 1))
                dve.tensor_tensor(flat_c[:, c], flat_r[:, c], ps[:, 6 + f % 2, :], ALU.subtract).then_inc(
                    emptied[6 + f % 2], 1)
            dve.wait_ge(emptied[7], reads[7].n)
            dve.sem_inc(centred, 1)
            n_cent.add()
            wait_branch("gates")

            def norm_ret(f, inverse):
                c = slice(512 * f, 512 * (f + 1))
                step(dve.tensor_tensor(flat_c[:, c], flat_c[:, c], inverse, ALU.mult))
                settle()
                step(dve.tensor_tensor(flat_r[:, c], flat_c[:, c], flat_z[:, 4096 + 512 * f:4096 + 512 * (f + 1)],
                                       ALU.mult))

            scaled_by_roots((6, 7, 6, 7), norm_ret)
            settle()
            dve.sem_inc(mix_ready, 1)

            dve.wait_ge(bias_in, 16)

            def max_m(m):
                hd, qt = divmod(m, 2)
                nk = P * (qt + 1)
                filled(m % 4)
                dve.tensor_tensor(m_s[:, m % 2, 0:nk], ps[:, m % 4, 0:nk], bias[:, hd, T - nk:T],
                                  ALU.add).then_inc(emptied[m % 4], 1)
                dve.wait_ge(emptied[m % 4], reads[m % 4].n)
                dve.tensor_reduce(nmax[:, m % 2:m % 2 + 1], m_s[:, m % 2, 0:nk], AX_X, ALU.max,
                                  negate=True).then_inc(nmax_ready, 1)

            def norm_m(m):
                nk = P * (m % 2 + 1)
                c = m % 2
                dve.wait_ge(exp_ready, n_exp.add())
                step(dve.reciprocal(inv[:, c:c + 1], sums[:, c:c + 1]))
                settle()
                dve.tensor_scalar(m_attn[:, c, 0:nk], m_exp[:, c, 0:nk], inv[:, c:c + 1], None,
                                  ALU.mult).then_inc(attn_ready, 1)

            def values_m(hd):
                if hd % 2 == 0:
                    return
                jt = hd // 2
                filled(6 + jt % 2)
                m = dve.tensor_copy(att[:, jt, :], ps[:, 6 + jt % 2, 0:T])
                m.then_inc(emptied[6 + jt % 2], 1)

            attention(16, max_m, norm_m, values_m)
            dve.wait_ge(emptied[7], reads[7].n)
            dve.sem_inc(mix_ready, 1)
            wait_branch("ret_out")
            step(dve.tensor_tensor(y_a, y_a, zz[:, 24:32, :], ALU.mult))
            wait_branch("moba_out")
            step(dve.tensor_tensor(y_b, y_b, zz[:, 32:40, :], ALU.mult))
            settle()
            dve.tensor_tensor(merged, y_a, y_b, ALU.add).then_inc(mix_ready, 1)
            wait_branch("out2")
            dve.tensor_tensor(resid[:, :, :], resid[:, :, :], branch, ALU.add).then_inc(block1_done, 1)
            rms_norm("ffn_g", h_hi_3)

            for un in range(2):
                for tt in range(2):
                    for g4 in range(2):
                        b = 2 * tt + g4
                        filled(b)
                        hc = 8 * un + 4 * g4
                        dve.tensor_copy(sco[:, tt, hc:hc + 4, :].rearrange("p a b -> p (a b)"),
                                        ps[:, b, :]).then_inc(emptied[b], 1)
            for b in range(4):
                dve.wait_ge(emptied[b], reads[b].n)

            def top16(vals, idx, src, n):
                for r in range(n):
                    step(dve.max(vals(r)[:, 0:8], src(r)))
                settle()
                for r in range(n):
                    step(dve.max_index(idx(r)[:, 0:8], vals(r)[:, 0:8], src(r)))
                settle()
                for r in range(n):
                    step(dve.match_replace(src(r), vals(r)[:, 0:8], src(r), TAKEN))
                settle()
                for r in range(n):
                    step(dve.max(vals(r)[:, 8:16], src(r)))
                settle()
                for r in range(n):
                    step(dve.max_index(idx(r)[:, 8:16], vals(r)[:, 8:16], src(r)))
                settle()

            v16 = top_v.rearrange("p h c k -> p (h c) k")
            i16 = top_i.rearrange("p h c k -> p (h c) k")
            bu = best_u.rearrange("p (h k) -> p h k", h=8)
            hot4 = hot.rearrange("p (h k) a -> p h k a", h=8)
            cand4 = cand.rearrange("p h (a b) -> p h a b", a=TOPK)
            for tt in range(2):
                top16(lambda r: v16[:, r, :], lambda r: top_iu[:, r, :], lambda r: sco[:, tt, r, :], 16)
                step(dve.tensor_copy(i16, top_iu))
                for hd in range(8):
                    step(dve.tensor_tensor(cand4[:, hd], top_v[:, hd, 0, :].unsqueeze(2).broadcast_to([P, TOPK, TOPK]),
                                           top_v[:, hd, 1, :].unsqueeze(1).broadcast_to([P, TOPK, TOPK]), ALU.add))
                settle()
                top16(lambda r: best_v[:, r, :], lambda r: bu[:, r, :], lambda r: cand[:, r, :], 8)
                for c, (op, by) in enumerate(((ALU.logical_shift_right, 4), (ALU.bitwise_and, 15))):
                    step(dve.tensor_scalar(pick_u, best_u, by, None, op))
                    settle()
                    step(dve.tensor_copy(pick, pick_u))
                    settle()
                    step(dve.tensor_tensor(hot, pick.unsqueeze(2).broadcast_to([P, P, TOPK]),
                                           spread(const("iota16", TOPK), P), ALU.is_equal))
                    settle()
                    for hd in range(8):
                        step(dve.tensor_tensor(hot4[:, hd], hot4[:, hd], spread(top_i[:, hd, c, :], TOPK), ALU.mult))
                    settle()
                    step(dve.tensor_reduce(found[tt][:, c, :], hot, AX_X, ALU.add))
                    settle()
                gates = found[tt][:, 2, :].rearrange("p (h k) -> p h k", h=8)
                step(dve.tensor_tensor(gates, best_v, best_v[:, :, 0:1].broadcast_to([P, 8, TOPK]), ALU.subtract))
            settle()
            dve.sem_inc(topk_done, 1)
            for tt in range(2):
                gates = found[tt][:, 2, :].rearrange("p (h k) -> p h k", h=8)
                dve.wait_ge(gate_exp, tt + 1)
                step(dve.tensor_reduce(exps, gates, AX_X, ALU.add))
                settle()
                step(dve.reciprocal(exps, exps))
                settle()
                dve.tensor_tensor(gates, gates, exps.unsqueeze(2).broadcast_to([P, 8, TOPK]),
                                  ALU.mult).then_inc(half_found, 1)
                dve.wait_ge(half_found, tt + 1)
            for a, dst in enumerate((i1_t, i2_t, gate_t)):
                filled(6 + a % 2)
                m = dve.tensor_copy(dst, ps[:, 6 + a % 2, 0:T])
                m.then_inc(emptied[6 + a % 2], 1)
            for b in (6, 7):
                dve.wait_ge(emptied[b], reads[b].n)
            dve.sem_inc(topk_done, 1)

            def one_hots(b, t0):
                for t in range(4):
                    m = dve.tensor_scalar(hot1[:, b, t, :], const("iota"), i1_t[:, bass.ds(t0 + t, 1)],
                                          gate_t[:, bass.ds(t0 + t, 1)], ALU.is_equal, ALU.mult)
                m.then_inc(hot1_ready, 1)

            def gate(b, t0):
                filled(b)
                a = act_e[:, :, bass.ds(t0, 4)]
                dve.tensor_tensor(a, a, ps[:, b, :].rearrange("p (t e) -> p e t", t=4), ALU.mult).then_inc(emptied[b], 1)

            dve.wait_ge(emptied[4], mark["peer_u"][0])
            dve.wait_ge(emptied[5], mark["peer_u"][1])
            one_hots(0, 0)
            with rolled(dve, T // 8 - 1, [(reads[0], 1), (reads[1], 1)]) as i:
                one_hots(1, i * 8 + 4)
                gate(0, i * 8)
                one_hots(0, i * 8 + 8)
                gate(1, i * 8 + 4)
            one_hots(1, T - 4)
            gate(0, T - 8)
            gate(1, T - 4)
            dve.wait_ge(emptied[1], reads[1].n)
            dve.sem_inc(gated, 1)

            def expert_lo(e, i=None, row=None):
                dve.wait_ge(e_hi_ready, at_trip(i, TRIP, e + 1))
                dve.tensor_tensor(e_lo[:, e % 4, :], act_e[:, e if row is None else row, :], e_hi[:, e % 4, :],
                                  ALU.subtract).then_inc(e_lo_ready, 1)
                if e % 2 == 0:
                    unit_lo(dve, FIRST_UNIT["peer_v"] + e, i)

            for e in range(8):
                expert_lo(e)
            with rolled(dve, N_EXP // 8 - 1, []) as i:
                for e in range(8):
                    expert_lo(8 + e, i, i * 8 + 8 + e)
            for b in range(4):
                filled(b)
                m = dve.tensor_tensor(resid[:, 2 * b:2 * b + 2, :], resid[:, 2 * b:2 * b + 2, :],
                                      ps[:, b, :].rearrange("p (a b) -> p a b", a=2), ALU.add)
            m.then_inc(final, 1)

        @block.gpsimd
        def _(pool):
            def units_lo(stage, trips, which=range(TRIP)):
                with pool.Fori(0, trips) as i:
                    for n in which:
                        unit_lo(pool, FIRST_UNIT[stage] + n, i)

            odd = range(1, TRIP, 2)
            units_lo("mlp0", 8, odd)
            units_lo("conv_in", 3)
            units_lo("mlp1", 8, odd)
            units_lo("in2_qk", 6)
            for n in range(20, 24):
                unit_lo(pool, FIRST_UNIT["in2_gates"] + n)
            units_lo("peer_q", 2)
            units_lo("peer_u", 16)
            pool.wait_ge(topk_done, 2)
            with pool.Fori(0, T // 8) as i:
                for b in range(2):
                    pool.wait_ge(full[b], i + mark["hot"][b])
                    pool.tensor_copy(i2_now[:, b, :], i2_t[:, bass.ds(i * 8 + 4 * b, 4)]).then_inc(pool_step, 1)
                    pool.wait_ge(pool_step, i * 2 + (1 + b))
                    pool.sem_inc(i2_copied, 1)
                    for t in range(4):
                        m = pool.tensor_scalar(hot2[:, b, t, :], const("iota"), i2_now[:, b, t:t + 1], None,
                                               ALU.is_equal)
                    m.then_inc(hot2_ready, 1)
            units_lo("peer_v", 16, odd)

        @block.sync
        def _(sp):
            def load(v, s):
                sp.dma_start(ring[:, s, :], stream[v]).then_inc(landed[s], 16)

            for s in range(RING):
                load(s, s)
            with sp.Fori(1, N_UNITS // RING) as r:
                for s in range(RING):
                    sp.wait_ge(units_begun, r * RING + (s + 2 - RING))
                    load(r * RING + s, s)
            for v in range(N_UNITS // RING * RING, N_UNITS):
                sp.wait_ge(units_begun, v + 2 - RING)
                load(v, v % RING)


def _constants():
    c = np.zeros((P, N_CONST), np.float32)

    def put(name, a):
        c[:, CONST[name]:CONST[name] + a.shape[1]] = a

    put("ident", np.eye(P))
    put("mean_d", np.full((P, P), 1.0 / D))
    put("mean_64", np.kron(np.eye(2), np.full((HEAD, HEAD), 1.0 / HEAD)))
    put("mean_128", np.full((P, P), 1.0 / P))
    f = np.arange(HEAD)

    def rotation(half):
        r = np.zeros((HEAD, HEAD))
        first = f % (2 * half) < half
        r[f[first], f[first] + half] = -1.0
        r[f[~first], f[~first] - half] = 1.0
        return np.kron(np.eye(2), r).T

    put("rot_2d", rotation(HEAD // 4))
    put("rot_1d", rotation(HEAD // 2))
    put("iota", np.tile(np.arange(P), (P, 1)))
    put("iota16", np.tile(np.arange(TOPK), (P, 1)))
    t = np.arange(T)
    nf = HEAD // 4
    inv_freq = np.float32(10000.0) ** (-np.arange(nf, dtype=np.float32) / nf)
    where = np.stack([t // 64, t % 64]).astype(np.float32)
    ang = (where[f // 32] * inv_freq[f % nf][:, None]).astype(np.float32)
    put("cos_2d", np.tile(np.cos(ang), (2, 1)))
    put("sin_2d", np.tile(np.sin(ang), (2, 1)))
    half = HEAD // 2
    inv = np.float32(10000.0) ** (-np.arange(half, dtype=np.float32) / half)
    ang = (t[None].astype(np.float32) * inv[f % half][:, None]).astype(np.float32)
    put("cos_1d", np.tile(np.cos(ang), (2, 1)))
    put("sin_1d", np.tile(np.sin(ang), (2, 1)))
    return c


def _decay():
    log_g = np.log1p(-np.exp2(-5.0 - np.arange(8)))
    rel = np.arange(T)[None, :] - np.arange(P)[:, None]
    d = np.where(rel[:, None, :] >= 0, np.exp(np.maximum(rel, 0)[:, None, :] * log_g[None, :, None]), 0.0) * SCALE
    return np.concatenate([d, d[:, :, 0:P]], axis=2).astype(np.float32)


def _distances():
    import math
    dist = 255 - np.arange(DIST)
    n = np.maximum(dist, 0)
    nf = np.maximum(n, 1).astype(np.float32)
    large = 16 + (np.log(nf / np.float32(16)) / np.float32(math.log(2048 / 16)) * np.float32(16)).astype(np.int32)
    bucket = np.where(n < 16, n, np.minimum(large, 31))
    onehot = (np.arange(32)[:, None] == bucket[None]).astype(np.float32)
    mask = np.where(dist < 0, np.float32(MASKED), np.float32(0.0))
    return onehot, np.tile(mask, (8, 1)).astype(np.float32)


def _units(a):
    def tiles(w):
        return w.reshape(KC, P, -1, P).transpose(2, 1, 0, 3).reshape(-1, P, UNIT)

    def wide(w):
        return w.reshape(4, 2, P, -1, 512).transpose(3, 0, 2, 1, 4).reshape(-1, P, UNIT)

    def mlp(w1, w2):
        up, down = tiles(w1), w2.reshape(HID_TILES, P, UNIT)
        body = np.stack([up[1:], down[:-1]], axis=1).reshape(-1, P, UNIT)
        return [up[:1], body, down[-1:]]

    w = a["attn_w_in"][0]
    aq, ak, v, bq, bk, bvw = np.split(w, [512, 1024, 1536, 2048, 2176], axis=1)
    bq = bq.reshape(D, 2, 4, HEAD).transpose(0, 2, 1, 3).reshape(D, 512)
    wo = a["attn_w_out"][0]
    wo_b = wo[512:].reshape(2, 4, HEAD, D).transpose(1, 0, 2, 3).reshape(512, D)
    w2 = a["w_in_2"][0]
    rq, rk, rvw, rg, mq, mk, mvw, ga, gb = np.split(w2, np.cumsum([512, 512, 1024, 1024, 512, 512, 512, 1024]), axis=1)
    gate_b, gate_c, xv = np.split(a["conv_w_in"][0], 3, axis=1)
    keys = a["peer_sub_keys_2"][0].reshape(16, N_EXP, P)
    u = a["peer_u_2"][0].reshape(N_EXP, N_EXP, KC, P)
    return [
        wide(a["ada_w"][0]), wide(a["ada_w"][1]),
        tiles(aq), tiles(bq), tiles(ak), wide(v), tiles(bk), tiles(bvw),
        tiles(np.concatenate([wo[:512], wo_b])), *mlp(a["mlp_w1"][0], a["mlp_w2"][0]),
        tiles(gate_c), tiles(xv), tiles(gate_b), tiles(a["conv_w_out"][0]), *mlp(a["mlp_w1"][1], a["mlp_w2"][1]),
        tiles(rq), tiles(rk), tiles(mq), tiles(mk), wide(rvw), wide(mvw), tiles(rg), tiles(ga), tiles(gb),
        tiles(a["ret_w_branch_2"][0]),
        a["moba_w_branch_2"][0].reshape(4, P, 4, 2 * P).transpose(2, 1, 0, 3).reshape(-1, P, UNIT),
        tiles(a["w_out_2"][0]), tiles(a["peer_w_q_2"][0]),
        keys.transpose(2, 0, 1).reshape(P, 2, UNIT).transpose(1, 0, 2),
        u.transpose(1, 3, 2, 0).reshape(N_EXP, P, UNIT),
        a["peer_v_2"][0].reshape(N_EXP, N_EXP, UNIT).transpose(1, 0, 2),
    ]


def _params(a):
    def cols(v):
        return np.ascontiguousarray(v).reshape(-1, P).T

    twice = lambda v: np.tile(v.reshape(-1), 2).reshape(P, 1)
    c = np.stack([a["c"][0], a["c_ctx"]], axis=-1).reshape(KC, P, 2).transpose(1, 0, 2).reshape(P, 16)
    parts = [c, cols(a["ada_b"][0]), cols(a["ada_b"][1]), cols(a["ln_g"]), cols(a["ln_b"]), cols(a["mix_norm_g_2"]),
             cols(a["ffn_norm_g_2"]), cols(a["conv_w"]), cols(a["conv_b"]), a["diff_subln_g"].reshape(P, 1),
             twice(a["q_norm_g"]), twice(a["k_norm_g"]), twice(a["moba_q_gain_2"]), twice(a["moba_k_gain_2"])]
    return np.ascontiguousarray(np.concatenate(parts, axis=1))


def kernel(**inputs):
    import concourse.bacc as bacc
    from concourse.bass_utils import run_bass_kernel_spmd

    a = {k: np.asarray(v) for k, v in inputs.items()}
    parts = _units(a)
    stream = np.empty((N_UNITS, P, UNIT), np.float32)
    at = 0
    for p in parts:
        stream[at:at + len(p)] = p
        at += len(p)
    assert at == N_UNITS

    def features(v):
        return np.ascontiguousarray(v.reshape(T, KC, P).transpose(2, 1, 0))

    onehot, dist_mask = _distances()
    arrays = {
        "stream": stream, "x_t": features(a["x"]), "ctx_t": features(a["ctx"]), "params": _params(a),
        "consts": _constants(), "decay": _decay(),
        "lam_in": np.ascontiguousarray(np.broadcast_to(a["diff_lambda"], (P, 4, HEAD))),
        "rel_bias": np.ascontiguousarray(a["rel_bias_2"]), "onehot": onehot, "dist_mask": dist_mask,
    }
    nc = bacc.Bacc("TRN2", target_bir_lowering=False, num_devices=1)
    args = [nc.dram_tensor(n, v.shape, F32, kind="ExternalInput").ap() for n, v in arrays.items()]
    bias_rows = nc.dram_tensor("bias_rows", (8, P, DIST), F32).ap()
    out = nc.dram_tensor("out", (P, KC, T), F32, kind="ExternalOutput").ap()
    build(nc, *args, bias_rows, out)
    r = run_bass_kernel_spmd(nc, [arrays], core_ids=[0])
    y = r.results[0]["out"]
    return np.ascontiguousarray(y.transpose(2, 1, 0)).reshape(1, T, D)
```

```python
from contextlib import ExitStack, contextmanager

import numpy as np

import concourse.bass as bass
from concourse import mybir

F32 = mybir.dt.float32
F32R = mybir.dt.float32r
U32 = mybir.dt.uint32
ALU = mybir.AluOpType
ACT = mybir.ActivationFunctionType
AX_X = mybir.AxisListType.X

P = 128
T = 256
D = 1024
KC = D // P
RING = 4
TRIP = 8
UNIT = 1024
ALPHA = 4.0 ** 0.25
LAM_INIT = 0.2
EPS = 1e-6
HEAD = 64
SCALE = HEAD ** -0.5
N_EXP = 128
TOPK = 16
HID_TILES = 4 * D // P
MASKED = -1e30
TAKEN = -3.0e38
POOL_TOKENS = (2, 2, 2, 2)

ADA_UNITS = 48
EARLY_ADA = 40
STAGES = [("ada0", EARLY_ADA), ("attn_in", 18), ("ada_late", 2 * ADA_UNITS - EARLY_ADA), ("attn_out", 8), ("mlp0", 64),
          ("conv_in", 24), ("conv_out", 8), ("mlp1", 64), ("in2_qk", 16), ("in2_v", 12), ("in2_gates", 24),
          ("ret_out", 8), ("moba_out", 4), ("out2", 8), ("peer_q", 16), ("peer_keys", 2),
          ("peer_u", N_EXP), ("peer_v", N_EXP)]
FIRST_UNIT = {}
N_UNITS = 0
for _name, _n in STAGES:
    FIRST_UNIT[_name] = N_UNITS
    N_UNITS += _n
SPLIT_STAGES = ("mlp0", "conv_in", "mlp1", "in2_qk", "in2_v", "in2_gates", "peer_q", "peer_u", "peer_v")
IS_SPLIT = [_name in SPLIT_STAGES for _name, _n in STAGES for _ in range(_n)]
SPLIT_NO = np.cumsum(IS_SPLIT).tolist()
SPLIT_IN_SLOT = [sum(IS_SPLIT[v] for v in range(_u % RING, _u + 1, RING)) for _u in range(N_UNITS)]

PARAM = {}
N_PARAM = 0
for _name, _n in (("c", 16), ("ada_b0", 48), ("ada_b1", 48), ("ln_g", 32), ("ln_b", 32), ("mix_g", 8),
                  ("ffn_g", 8), ("conv_w", 24), ("conv_b", 8), ("subln_g", 1), ("qn_g", 1), ("kn_g", 1),
                  ("mq_g", 1), ("mk_g", 1)):
    PARAM[_name] = N_PARAM
    N_PARAM += _n

CONST = {}
N_CONST = 0
for _name, _n in (("ident", P), ("mean_d", P), ("mean_64", P), ("mean_128", P), ("rot_2d", P), ("rot_1d", P),
                  ("iota", P), ("iota16", TOPK), ("cos_2d", T), ("sin_2d", T), ("cos_1d", T), ("sin_1d", T)):
    CONST[_name] = N_CONST
    N_CONST += _n
DIST = 384
DEC = 384

SH1, SC1, G1, SH2, SC2, G2 = range(0, 48, 8)


class Count:

    def __init__(self):
        self.n, self.i, self.per = 0, None, 0

    def add(self, k=1):
        self.n += k
        return self.now()

    def now(self):
        return self.n if self.i is None else self.i * self.per + self.n


@contextmanager
def rolled(eng, trips, counts):
    was = {c: c.n for c, _ in counts}
    with eng.Fori(0, trips) as i:
        for c, per in counts:
            c.i, c.per = i, per
        yield i
        for c, per in counts:
            assert c.n - was[c] == per, (c.n, was[c], per)
    for c, per in counts:
        c.i, c.n = None, was[c] + per * trips


def build(nc, stream, x_t, ctx_t, params, consts, decay, lam_in, rel_bias, onehot, dist_mask, bias_rows, out):
    with ExitStack() as ctx:
        at = {}

        def sb(name, shape, dt=F32):
            t = ctx.enter_context(nc.sbuf_tensor(name, shape, dt))
            at[name] = nc.sbuf_base - 4 * int(np.prod(shape[1:]))
            return t

        def rounded(name, like, shape):
            return nc.alloc_sbuf_tensor_at(name, shape, F32R, offset=at[like])

        def sem(name):
            return ctx.enter_context(nc.semaphore(name))

        ring = sb("ring", [P, RING, UNIT])
        ring_hi = sb("ring_hi", [P, RING, UNIT], F32R)
        arena = sb("arena", [P, N_EXP * T])
        late = sb("late", [P, 4096])
        resid = sb("resid", [P, KC, T])
        h = sb("h", [P, KC, T])
        par = sb("par", [P, N_PARAM])
        cst = sb("cst", [P, N_CONST])
        mod = [sb(f"mod{l}", [P, 48, 2]) for l in range(2)]
        cact = sb("cact", [P, KC, 2])
        small = sb("small", [P, 160])

        ring_lo = rounded("ring_lo", "ring", [P, RING, UNIT])
        arena_r = rounded("arena_r", "arena", [P, 21504])
        late_r = rounded("late_r", "late", [P, 2048])
        h_lo = rounded("h_lo", "h", [P, KC, T])

        def param(name, k=0, n=1):
            a = PARAM[name] + k
            return par[:, a:a + n]

        def const(name, n=P):
            return cst[:, CONST[name]:CONST[name] + n]

        def area(at, *shape):
            size = int(np.prod(shape))
            a = arena[:, at:at + size]
            if len(shape) == 2:
                a = a.rearrange("p (a b) -> p a b", b=shape[1])
            if len(shape) == 3:
                a = a.rearrange("p (a b c) -> p a b c", b=shape[1], c=shape[2])
            return a

        branch = area(19456, KC, T)
        z = area(21504, KC, T)
        sq = area(23552, KC, T)
        zc = area(25600, KC, T)
        rope_a = area(27648, 2, T)
        rope_b = area(28160, 2, T)
        hid = area(28672, 2, T)
        hid2 = area(29184, 2, T)
        vare = area(29696, 2, 512)
        rstd = area(30720, 2, 512)
        h_hi_1 = arena_r[:, 10752:12800].rearrange("p (a b) -> p a b", a=KC)
        h_hi_2 = arena_r[:, 19456:21504].rearrange("p (a b) -> p a b", a=KC)
        h_hi_3 = late_r[:, :].rearrange("p (a b) -> p a b", a=KC)
        hid_hi = arena_r[:, 12800:13312].rearrange("p (a b) -> p a b", a=2)
        hid_lo = arena_r[:, 13312:13824].rearrange("p (a b) -> p a b", a=2)
        hcat = area(0, KC, 2 * T)
        zq = area(4096, 8, T)
        zk = area(6144, 5, 2 * T)
        av = area(8704, 4, 512)
        bv = area(10752, 4, P)
        pexp = area(11264, 4, 512)
        attn = area(13312, 2, 512)
        attn_t = area(14336, 2, 4, T)
        o_a = area(16384, 4, T)
        mix = area(17408, 8, T)
        conv_z = area(0, 24, T)
        conv_u = area(6144, KC, T + 2)
        conv_y = area(8208, KC, T)
        zz = area(0, 40, T)
        rv = area(10240, 2, D)
        mv = area(12288, 2, 512)
        dec = area(13312, 8, DEC)
        ret = area(16384, 8, T)
        att = area(18432, 4, T)
        sdec = area(31744, 2, DEC)
        m_s = area(27648, 2, T)
        m_exp = area(28160, 2, T)
        m_attn = area(28672, 2, T)
        m_attn_t = area(11264, 2, 2, T)
        y_a, y_b = area(0, KC, T), area(2048, KC, T)
        merged = area(10240, KC, T)
        qp = area(0, 16, T)
        act_e = area(0, N_EXP, T)
        QUARTER = 3 * N_EXP * T // 4
        sco = area(QUARTER, 2, 16, P)
        cand = area(QUARTER + 4096, 8, TOPK * TOPK)
        hot = area(QUARTER + 6144, P, TOPK)
        mod_row = late[:, 2048:3072].rearrange("p (b n) -> p b n", b=2)
        bias = late[:, 0:2048].rearrange("p (h k) -> p h k", h=8)
        rowbuf = late[:, 3072:3072 + DIST]
        relb = late[:, 3456:3464]
        lamb = late[:, 3464:3720].rearrange("p (a n) -> p a n", a=4)
        lamw = late[:, 3720:3848].rearrange("p (a n) -> p a n", a=2)
        dmask = late[:, 2048:2048 + DIST]
        oneh = late[:, 2432:2432 + DIST]
        e_pair = late_r[:, :].rearrange("p (s n) -> p s n", s=4)
        e_hi, e_lo = e_pair[:, :, 0:T], e_pair[:, :, T:2 * T]
        i1_t, i2_t, gate_t = late[:, 0:256], late[:, 256:512], late[:, 512:768]
        hot1 = late[:, 768:2816].rearrange("p (b t n) -> p b t n", b=4, t=4)
        hot2 = h[:, :, :].rearrange("p a (c n) -> p (a c) n", n=P).rearrange("p (b t) n -> p b t n", b=4)
        top_v = late[:, 2816:3072].rearrange("p (h c k) -> p h c k", h=8, c=2)
        top_i = late[:, 3072:3328].rearrange("p (h c k) -> p h c k", h=8, c=2)
        top_iu = late[:, 3328:3584].bitcast(U32).rearrange("p (h k) -> p h k", h=16)
        best_v = late[:, 3584:3712].rearrange("p (h k) -> p h k", h=8)
        best_u = late[:, 3712:3840].bitcast(U32)
        pick_u = late[:, 3840:3968].bitcast(U32)
        pick = late[:, 3968:4096]
        found = [cst[:, CONST["cos_2d"] + 384 * i:CONST["cos_2d"] + 384 * (i + 1)].rearrange("p (a n) -> p a n", a=3) for i in range(2)]

        i2_now = cst[:, CONST["cos_2d"] + 768:CONST["cos_2d"] + 784].rearrange("p (b t) -> p b t", b=4)
        nmax, sums, inv = small[:, 0:32], small[:, 32:64], small[:, 64:96]
        lam2, nlam, gsub = small[:, 96:98], small[:, 98:99], small[:, 99:100]
        mqg = small[:, 100:101]
        sc1p = small[:, 104:120].rearrange("p (k c) -> p k c", c=2)
        gs, bs = small[:, 120:128], small[:, 128:136]
        ga_, ba_ = small[:, 136:144], small[:, 144:152]
        exps = small[:, 152:160]

        ps = ctx.enter_context(nc.psum_tensor("ps", [P, 8, 512], F32))

        landed = [sem(f"landed{s}") for s in range(RING)]
        hi_ready = sem("hi_ready")
        lo_ready = [sem(f"lo_ready{s}") for s in range(RING)]
        units_begun = sem("units_begun")
        full = [sem(f"full{b}") for b in range(8)]
        emptied = [sem(f"emptied{b}") for b in range(8)]
        params_in = sem("params_in")
        inputs = sem("inputs")
        bias_in = sem("bias_in")
        cact_ready = sem("cact_ready")
        h_dve = sem("h_dve")
        h_act = sem("h_act")
        h_lo_ready = sem("h_lo_ready")
        h_own = sem("h_own")
        dve_step = sem("dve_step")
        act_step = sem("act_step")
        squared = sem("squared")
        var_ready = sem("var_ready")
        std_ready = sem("std_ready")
        centred = sem("centred")
        normed = sem("normed")
        summed = sem("summed")
        roped = sem("roped")
        qk_ready = sem("qk_ready")
        nmax_ready = sem("nmax_ready")
        exp_ready = sem("exp_ready")
        attn_ready = sem("attn_ready")
        mix_ready = sem("mix_ready")
        o_ready = sem("o_ready")
        hid_ready = sem("hid_ready")
        hid_hi_ready = sem("hid_hi_ready")
        hid_lo_ready = sem("hid_lo_ready")
        e_hi_ready = sem("e_hi_ready")
        e_lo_ready = sem("e_lo_ready")
        lam_sum = sem("lam_sum")
        mod_cols = sem("mod_cols")
        row_ready = sem("row_ready")
        row_out = sem("row_out")
        dec_in = sem("dec_in")
        block1_done = sem("block1_done")
        sdec_ready = sem("sdec_ready")
        topk_done = sem("topk_done")
        half_found = sem("half_found")
        hot1_ready = sem("hot1_ready")
        hot2_ready = sem("hot2_ready")
        plain_ready = sem("plain_ready")
        gated = sem("gated")
        final = sem("final")
        stored = sem("stored")
        pool_step = sem("pool_step")
        i2_copied = sem("i2_copied")
        gate_exp = sem("gate_exp")

        mark = {}

        def at_trip(i, per, value):
            return value if i is None else i * per + value

        def unit_hi(act, u, i=None):
            s = u % RING
            act.wait_ge(landed[s], at_trip(i, 16 * TRIP // RING, 16 * (u // RING + 1)))
            act.activation(ring_hi[:, s, :], ring[:, s, :], ACT.Copy).then_inc(hi_ready, 1)

        def unit_lo(eng, u, i=None):
            s = u % RING
            eng.wait_ge(hi_ready, at_trip(i, TRIP, SPLIT_NO[u]))
            eng.tensor_tensor(ring_lo[:, s, :], ring[:, s, :], ring_hi[:, s, :],
                              ALU.subtract).then_inc(lo_ready[s], 1)

        block = ctx.enter_context(nc.Block())

        @block.tensor
        def _(pe):
            fills = [Count() for _ in range(8)]
            n_h, n_h_lo = Count(), Count()
            n_centred, n_squared, n_summed = Count(), Count(), Count()

            def start_fill(b):
                if fills[b].i is not None:
                    assert fills[b].n > 0
                if fills[b].n:
                    pe.wait_ge(emptied[b], fills[b].now())

            def unit(u, i=None):
                s = u % RING
                pe.wait_ge(landed[s], at_trip(i, 16 * TRIP // RING, 16 * (u // RING + 1)))
                return ring[:, s, :]

            def split_unit(u, i=None):
                pe.wait_ge(hi_ready, at_trip(i, TRIP, SPLIT_NO[u]))
                return ring_hi[:, u % RING, :], ring_lo[:, u % RING, :]

            def wait_unit_lo(u, i=None):
                pe.wait_ge(lo_ready[u % RING], at_trip(i, TRIP // RING, SPLIT_IN_SLOT[u]))

            def k_tile(u, rhs, bank, i=None):
                w = unit(u, i)
                start_fill(bank)
                for kc in range(KC):
                    r = rhs(kc)
                    n = r.shape[-1]
                    m = pe.matmul(ps[:, bank, 0:n], w[:, kc * P:(kc + 1) * P], r, start=kc == 0, stop=kc == KC - 1)
                    if kc == 0:
                        m.then_inc(units_begun, 1)
                m.then_inc(full[bank], 1)
                fills[bank].add()

            def h_tile(u, h_hi, bank, i=None, first=False):
                w_hi, w_lo = split_unit(u, i)
                start_fill(bank)
                for w, x in ((w_hi, h_hi), (w_hi, h_lo), (w_lo, h_hi)):
                    if first and x is h_lo:
                        pe.wait_ge(h_lo_ready, n_h_lo.now())
                    if w is w_lo:
                        wait_unit_lo(u, i)
                    for kc in range(KC):
                        begin = w is w_hi and x is h_hi and kc == 0
                        m = pe.matmul(ps[:, bank, 0:T], w[:, kc * P:(kc + 1) * P], x[:, kc, :], start=begin,
                                      stop=w is w_lo and kc == KC - 1)
                        if begin:
                            m.then_inc(units_begun, 1)
                m.then_inc(full[bank], 1)
                fills[bank].add()

            def ones_sum(name, src, bank, n):
                start_fill(bank)
                for k in range(n):
                    r = src(k)
                    m = pe.matmul(ps[:, bank, 0:r.shape[-1]], const(name), r, start=k == 0, stop=k == n - 1)
                m.then_inc(full[bank], 1)
                fills[bank].add()

            def one(bank, lhs, rhs, shape):
                start_fill(bank)
                pe.matmul(shape, lhs, rhs, start=True, stop=True).then_inc(full[bank], 1)
                fills[bank].add()

            def wait_h():
                pe.wait_ge(h_dve, n_h.add())
                pe.wait_ge(h_act, n_h.now())
                n_h_lo.n = n_h.n - 1

            def bias_row():
                pe.wait_ge(inputs, 16 * 7)
                one(7, relb[0:32, 0:8], oneh[0:32, :], ps[0:8, 7, 0:DIST])

            pe.wait_ge(cact_ready, 1)
            def ada_rows(u, i=None, between=None):
                for g in range(2):
                    start_fill(4 + g)
                    for k4 in range(4):
                        w = unit(u + 4 * g + k4, i)
                        for k2 in range(2):
                            kc = 2 * k4 + k2
                            m = pe.matmul(ps[0:2, 4 + g, :], cact[:, kc, :], w[:, k2 * 512:(k2 + 1) * 512],
                                          start=kc == 0, stop=kc == KC - 1)
                            if k2 == 0:
                                m.then_inc(units_begun, 1)
                    m.then_inc(full[4 + g], 1)
                    fills[4 + g].add()
                if between is not None:
                    between()
                for g in range(2):
                    pe.wait_ge(emptied[4 + g], fills[4 + g].now())
                    start_fill(6 + g)
                    for q in range(4):
                        m = pe.matmul(ps[:, 6 + g, 2 * q:2 * q + 2], mod_row[0:2, g, q * P:(q + 1) * P],
                                      const("ident")[0:2, 0:2], start=True, stop=True)
                    m.then_inc(full[6 + g], 1)
                    fills[6 + g].add()

            ada_rows(FIRST_UNIT["ada0"], between=bias_row)
            with rolled(pe, EARLY_ADA // 8 - 1, [(fills[b], 1) for b in (4, 5, 6, 7)]) as i:
                ada_rows(FIRST_UNIT["ada0"] + 8, i)

            def ada_units(m):
                if m % 2 == 0:
                    start_fill(7)
                for n in (2 * m, 2 * m + 1):
                    w = unit(FIRST_UNIT["ada_late"] + n)
                    for k2 in range(2):
                        kc = 2 * (n % 4) + k2
                        t = pe.matmul(ps[0:2, 7, :], cact[:, kc, :], w[:, k2 * 512:(k2 + 1) * 512],
                                      start=kc == 0, stop=kc == KC - 1)
                        if k2 == 0:
                            t.then_inc(units_begun, 1)
                if m % 2 == 1:
                    t.then_inc(full[7], 1)
                    fills[7].add()

            def ada_columns():
                pe.wait_ge(emptied[7], fills[7].now())
                for q in range(4):
                    t = pe.matmul(ps[:, 7, 2 * q:2 * q + 2], mod_row[0:2, 0, q * P:(q + 1) * P],
                                  const("ident")[0:2, 0:2], start=True, stop=True)
                t.then_inc(full[7], 1)
                fills[7].add()

            def ada_between(m, last):
                if m % 2 == 0:
                    ada_columns()
                if m < last:
                    ada_units(m)

            def projections(src, wide):
                u = FIRST_UNIT["attn_in"]
                tile = 0
                for _ in range(8):
                    k_tile(u, lambda kc: hcat[:, kc, T:2 * T], 4 + tile % 2)
                    u, tile = u + 1, tile + 1
                for _ in range(4):
                    k_tile(u, lambda kc: hcat[:, kc, :], 4 + tile % 2)
                    u, tile = u + 1, tile + 1
                v_units(u, 4, lambda kc, tt: hcat[:, kc, tt * P:(tt + 1) * P], 4)
                u += 4
                k_tile(u, lambda kc: hcat[:, kc, :], 4 + tile % 2)
                w = unit(u + 1)
                start_fill(6)
                for tt in range(4):
                    for kc in range(KC):
                        m = pe.matmul(ps[:, 6, tt * P:(tt + 1) * P], hcat[:, kc, tt * P:(tt + 1) * P],
                                      w[:, kc * P:(kc + 1) * P], start=kc == 0, stop=kc == KC - 1)
                        if tt == 0 and kc == 0:
                            m.then_inc(units_begun, 1)
                m.then_inc(full[6], 1)
                fills[6].add()

            def v_units(u, n_units, lhs, n_tok):
                for tt in range(n_tok):
                    start_fill(tt)
                for k4 in range(4):
                    w = unit(u + k4)
                    for k2 in range(2):
                        kc = 2 * k4 + k2
                        for tt in range(n_tok):
                            m = pe.matmul(ps[:, tt, :], lhs(kc, tt), w[:, k2 * 512:(k2 + 1) * 512],
                                          start=kc == 0, stop=kc == KC - 1)
                            if k2 == 0 and tt == 0:
                                m.then_inc(units_begun, 1)
                            elif kc == KC - 1:
                                m.then_inc(full[tt], 1)
                for tt in range(n_tok):
                    fills[tt].add()

            def h_v_units(u, h_hi):
                for tt in range(2):
                    start_fill(tt)
                for k4 in range(4):
                    w_hi, w_lo = split_unit(u + k4)
                    for w, x in ((w_hi, h_hi), (w_hi, h_lo), (w_lo, h_hi)):
                        if w is w_lo:
                            wait_unit_lo(u + k4)
                        for k2 in range(2):
                            kc = 2 * k4 + k2
                            for tt in range(2):
                                begin = w is w_hi and x is h_hi
                                m = pe.matmul(ps[:, tt, :], x[:, kc, tt * P:(tt + 1) * P],
                                              w[:, k2 * 512:(k2 + 1) * 512], start=begin and kc == 0,
                                              stop=w is w_lo and kc == KC - 1)
                                if begin and k2 == 0 and tt == 0:
                                    m.then_inc(units_begun, 1)
                                elif w is w_lo and kc == KC - 1:
                                    m.then_inc(full[tt], 1)
                for tt in range(2):
                    fills[tt].add()

            n_attn, n_qk = Count(), Count()

            def attention(n_maps, scores, keys_of, at_t, values, between=None):
                for m in range(n_maps + 1):
                    if m < n_maps:
                        scores(m)
                    if between is not None:
                        between(m)
                    if m >= 1:
                        k = m - 1
                        b = 4 + k % 2
                        pe.wait_ge(attn_ready, n_attn.add())
                        start_fill(b)
                        for kt in range(keys_of(k)):
                            t = pe.transpose(ps[:, b, kt * P:(kt + 1) * P], at_t(k, kt), const("ident"))
                        t.then_inc(full[b], 1)
                        fills[b].add()
                        if k % 2 == 1:
                            pe.wait_ge(emptied[4], fills[4].now())
                            pe.wait_ge(emptied[5], fills[5].now())
                            values(k // 2)

            wait_h()
            projections(None, None)
            pe.wait_ge(emptied[4], fills[4].now())
            pe.wait_ge(emptied[5], fills[5].now())
            for f in range(2):
                one(6 + f, const("rot_2d"), zq[:, 2 * f:2 * f + 2, :], ps[:, 6 + f, :])
            for f in range(2):
                one(6 + f, const("rot_2d"), zk[:, 2 * f:2 * f + 2, T:2 * T], ps[:, 6 + f, :])
            pe.wait_ge(squared, n_squared.add(2))
            for f in range(2):
                one(6 + f, const("mean_64"), sq[:, 2 * f:2 * f + 2, :], ps[:, 6 + f, :])
            one(6, const("mean_64"), sq[:, 4:6, :], ps[:, 6, :])
            pe.wait_ge(roped, 1)
            for f in range(2):
                one(7 - f, const("rot_2d"), zq[:, 4 + 2 * f:6 + 2 * f, :], ps[:, 7 - f, :])
            one(7, const("rot_2d"), zk[:, 4, T:2 * T], ps[:, 7, 0:T])
            ada_units(0)
            ada_units(1)
            pe.wait_ge(qk_ready, n_qk.add())

            def scores_a(m):
                hd, qt = divmod(m, 2)
                for i in range(2):
                    r = slice(HEAD * i, HEAD * (i + 1))
                    b = 2 * (m % 2) + i
                    one(b, zq[r, hd, qt * P:(qt + 1) * P], zk[r, hd, :], ps[:, b, :])

            def values_a(hd):
                b = 6
                start_fill(b)
                for kt in range(4):
                    m = pe.matmul(ps[:, b, 0:T], av[:, kt, hd * P:(hd + 1) * P], attn_t[:, hd % 2, kt, :],
                                  start=kt == 0, stop=kt == 3)
                m.then_inc(full[b], 1)
                fills[b].add()

            attention(8, scores_a, lambda k: 4, lambda k, kt: attn[:, k % 2, kt * P:(kt + 1) * P], values_a,
                      lambda m: ada_between(m + 2, 28) if m < 8 else None)

            def scores_b(m):
                hd, qt = divmod(m, 2)
                jt, g = divmod(hd, 2)
                r = slice(HEAD * g, HEAD * (g + 1))
                one(m % 4, zq[r, 4 + jt, qt * P:(qt + 1) * P], zk[r, 4, :], ps[:, m % 4, :])

            def values_b(hd):
                g = hd % 2
                b = 6
                if g == 0:
                    start_fill(b)
                for kt in range(4):
                    m = pe.matmul(ps[HEAD * g:HEAD * (g + 1), b, 0:T], bv[:, kt, HEAD * g:HEAD * (g + 1)],
                                  attn_t[:, hd % 2, kt, :], start=kt == 0, stop=kt == 3)
                if g == 1:
                    m.then_inc(full[b], 1)
                    fills[b].add()

            attention(16, scores_b, lambda k: 4, lambda k, kt: attn[:, k % 2, kt * P:(kt + 1) * P], values_b,
                      lambda m: ada_between(m + 10, 26))
            pe.wait_ge(squared, n_squared.add())
            for f in range(2):
                one(6 + f, const("mean_128"), sq[:, 2 * f:2 * f + 2, :], ps[:, 6 + f, :])
            ada_units(26)
            ada_units(27)
            pe.wait_ge(mix_ready, 1)

            def out_tiles(stage, src, mark_name, to_norm=False):
                for n in range(KC):
                    if stage == "attn_out" and n == 1:
                        ada_columns()
                    if to_norm and n == KC - 1:
                        mean_half(0, 6, z, summed, n_summed)
                    k_tile(FIRST_UNIT[stage] + n, lambda kc: src[:, kc, :], 4 + n % 2)
                mark[mark_name] = (fills[4].n, fills[5].n)

            def mean_half(half, bank, src, ready, count):
                if half == 0:
                    start_fill(bank)
                pe.wait_ge(ready, count.add())
                for k in range(4 * half, 4 * half + 4):
                    m = pe.matmul(ps[:, bank, 0:T], const("mean_d"), src[:, k, :], start=k == 0, stop=k == KC - 1)
                if half == 1:
                    m.then_inc(full[bank], 1)
                    fills[bank].add()

            out_tiles("attn_out", mix, "attn_out", to_norm=True)

            def layer_norm(half_summed=False):
                if not half_summed:
                    mean_half(0, 6, z, summed, n_summed)
                mean_half(1, 6, z, summed, n_summed)
                for half in range(2):
                    mean_half(half, 7, sq, squared, n_squared)

            n_hid = Count()

            def rows_in(u, i, w_hi, w_lo, x_hi, x_lo, x_lo_ready, x_no, first, last):
                for w, x in ((w_hi, x_hi), (w_lo, x_hi), (w_hi, x_lo)):
                    if w is w_lo:
                        wait_unit_lo(u, i)
                    if x is x_lo:
                        pe.wait_ge(x_lo_ready, x_no)
                    begin, end = w is w_hi and x is x_hi, last and x is x_lo
                    for n in range(KC):
                        m = pe.matmul(ps[:, n // 2, (n % 2) * T:(n % 2 + 1) * T], w[:, n * P:(n + 1) * P], x,
                                      start=first and begin and n % 2 == 0, stop=end, skip_group_check=True)
                        if begin and n == 0:
                            m.then_inc(units_begun, 1)
                        elif end and n % 2 == 1:
                            m.then_inc(full[n // 2], 1)

            def mlp(l):
                u0 = FIRST_UNIT[f"mlp{l}"]

                def up(j_static, u, i=None, first=False):
                    h_tile(u, h_hi_1, 4 + j_static % 2, i, first)

                def down(j_static, u, i=None, first=False, last=False):
                    w_hi, w_lo = split_unit(u, i)
                    j = j_static % 2
                    pe.wait_ge(hid_hi_ready, n_hid.add())
                    if first:
                        for b in range(4):
                            start_fill(b)
                    rows_in(u, i, w_hi, w_lo, hid_hi[:, j, :], hid_lo[:, j, :], hid_lo_ready, n_hid.now(), first, last)
                    if last:
                        for b in range(4):
                            fills[b].add()

                up(0, u0, first=True)
                up(1, u0 + 1)
                down(0, u0 + 2, first=True)
                with rolled(pe, 7, [(fills[4], 2), (fills[5], 2), (n_hid, 4)]) as i:
                    for j in range(1, 5):
                        up(j + 1, u0 + 1 + 2 * j, i)
                        down(j, u0 + 2 + 2 * j, i)
                for j in (29, 30):
                    up(j + 1, u0 + 1 + 2 * j)
                    down(j, u0 + 2 + 2 * j)
                down(31, u0 + 63, last=True)

            layer_norm(half_summed=True)
            wait_h()
            mlp(0)
            layer_norm()
            wait_h()
            with rolled(pe, 3, [(fills[4], 4), (fills[5], 4)]) as i:
                for n in range(8):
                    h_tile(FIRST_UNIT["conv_in"] + n, h_hi_1, 4 + n % 2, i, n == 0)
            mark["conv_gb"] = (fills[4].n, fills[5].n)
            pe.wait_ge(mix_ready, 2)
            out_tiles("conv_out", conv_y, "conv_out", to_norm=True)
            layer_norm(half_summed=True)
            wait_h()
            mlp(1)
            layer_norm()

            def rms_norm():
                for half in range(2):
                    mean_half(half, 6, sq, squared, n_squared)

            rms_norm()
            wait_h()
            with rolled(pe, 2, [(fills[4], 4), (fills[5], 4)]) as i:
                for n in range(8):
                    h_tile(FIRST_UNIT["in2_qk"] + n, h_hi_2, 4 + n % 2, i, n == 0)
            u = FIRST_UNIT["in2_v"]
            for _ in range(3):
                h_v_units(u, h_hi_2)
                u += 4
            pe.wait_ge(emptied[4], fills[4].now())
            pe.wait_ge(emptied[5], fills[5].now())
            pe.wait_ge(squared, n_squared.add())
            def gate_tile(n, bank=None):
                h_tile(FIRST_UNIT["in2_gates"] + n, h_hi_2, 4 + n % 2 if bank is None else bank)

            for f in range(4):
                one(6 + f % 2, const("mean_64"), sq[:, 2 * f:2 * f + 2, :], ps[:, 6 + f % 2, :])
                if f >= 1:
                    gate_tile(f - 1)
            for f in range(4):
                one(6 + f % 2, const("rot_1d"), zz[:, 2 * f:2 * f + 2, :], ps[:, 6 + f % 2, :])
                gate_tile(3 + f)
            gate_tile(7)
            mark["gates"] = (fills[4].n, fills[5].n)
            pe.wait_ge(qk_ready, n_qk.add())
            for hd in range(9):
                if hd < 8:
                    r = slice(HEAD * (hd % 2), HEAD * (hd % 2 + 1))
                    b = hd % 4
                    start_fill(b)
                    pe.matmul(ps[:, b, 0:T], zz[r, 4 + hd // 2, 0:P], zz[r, hd // 2, :], start=True, stop=True)
                    pe.matmul(ps[:, b, T:T + P], zz[r, 4 + hd // 2, P:T], zz[r, hd // 2, P:T],
                              start=True, stop=True).then_inc(full[b], 1)
                    fills[b].add()
                if hd >= 1:
                    k = hd - 1
                    b = 6 + k % 2
                    pe.wait_ge(sdec_ready, k + 1)
                    start_fill(b)
                    pe.matmul(ps[:, b, 0:T], rv[:, 0, k * P:(k + 1) * P], sdec[:, k % 2, 0:T], start=True, stop=False,
                              skip_group_check=True)
                    pe.matmul(ps[:, b, P:T], rv[:, 1, k * P:(k + 1) * P], sdec[:, k % 2, T:T + P], start=False,
                              stop=True, skip_group_check=True).then_inc(full[b], 1)
                    fills[b].add()
            pe.wait_ge(o_ready, 1)
            for f in range(4):
                one(6 + f % 2, const("mean_128"), ret[:, 2 * f:2 * f + 2, :], ps[:, 6 + f % 2, :])
            gate_tile(8)
            gate_tile(9)
            pe.wait_ge(squared, n_squared.add())
            for f in range(4):
                one(6 + f % 2, const("mean_128"), sq[:, 2 * f:2 * f + 2, :], ps[:, 6 + f % 2, :])
                gate_tile(10 + f)
            gate_tile(14)
            gate_tile(15)

            def scores_m(m):
                hd, qt = divmod(m, 2)
                r = slice(HEAD * (hd % 2), HEAD * (hd % 2 + 1))
                nk = P * (qt + 1)
                one(m % 4, zz[r, 8 + hd // 2, qt * P:(qt + 1) * P], zz[r, 12 + hd // 2, 0:nk], ps[:, m % 4, 0:nk])

            def values_m(hd):
                jt, g = divmod(hd, 2)
                b = 6 + jt % 2
                if g == 0:
                    start_fill(b)
                r = slice(HEAD * g, HEAD * (g + 1))
                pe.matmul(ps[r, b, 0:T], mv[:, 0, hd * HEAD:(hd + 1) * HEAD], m_attn_t[:, hd % 2, 0, :],
                          start=True, stop=False, skip_group_check=True)
                m = pe.matmul(ps[r, b, P:T], mv[:, 1, hd * HEAD:(hd + 1) * HEAD], m_attn_t[:, hd % 2, 1, P:T],
                              start=False, stop=True, skip_group_check=True)
                if g == 1:
                    m.then_inc(full[b], 1)
                    fills[b].add()

            attention(16, scores_m, lambda k: k % 2 + 1, lambda k, kt: m_attn[:, k % 2, kt * P:(kt + 1) * P],
                      values_m, lambda m: gate_tile(16 + m // 2, 4 + m % 2) if m % 2 == 0 and m < 16 else None)
            pe.wait_ge(mix_ready, 3)
            out_tiles("ret_out", ret, "ret_out")
            pe.wait_ge(mix_ready, 4)
            for n in range(4):
                w = unit(FIRST_UNIT["moba_out"] + n)
                for half in range(2):
                    b = 4 + half
                    start_fill(b)
                    for kc in range(4):
                        m = pe.matmul(ps[:, b, 0:T], w[:, kc * T + half * P:kc * T + (half + 1) * P], att[:, kc, :],
                                      start=kc == 0, stop=kc == 3)
                        if half == 0 and kc == 0:
                            m.then_inc(units_begun, 1)
                    m.then_inc(full[b], 1)
                    fills[b].add()
            mark["moba_out"] = (fills[4].n, fills[5].n)
            pe.wait_ge(mix_ready, 5)
            out_tiles("out2", merged, "out2")
            rms_norm()
            wait_h()
            with rolled(pe, 2, [(fills[4], 4), (fills[5], 4)]) as i:
                for n in range(8):
                    h_tile(FIRST_UNIT["peer_q"] + n, h_hi_3, 4 + n % 2, i, n == 0)
            pe.wait_ge(emptied[4], fills[4].now())
            pe.wait_ge(emptied[5], fills[5].now())
            for un in range(2):
                w = unit(FIRST_UNIT["peer_keys"] + un)
                for tt in range(2):
                    for g4 in range(2):
                        b = 2 * tt + g4
                        start_fill(b)
                        for q in range(4):
                            hc = 8 * un + 4 * g4 + q
                            m = pe.matmul(ps[:, b, q * P:(q + 1) * P], qp[:, hc, tt * P:(tt + 1) * P],
                                          w[:, (hc % 8) * P:(hc % 8 + 1) * P], start=True, stop=True)
                            if tt == 0 and g4 == 0 and q == 0:
                                m.then_inc(units_begun, 1)
                        m.then_inc(full[b], 1)
                        fills[b].add()
            with rolled(pe, N_EXP // 8, [(fills[4], 4), (fills[5], 4)]) as i:
                for n in range(8):
                    h_tile(FIRST_UNIT["peer_u"] + n, h_hi_3, 4 + n % 2, i)
            mark["peer_u"] = (fills[4].n, fills[5].n)
            mark["hot"] = [fills[b].n for b in range(4)]
            pe.wait_ge(half_found, 2)
            for a in range(3):
                start_fill(6 + a % 2)
                for tt in range(2):
                    m = pe.transpose(ps[:, 6 + a % 2, tt * P:(tt + 1) * P], found[tt][:, a, :], const("ident"))
                m.then_inc(full[6 + a % 2], 1)
                fills[6 + a % 2].add()
            n_hot = Count()
            with rolled(pe, T // 16, [(fills[b], 1) for b in range(4)] + [(n_hot, 4)]) as i:
                for b in range(4):
                    pe.wait_ge(hot1_ready, n_hot.add())
                    pe.wait_ge(hot2_ready, n_hot.now())
                    start_fill(b)
                    for t in range(4):
                        m = pe.matmul(ps[:, b, t * P:(t + 1) * P], hot1[:, b, t, :], hot2[:, b, t, :],
                                      start=True, stop=True)
                    m.then_inc(full[b], 1)
                    fills[b].add()
            pe.wait_ge(gated, 1)

            def expert_rows(e, i=None, first=False, last=False):
                u = FIRST_UNIT["peer_v"] + e
                w_hi, w_lo = split_unit(u, i)
                pe.wait_ge(e_hi_ready, at_trip(i, TRIP, e + 1))
                pe.wait_ge(e_lo_ready, at_trip(i, TRIP, e + 1))
                for n in range(KC):
                    m = pe.matmul(ps[:, n, :], w_hi[:, n * P:(n + 1) * P], e_pair[:, e % 4, :], start=first,
                                  stop=False, skip_group_check=True)
                    if n == 0:
                        m.then_inc(units_begun, 1)
                wait_unit_lo(u, i)
                for n in range(KC):
                    m = pe.matmul(ps[:, n, 0:T], w_lo[:, n * P:(n + 1) * P], e_hi[:, e % 4, :], start=False,
                                  stop=last, skip_group_check=True)
                    if last:
                        m.then_inc(full[n], 1)

            for b in range(8):
                start_fill(b)
            mark["experts"] = (fills[4].n + 1, fills[5].n + 1)
            for e in range(8):
                expert_rows(e, first=e == 0)
            with rolled(pe, N_EXP // 8 - 2, []) as i:
                for e in range(8):
                    expert_rows(8 + e, i)
            for e in range(N_EXP - 8, N_EXP):
                expert_rows(e, last=e == N_EXP - 1)

        @block.scalar
        def _(act):
            drains = {4: Count(), 5: Count()}
            steps = Count()

            act.dma_start(par[:, :], params).then_inc(params_in, 16)
            for dst, src in ((relb[0:32, :], rel_bias), (oneh[0:32, :], onehot), (dmask[0:8, :], dist_mask),
                             (lamb, lam_in), (cst[:, :], consts), (resid[:, :, :], x_t), (z, ctx_t)):
                act.dma_start(dst, src).then_inc(inputs, 16)
            act.wait_ge(params_in, 16)
            act.activation(cact[:, :, :], param("c", 0, 16).rearrange("p (k c) -> p k c", c=2),
                           ACT.Silu).then_inc(cact_ready, 1)
            act.wait_ge(lam_sum, 1)
            act.activation(lam2, lam2, ACT.Exp).then_inc(act_step, 1)
            act.wait_ge(row_ready, 1)
            act.dma_start(bias_rows, rowbuf[0:8, :].unsqueeze(1).broadcast_to([8, P, DIST])).then_inc(row_out, 16)

            def drain(b, dst, func=ACT.Copy, n=T, **kw):
                act.wait_ge(full[b], drains[b].add())
                act.activation(dst, ps[:, b, 0:n], func, **kw).then_inc(emptied[b], 1)

            with rolled(act, EARLY_ADA // 8, [(drains[4], 1), (drains[5], 1)]):
                for g in range(2):
                    act.wait_ge(full[4 + g], drains[4 + g].add())
                    act.activation(mod_row[0:2, g, :], ps[0:2, 4 + g, :], ACT.Copy).then_inc(emptied[4 + g], 1)

            act.wait_ge(row_out, 16)
            toeplitz = bass.AP(bias_rows.tensor, bias_rows.offset + P - 1, [[DIST - 1, P], [P * DIST, 8], [1, T]])
            act.dma_start(bias, toeplitz).then_inc(bias_in, 16)

            n_norm, n_var, n_act_step = Count(), Count(), Count()
            n_act_step.add()

            def roots(n, k=1):
                for _ in range(k):
                    act.wait_ge(var_ready, n_var.add())
                    s = (n_var.n - 1) % 2
                    act.activation(vare[:, s, 0:n], vare[:, s, 0:n], ACT.Sqrt).then_inc(std_ready, 1)

            act.wait_ge(mod_cols, 1)
            for kc in range(KC):
                m = act.activation(hcat[:, kc, 0:T], z[:, kc, :], ACT.Identity, scale=sc1p[:, kc, 1:2],
                                   bias=mod[0][:, SH1 + kc, 1:2])
            m.then_inc(h_act, 1)
            for n in range(8):
                drain(4 + n % 2, zq[:, n, :])
            for n in range(5):
                drain(4 + n % 2, zk[:, n, :], n=2 * T)
            act.wait_ge(emptied[4], drains[4].now())
            act.activation(sq[:, 0:4, :], zq[:, 4:8, :], ACT.Square).then_inc(squared, 1)
            act.activation(sq[:, 4:6, :].rearrange("p a b -> p (a b)"), zk[:, 4, :], ACT.Square).then_inc(squared, 1)
            roots(512, 3)

            n_nmax = Count()

            def attention(n_maps, exp_of, evac_of, between=None):
                for m in range(n_maps + 1):
                    if m < n_maps:
                        act.wait_ge(nmax_ready, n_nmax.add())
                        exp_of(m)
                    if between is not None:
                        between(m)
                    if m >= 1:
                        k = m - 1
                        b = 4 + k % 2
                        act.wait_ge(full[b], drains[b].add())
                        evac_of(k, b)

            def exp_a(m):
                for i in range(2):
                    c = 2 * (m % 2) + i
                    act.activation(pexp[:, c, :], ps[:, c, :], ACT.Exp, bias=nmax[:, c:c + 1], scale=SCALE,
                                   accum_out=sums[:, c:c + 1]).then_inc(exp_ready, 1)

            def exp_b(m):
                c = m % 4
                act.activation(pexp[:, c, :], ps[:, c, :], ACT.Exp, bias=nmax[:, c:c + 1], scale=SCALE,
                               accum_out=sums[:, c:c + 1]).then_inc(exp_ready, 1)

            def evac_ab(k, b):
                hd, qt = divmod(k, 2)
                act.activation(attn_t[:, hd % 2, :, qt * P:(qt + 1) * P],
                               ps[:, b, :].rearrange("p (a b) -> p a b", a=4), ACT.Copy).then_inc(emptied[b], 1)

            attention(8, exp_a, evac_ab)
            attention(16, exp_b, evac_ab)
            act.wait_ge(o_ready, 1)
            act.activation(sq[:, 0:4, :], o_a, ACT.Square).then_inc(squared, 1)
            roots(512, 2)
            for n in range(KC):
                drain(4 + n % 2, branch[:, n, :], ACT.Identity, scale=mod[0][:, G1 + n, 0:1])

            n_centred = Count()

            def square_halves(src, ready, count):
                for half in range(2):
                    c = slice(4 * half, 4 * half + 4)
                    act.wait_ge(ready, count.add())
                    act.activation(sq[:, c, :], src[:, c, :], ACT.Square).then_inc(squared, 1)

            def norm_square():
                square_halves(zc, centred, n_centred)
                roots(T)

            def half_h(scale, bias_, h_hi):
                act.wait_ge(normed, n_norm.add())
                for kc in range(4, KC):
                    kw = {} if bias_ is None else {"bias": bias_[:, kc:kc + 1]}
                    m = act.activation(h[:, kc, :], zc[:, kc, :], ACT.Identity, scale=scale[:, kc:kc + 1], **kw)
                m.then_inc(act_step, 1)
                act.wait_ge(act_step, n_act_step.add())
                act.activation(h_hi[:, 4:8, :], h[:, 4:8, :], ACT.Copy).then_inc(h_act, 1)

            def mlp(l):
                u0 = FIRST_UNIT[f"mlp{l}"]

                def hidden(j):
                    b = 4 + j % 2
                    act.wait_ge(full[b], drains[b].add())
                    act.activation(hid[:, j % 2, :], ps[:, b, 0:T], ACT.Relu).then_inc(emptied[b], 1)
                    act.wait_ge(emptied[b], drains[b].now())
                    act.activation(hid2[:, j % 2, :], hid[:, j % 2, :], ACT.Square).then_inc(hid_ready, 1)

                with rolled(act, HID_TILES // 4, [(drains[4], 2), (drains[5], 2)]) as i:
                    for j in range(4):
                        hidden(j)
                        unit_hi(act, u0 + 2 * j + 2, i)
                        unit_hi(act, u0 + 2 * j + 3, i)

            def first_hi(stage):
                for n in range(2):
                    unit_hi(act, FIRST_UNIT[stage] + n)

            def split_and_drain(stage, n, dst, func=ACT.Copy, i=None, ahead=True):
                if ahead:
                    unit_hi(act, FIRST_UNIT[stage] + n + 2, i)
                drain(4 + n % 2, dst, func)

            first_hi("mlp0")
            norm_square()
            half_h(gs, bs, h_hi_1)
            mlp(0)
            norm_square()
            half_h(gs, bs, h_hi_1)
            with rolled(act, 2, [(drains[4], 4), (drains[5], 4)]) as i:
                for n in range(8):
                    split_and_drain("conv_in", n, conv_z[:, i * 8 + n, :], i=i)
            for n in range(16, 24):
                split_and_drain("conv_in", n, conv_z[:, n, :], ahead=n < 22)
            for n in range(KC):
                drain(4 + n % 2, branch[:, n, :], ACT.Identity, scale=mod[1][:, G1 + n, 0:1])
            first_hi("mlp1")
            norm_square()
            half_h(gs, bs, h_hi_1)
            mlp(1)
            norm_square()

            act.wait_ge(block1_done, 1)
            act.dma_start(dec, decay).then_inc(dec_in, 16)
            n_resid = Count()
            square_halves(resid, block1_done, n_resid)
            roots(T)
            half_h(param("mix_g", 0, 8), None, h_hi_2)
            with rolled(act, 2, [(drains[4], 4), (drains[5], 4)]) as i:
                for n in range(8):
                    split_and_drain("in2_qk", n, zz[:, i * 8 + n, :], i=i)
            act.wait_ge(emptied[5], drains[5].now())
            act.activation(sq, zz[:, 8:16, :], ACT.Square).then_inc(squared, 1)
            for n in range(2, 12):
                unit_hi(act, FIRST_UNIT["in2_v"] + n)
            first_hi("in2_gates")

            def gate_drain(n, func=ACT.Copy, bank=None):
                if n < 22:
                    unit_hi(act, FIRST_UNIT["in2_gates"] + n + 2)
                drain(4 + n % 2 if bank is None else bank, zz[:, 16 + n, :], func)

            roots(512, 2)
            gate_drain(0, ACT.Silu)
            roots(512)
            gate_drain(1, ACT.Silu)
            roots(512)
            for n in range(2, 8):
                gate_drain(n, ACT.Silu)
            gate_drain(8)
            act.wait_ge(centred, n_centred.add())
            act.activation(sq, zc, ACT.Square).then_inc(squared, 1)
            gate_drain(9)
            for f in range(4):
                roots(512)
                gate_drain(10 + f)
            gate_drain(14)
            gate_drain(15)

            def exp_m(m):
                hd, qt = divmod(m, 2)
                nk = P * (qt + 1)
                c = m % 2
                act.activation(m_exp[:, c, 0:nk], m_s[:, c, 0:nk], ACT.Exp, bias=nmax[:, c:c + 1],
                               accum_out=sums[:, c:c + 1]).then_inc(exp_ready, 1)

            def evac_m(k, b):
                hd, qt = divmod(k, 2)
                nt = qt + 1
                act.activation(m_attn_t[:, hd % 2, 0:nt, qt * P:(qt + 1) * P],
                               ps[:, b, 0:nt * P].rearrange("p (a b) -> p a b", a=nt), ACT.Copy).then_inc(emptied[b], 1)

            attention(16, exp_m, evac_m, lambda m: gate_drain(16 + m // 2, bank=4) if m % 2 == 0 and m < 16 else None)
            for n in range(KC):
                drain(4 + n % 2, y_a[:, n, :])
                if n in (1, 3):
                    c = slice(24 + 4 * (n - 1), 32 + 4 * (n - 1))
                    act.activation(zz[:, c, :], zz[:, c, :], ACT.Sigmoid).then_inc(gate_exp, 1)
            for n in range(KC):
                drain(4 + n % 2, y_b[:, n, :])
            for n in range(KC):
                drain(4 + n % 2, branch[:, n, :])
            first_hi("peer_q")
            square_halves(resid, block1_done, n_resid)
            roots(T)
            half_h(param("ffn_g", 0, 8), None, h_hi_3)
            with rolled(act, 1, [(drains[4], 4), (drains[5], 4)]) as i:
                for n in range(8):
                    split_and_drain("peer_q", n, qp[:, i * 8 + n, :], i=i)
            for n in range(8, 16):
                split_and_drain("peer_q", n, qp[:, n, :], ahead=n < 14)
            first_hi("peer_u")
            with rolled(act, 12, [(drains[4], 4), (drains[5], 4)]) as i:
                for n in range(8):
                    split_and_drain("peer_u", n, act_e[:, i * 8 + n, :], ACT.Gelu, i=i)
            act.wait_ge(topk_done, 1)
            for tt in range(2):
                act.activation(found[tt][:, 2, :], found[tt][:, 2, :], ACT.Exp).then_inc(gate_exp, 1)
            with rolled(act, 4, [(drains[4], 4), (drains[5], 4)]) as i:
                for n in range(8):
                    split_and_drain("peer_u", 96 + n, act_e[:, i * 8 + 96 + n, :], ACT.Gelu, i=i)
            unit_hi(act, FIRST_UNIT["peer_v"] + 2)
            act.wait_ge(topk_done, 2)
            with act.Fori(0, T // 16) as i:
                for b in range(4):
                    act.wait_ge(plain_ready, i * 4 + (b + 1))
                    for t in range(4):
                        m = act.activation(hot1[:, b, t, :], hot1[:, b, t, :], ACT.Copy,
                                           scale=gate_t[:, bass.ds(i * 16 + 4 * b + t, 1)])
                    m.then_inc(hot1_ready, 1)
            act.wait_ge(gated, 1)

            def expert_hi(e, i=None, row=None):
                if e >= 3:
                    unit_hi(act, FIRST_UNIT["peer_v"] + e, i)
                act.activation(e_hi[:, e % 4, :], act_e[:, e if row is None else row, :], ACT.Copy).then_inc(e_hi_ready, 1)

            for e in range(8):
                expert_hi(e)
            with rolled(act, N_EXP // 8 - 1, []) as i:
                for e in range(8):
                    expert_hi(8 + e, i, i * 8 + 8 + e)
            for half in range(2):
                c = slice(4 * half, 4 * half + 4)
                act.wait_ge(final, half + 1)
                act.dma_start(out[:, c, :], resid[:, c, :]).then_inc(stored, 16)
            act.wait_ge(stored, 32)

        @block.vector
        def _(dve):
            steps = Count()
            reads = {b: Count() for b in (0, 1, 2, 3, 6, 7)}

            def step(ins):
                ins.then_inc(dve_step, 1)
                steps.add()

            def settle():
                dve.wait_ge(dve_step, steps.now())

            def filled(b):
                dve.wait_ge(full[b], reads[b].add())

            def spread(a, n):
                return a.unsqueeze(1).broadcast_to([P, n, a.shape[-1]])

            n_rstd = Count()

            dve.wait_ge(params_in, 16)
            dve.wait_ge(inputs, 16 * 7)
            step(dve.tensor_tensor(lamw, lamb[:, 0:4:2, :], lamb[:, 1:4:2, :], ALU.mult))
            settle()
            dve.tensor_reduce(lam2, lamw, AX_X, ALU.add).then_inc(lam_sum, 1)
            filled(7)
            step(dve.tensor_copy(rowbuf[0:8, :], ps[0:8, 7, 0:DIST]))
            settle()
            dve.tensor_tensor(rowbuf[0:8, :], rowbuf[0:8, :], dmask[0:8, :], ALU.add).then_inc(row_ready, 1)
            dve.wait_ge(row_ready, 1)
            dve.sem_inc(emptied[7], 1)
            step(dve.tensor_scalar(gsub, param("subln_g"), 1.0 - LAM_INIT, None, ALU.mult))
            step(dve.tensor_scalar(mqg, param("mq_g"), SCALE, None, ALU.mult))
            dve.wait_ge(act_step, 1)
            step(dve.tensor_tensor(nlam, lam2[:, 1:2], lam2[:, 0:1], ALU.subtract))
            settle()
            step(dve.tensor_scalar(nlam, nlam, -LAM_INIT, None, ALU.add))

            def mod_columns(l, bank, at):
                filled(bank)
                dve.tensor_tensor(mod[l][:, bass.ds(at, 4), :], ps[:, bank, 0:8].rearrange("p (a b) -> p a b", b=2),
                                  par[:, bass.ds(PARAM[f"ada_b{l}"] + at, 4)].unsqueeze(2).broadcast_to([P, 4, 2]),
                                  ALU.add).then_inc(emptied[bank], 1)

            with rolled(dve, EARLY_ADA // 8, [(reads[6], 1), (reads[7], 1)]) as i:
                for g in range(2):
                    mod_columns(0, 6 + g, i * 8 + 4 * g)

            def late_columns(row):
                at = EARLY_ADA + 4 * row
                mod_columns(at // ADA_UNITS, 7, at % ADA_UNITS)

            def late_row():
                filled(7)
                dve.tensor_copy(mod_row[0:2, 0, :], ps[0:2, 7, :]).then_inc(emptied[7], 1)

            dve.wait_ge(emptied[7], reads[7].now())
            dve.tensor_scalar(sc1p, mod[0][:, SC1:SC1 + 8, :], 1.0, None, ALU.add).then_inc(mod_cols, 1)
            dve.wait_ge(mod_cols, 1)
            for kc in range(KC):
                m = dve.tensor_scalar(hcat[:, kc, T:2 * T], resid[:, kc, :], sc1p[:, kc, 0:1],
                                      mod[0][:, SH1 + kc, 0:1], ALU.mult, ALU.add)
            m.then_inc(h_dve, 1)
            dve.wait_ge(h_dve, 1)
            step(dve.tensor_scalar(resid[:, :, :], resid[:, :, :], ALPHA, None, ALU.mult))

            for tt in range(4):
                filled(tt)
                dve.tensor_copy(av[:, tt, :], ps[:, tt, :]).then_inc(emptied[tt], 1)
            filled(6)
            dve.tensor_copy(bv.rearrange("p a b -> p (a b)"), ps[:, 6, :]).then_inc(emptied[6], 1)

            def rope(b, zs, n, cos, sin):
                filled(b)
                ra, rb = rope_a[:, 0:n, :], rope_b[:, 0:n, :]
                dve.tensor_tensor(ra, ps[:, b, 0:n * T].rearrange("p (a b) -> p a b", a=n), spread(const(sin, T), n),
                                  ALU.mult).then_inc(emptied[b], 1)
                step(dve.tensor_tensor(rb, zs, spread(const(cos, T), n), ALU.mult))
                settle()
                step(dve.tensor_tensor(zs, ra, rb, ALU.add))
                settle()

            def variance(b, n=512):
                k = n_rstd.add()
                filled(b)
                dve.tensor_scalar(vare[:, (k - 1) % 2, 0:n], ps[:, b, 0:n], EPS, None, ALU.add).then_inc(var_ready, 1)
                dve.wait_ge(var_ready, k)
                dve.sem_inc(emptied[b], 1)
                return k

            def inverse_root(k, n=512):
                s = (k - 1) % 2
                dve.wait_ge(std_ready, k)
                step(dve.reciprocal(rstd[:, s, 0:n], vare[:, s, 0:n]))
                settle()
                return rstd[:, s, 0:n]

            def scaled_by_roots(banks, apply):
                ks = []
                for f in range(len(banks) + 1):
                    if f < len(banks):
                        ks.append(variance(banks[f]))
                    if f >= 1:
                        apply(f - 1, inverse_root(ks[f - 1]))

            for f in range(2):
                rope(6 + f, zq[:, 2 * f:2 * f + 2, :], 2, "cos_2d", "sin_2d")
            for f in range(2):
                rope(6 + f, zk[:, 2 * f:2 * f + 2, T:2 * T], 2, "cos_2d", "sin_2d")
            flat_q = zq.rearrange("p a b -> p (a b)")
            normed_b = ((flat_q[:, 1024:1536], "qn_g"), (flat_q[:, 1536:2048], "qn_g"), (zk[:, 4, :], "kn_g"))

            def norm_bqk(f, inverse):
                dst, g = normed_b[f]
                step(dve.scalar_tensor_tensor(out=dst, in0=dst, scalar=param(g), in1=inverse, op0=ALU.mult,
                                              op1=ALU.mult))

            scaled_by_roots((6, 7, 6), norm_bqk)
            settle()
            dve.sem_inc(roped, 1)
            rope(7, zq[:, 4:6, :], 2, "cos_2d", "sin_2d")
            rope(6, zq[:, 6:8, :], 2, "cos_2d", "sin_2d")
            rope(7, zk[:, 4:5, T:2 * T], 1, "cos_2d", "sin_2d")
            dve.sem_inc(qk_ready, 1)

            n_exp = Count()

            def attention(n_maps, max_of, norm_of, values_of, ada_map=None):
                for m in range(n_maps + 1):
                    if m < n_maps:
                        max_of(m)
                    n = None if ada_map is None else ada_map(m)
                    if n and n % 2 == 0:
                        late_columns(n // 2 - 1)
                    if m >= 1:
                        norm_of(m - 1)
                    if n and n % 2 == 1:
                        late_row()
                    if m >= 1:
                        if m >= 4 and m % 2 == 0:
                            values_of(m // 2 - 2)
                values_of(n_maps // 2 - 1)

            def max_a(m):
                c = 2 * (m % 2)
                for i in range(2):
                    filled(c + i)
                    step(dve.tensor_reduce(nmax[:, c + i:c + i + 1], ps[:, c + i, :], AX_X, ALU.max, negate=True))
                settle()
                dve.tensor_scalar(nmax[:, c:c + 2], nmax[:, c:c + 2], SCALE, None, ALU.mult).then_inc(nmax_ready, 1)

            def norm_a(m):
                c = 2 * (m % 2)
                dve.wait_ge(exp_ready, n_exp.add(2))
                for i in range(2):
                    dve.sem_inc(emptied[c + i], 1)
                step(dve.reciprocal(inv[:, c:c + 2], sums[:, c:c + 2]))
                settle()
                step(dve.tensor_tensor(inv[:, c + 1:c + 2], inv[:, c + 1:c + 2], nlam, ALU.mult))
                step(dve.tensor_scalar(pexp[:, c, :], pexp[:, c, :], inv[:, c:c + 1], None, ALU.mult))
                settle()
                dve.scalar_tensor_tensor(out=attn[:, m % 2, :], in0=pexp[:, c + 1, :], scalar=inv[:, c + 1:c + 2],
                                         in1=pexp[:, c, :], op0=ALU.mult, op1=ALU.add).then_inc(attn_ready, 1)

            def values_a(hd):
                b = 6
                filled(b)
                dve.tensor_copy(o_a[:, hd, :], ps[:, b, 0:T]).then_inc(emptied[b], 1)

            def max_b(m):
                c = m % 4
                filled(c)
                step(dve.tensor_reduce(nmax[:, c:c + 1], ps[:, c, :], AX_X, ALU.max, negate=True))
                settle()
                dve.tensor_scalar(nmax[:, c:c + 1], nmax[:, c:c + 1], SCALE, None, ALU.mult).then_inc(nmax_ready, 1)

            def norm_b(m):
                c = m % 4
                dve.wait_ge(exp_ready, n_exp.add())
                dve.sem_inc(emptied[c], 1)
                step(dve.reciprocal(inv[:, c:c + 1], sums[:, c:c + 1]))
                settle()
                dve.tensor_scalar(attn[:, m % 2, :], pexp[:, c, :], inv[:, c:c + 1], None,
                                  ALU.mult).then_inc(attn_ready, 1)

            def values_b(hd):
                if hd % 2 == 0:
                    return
                jt = hd // 2
                filled(6)
                dve.tensor_copy(mix[:, 4 + jt, :], ps[:, 6, 0:T]).then_inc(emptied[6], 1)

            late_row()
            attention(8, max_a, norm_a, values_a, lambda m: m + 2 if m < 8 else None)
            dve.wait_ge(emptied[6], reads[6].n)
            dve.sem_inc(o_ready, 1)
            attention(16, max_b, norm_b, values_b, lambda m: m + 10)
            flat_o, flat_m = o_a.rearrange("p a b -> p (a b)"), mix.rearrange("p a b -> p (a b)")

            def norm_o(f, inverse):
                c = slice(512 * f, 512 * (f + 1))
                step(dve.scalar_tensor_tensor(out=flat_m[:, c], in0=flat_o[:, c], scalar=gsub, in1=inverse,
                                              op0=ALU.mult, op1=ALU.mult))

            scaled_by_roots((6, 7), norm_o)
            settle()
            dve.sem_inc(mix_ready, 1)
            late_row()
            late_columns(2 * (ADA_UNITS // 4) - EARLY_ADA // 4 - 1)

            def wait_branch(name):
                dve.wait_ge(emptied[4], mark[name][0])
                dve.wait_ge(emptied[5], mark[name][1])

            def fold(ln, md, sc, sh):
                g, b = param("ln_g", 8 * ln, 8), param("ln_b", 8 * ln, 8)
                dve.wait_ge(h_act, n_hact.now())
                step(dve.tensor_scalar(ga_, g, ALPHA, None, ALU.mult))
                step(dve.tensor_scalar(ba_, b, ALPHA, None, ALU.mult))
                step(dve.tensor_scalar(exps, mod[md][:, sc:sc + 8, 0], 1.0, None, ALU.add))
                settle()
                step(dve.tensor_tensor(gs, g, exps, ALU.mult))
                step(dve.tensor_tensor(bs, b, exps, ALU.mult))
                settle()
                step(dve.tensor_tensor(bs, bs, mod[md][:, sh:sh + 8, 0], ALU.add))

            def half_h(scale, bias_, h_hi):
                for kc in range(4):
                    if bias_ is None:
                        m = dve.tensor_scalar(h[:, kc, :], zc[:, kc, :], scale[:, kc:kc + 1], None, ALU.mult)
                    else:
                        m = dve.tensor_scalar(h[:, kc, :], zc[:, kc, :], scale[:, kc:kc + 1], bias_[:, kc:kc + 1],
                                              ALU.mult, ALU.add)
                m.then_inc(h_own, 1)
                dve.wait_ge(h_own, n_h_own.add())
                dve.tensor_copy(h_hi[:, 0:4, :], h[:, 0:4, :]).then_inc(h_dve, 1)
                dve.wait_ge(h_dve, n_h_own.n + 1)
                dve.tensor_tensor(h_lo[:, 0:4, :], h[:, 0:4, :], h_hi[:, 0:4, :], ALU.subtract)
                dve.wait_ge(h_act, n_hact.add())
                dve.tensor_tensor(h_lo[:, 4:8, :], h[:, 4:8, :], h_hi[:, 4:8, :],
                                  ALU.subtract).then_inc(h_lo_ready, 1)

            def centre():
                filled(6)
                for c in (slice(0, 4), slice(4, 8)):
                    dve.tensor_tensor(zc[:, c, :], z[:, c, :], spread(ps[:, 6, 0:T], 4),
                                      ALU.subtract).then_inc(centred, 1)

            n_cent, n_hact, n_h_own = Count(), Count(), Count()
            n_hact.add()

            def layer_norm(to_h):
                centre()
                dve.wait_ge(centred, n_cent.add(2))
                dve.sem_inc(emptied[6], 1)
                normalise(variance(7, T), zc, to_h)
                if to_h:
                    half_h(gs, bs, h_hi_1)
                    for kc in range(KC):
                        step(dve.tensor_scalar(resid[:, kc, :], zc[:, kc, :], ga_[:, kc:kc + 1], ba_[:, kc:kc + 1],
                                               ALU.mult, ALU.add))
                    settle()

            def normalise(k, src, to_h=True):
                r = spread(inverse_root(k, T), 4)
                dve.tensor_tensor(zc[:, 4:8, :], src[:, 4:8, :], r, ALU.mult).then_inc(normed if to_h else dve_step, 1)
                if not to_h:
                    steps.add()
                step(dve.tensor_tensor(zc[:, 0:4, :], src[:, 0:4, :], r, ALU.mult))
                settle()

            def mixer_norm(l, name):
                fold(2 * l, l, SC2, SH2)
                for half in range(2):
                    for b in (4, 5):
                        dve.wait_ge(emptied[b], mark[name][b - 4] - 2 * (1 - half))
                    if half == 0:
                        settle()
                    c = slice(4 * half, 4 * half + 4)
                    dve.tensor_tensor(z[:, c, :], branch[:, c, :], resid[:, c, :], ALU.add).then_inc(summed, 1)
                layer_norm(True)

            def mlp_norm(l):
                if l == 0:
                    fold(1, 1, SC1, SH1)
                    settle()
                for n in range(KC):
                    b = n // 2
                    if n % 2 == 0:
                        filled(b)
                    m = dve.scalar_tensor_tensor(out=z[:, n, :], in0=ps[:, b, (n % 2) * T:(n % 2 + 1) * T],
                                                 scalar=mod[l][:, G2 + n, 0:1], in1=resid[:, n, :],
                                                 op0=ALU.mult, op1=ALU.add)
                    if n % 4 == 3:
                        m.then_inc(summed, 1)
                    elif n % 2 == 1:
                        m.then_inc(emptied[b], 1)
                dve.wait_ge(summed, 4 * l + 4)
                dve.sem_inc(emptied[1], 1)
                dve.sem_inc(emptied[3], 1)
                layer_norm(l == 0)

            n_hid = Count()

            def split_hidden(u0):
                def hidden(j):
                    dve.wait_ge(hid_ready, n_hid.add())
                    dve.tensor_copy(hid_hi[:, j % 2, :], hid2[:, j % 2, :]).then_inc(hid_hi_ready, 1)
                    dve.wait_ge(hid_hi_ready, n_hid.now())
                    dve.tensor_tensor(hid_lo[:, j % 2, :], hid2[:, j % 2, :], hid_hi[:, j % 2, :],
                                      ALU.subtract).then_inc(hid_lo_ready, 1)

                with rolled(dve, 7, [(n_hid, 4)]) as i:
                    for j in range(4):
                        hidden(j)
                        unit_lo(dve, u0 + 2 * j + 2, i)
                for j in range(28, 32):
                    hidden(j)
                    if j < 31:
                        unit_lo(dve, u0 + 2 * j + 2)

            mixer_norm(0, "attn_out")
            split_hidden(FIRST_UNIT["mlp0"])
            mlp_norm(0)
            step(dve.memset(conv_u[:, :, 0:1], 0.0))
            step(dve.memset(conv_u[:, :, T + 1:T + 2], 0.0))
            dve.wait_ge(emptied[4], mark["conv_gb"][0] - 4)
            dve.wait_ge(emptied[5], mark["conv_gb"][1] - 4)
            step(dve.tensor_tensor(conv_u[:, :, 1:T + 1], conv_z[:, 0:8, :], conv_z[:, 8:16, :], ALU.mult))
            settle()
            for kc in range(KC):
                step(dve.tensor_scalar(conv_y[:, kc, :], conv_u[:, kc, 0:T], param("conv_w", kc), param("conv_b", kc),
                                       ALU.mult, ALU.add))
            for tap in (1, 2):
                settle()
                for kc in range(KC):
                    step(dve.scalar_tensor_tensor(out=conv_y[:, kc, :], in0=conv_u[:, kc, tap:tap + T],
                                                  scalar=param("conv_w", 8 * tap + kc), in1=conv_y[:, kc, :],
                                                  op0=ALU.mult, op1=ALU.add))
            settle()
            wait_branch("conv_gb")
            dve.tensor_tensor(conv_y, conv_y, conv_z[:, 16:24, :], ALU.mult).then_inc(mix_ready, 1)
            mixer_norm(1, "conv_out")
            split_hidden(FIRST_UNIT["mlp1"])
            mlp_norm(1)
            for kc in range(KC):
                m = dve.tensor_scalar(resid[:, kc, :], zc[:, kc, :], param("ln_g", 24 + kc), param("ln_b", 24 + kc),
                                      ALU.mult, ALU.add)
                if kc % 4 == 3:
                    m.then_inc(block1_done, 1)

            n_b1 = Count()

            def rms_norm(g, h_hi):
                dve.wait_ge(block1_done, n_b1.add(2))
                normalise(variance(6, T), resid)
                half_h(param(g, 0, 8), None, h_hi)

            rms_norm("mix_g", h_hi_2)
            for v in range(3):
                for tt in range(2):
                    dst = rv[:, tt, 512 * v:512 * (v + 1)] if v < 2 else mv[:, tt, :]
                    filled(tt)
                    dve.tensor_copy(dst, ps[:, tt, :]).then_inc(emptied[tt], 1)
            flat_z = zz.rearrange("p a b -> p (a b)")

            def norm_mqk(f, inverse):
                dst = flat_z[:, 2048 + 512 * f:2048 + 512 * (f + 1)]
                step(dve.scalar_tensor_tensor(out=dst, in0=dst, scalar=mqg if f < 2 else param("mk_g"), in1=inverse,
                                              op0=ALU.mult, op1=ALU.mult))

            scaled_by_roots((6, 7, 6, 7), norm_mqk)
            for f in range(4):
                rope(6 + f % 2, zz[:, 2 * f:2 * f + 2, :], 2, "cos_1d", "sin_1d")
            dve.sem_inc(qk_ready, 1)
            dve.wait_ge(dec_in, 16)

            def ret_copy(hd):
                b = 6 + hd % 2
                filled(b)
                dve.tensor_copy(ret[:, hd, :], ps[:, b, 0:T]).then_inc(emptied[b], 1)

            for hd in range(8):
                b = hd % 4
                filled(b)
                dve.tensor_tensor(sdec[:, hd % 2, :], ps[:, b, 0:DEC], dec[:, hd, :], ALU.mult).then_inc(sdec_ready, 1)
                dve.wait_ge(sdec_ready, hd + 1)
                dve.sem_inc(emptied[b], 1)
                if hd >= 1:
                    ret_copy(hd - 1)
            ret_copy(7)
            dve.wait_ge(emptied[7], reads[7].n)
            dve.sem_inc(o_ready, 1)
            flat_r, flat_c = ret.rearrange("p a b -> p (a b)"), zc.rearrange("p a b -> p (a b)")
            for f in range(4):
                filled(6 + f % 2)
                c = slice(512 * f, 512 * (f + 1))
                dve.tensor_tensor(flat_c[:, c], flat_r[:, c], ps[:, 6 + f % 2, :], ALU.subtract).then_inc(
                    emptied[6 + f % 2], 1)
            dve.wait_ge(emptied[7], reads[7].n)
            dve.sem_inc(centred, 1)
            n_cent.add()
            wait_branch("gates")

            def norm_ret(f, inverse):
                c = slice(512 * f, 512 * (f + 1))
                step(dve.tensor_tensor(flat_c[:, c], flat_c[:, c], inverse, ALU.mult))
                settle()
                step(dve.tensor_tensor(flat_r[:, c], flat_c[:, c], flat_z[:, 4096 + 512 * f:4096 + 512 * (f + 1)],
                                       ALU.mult))

            scaled_by_roots((6, 7, 6, 7), norm_ret)
            settle()
            dve.sem_inc(mix_ready, 1)

            dve.wait_ge(bias_in, 16)

            def max_m(m):
                hd, qt = divmod(m, 2)
                nk = P * (qt + 1)
                filled(m % 4)
                dve.tensor_tensor(m_s[:, m % 2, 0:nk], ps[:, m % 4, 0:nk], bias[:, hd, T - nk:T],
                                  ALU.add).then_inc(emptied[m % 4], 1)
                dve.wait_ge(emptied[m % 4], reads[m % 4].n)
                dve.tensor_reduce(nmax[:, m % 2:m % 2 + 1], m_s[:, m % 2, 0:nk], AX_X, ALU.max,
                                  negate=True).then_inc(nmax_ready, 1)

            def norm_m(m):
                nk = P * (m % 2 + 1)
                c = m % 2
                dve.wait_ge(exp_ready, n_exp.add())
                step(dve.reciprocal(inv[:, c:c + 1], sums[:, c:c + 1]))
                settle()
                dve.tensor_scalar(m_attn[:, c, 0:nk], m_exp[:, c, 0:nk], inv[:, c:c + 1], None,
                                  ALU.mult).then_inc(attn_ready, 1)

            def values_m(hd):
                if hd % 2 == 0:
                    return
                jt = hd // 2
                filled(6 + jt % 2)
                m = dve.tensor_copy(att[:, jt, :], ps[:, 6 + jt % 2, 0:T])
                m.then_inc(emptied[6 + jt % 2], 1)

            attention(16, max_m, norm_m, values_m)
            dve.wait_ge(emptied[7], reads[7].n)
            dve.sem_inc(mix_ready, 1)
            wait_branch("ret_out")
            step(dve.tensor_tensor(y_a, y_a, zz[:, 24:32, :], ALU.mult))
            wait_branch("moba_out")
            step(dve.tensor_tensor(y_b, y_b, zz[:, 32:40, :], ALU.mult))
            settle()
            dve.tensor_tensor(merged, y_a, y_b, ALU.add).then_inc(mix_ready, 1)
            for half in range(2):
                for b in (4, 5):
                    dve.wait_ge(emptied[b], mark["out2"][b - 4] - 2 * (1 - half))
                c = slice(4 * half, 4 * half + 4)
                dve.tensor_tensor(resid[:, c, :], resid[:, c, :], branch[:, c, :], ALU.add).then_inc(block1_done, 1)
            rms_norm("ffn_g", h_hi_3)

            for un in range(2):
                for tt in range(2):
                    for g4 in range(2):
                        b = 2 * tt + g4
                        filled(b)
                        hc = 8 * un + 4 * g4
                        dve.tensor_copy(sco[:, tt, hc:hc + 4, :].rearrange("p a b -> p (a b)"),
                                        ps[:, b, :]).then_inc(emptied[b], 1)
            for b in range(4):
                dve.wait_ge(emptied[b], reads[b].n)

            def top16(vals, idx, src, n):
                for r in range(n):
                    step(dve.max(vals(r)[:, 0:8], src(r)))
                settle()
                for r in range(n):
                    step(dve.max_index(idx(r)[:, 0:8], vals(r)[:, 0:8], src(r)))
                settle()
                for r in range(n):
                    step(dve.match_replace(src(r), vals(r)[:, 0:8], src(r), TAKEN))
                settle()
                for r in range(n):
                    step(dve.max(vals(r)[:, 8:16], src(r)))
                settle()
                for r in range(n):
                    step(dve.max_index(idx(r)[:, 8:16], vals(r)[:, 8:16], src(r)))
                settle()

            v16 = top_v.rearrange("p h c k -> p (h c) k")
            i16 = top_i.rearrange("p h c k -> p (h c) k")
            bu = best_u.rearrange("p (h k) -> p h k", h=8)
            hot4 = hot.rearrange("p (h k) a -> p h k a", h=8)
            cand4 = cand.rearrange("p h (a b) -> p h a b", a=TOPK)
            for tt in range(2):
                top16(lambda r: v16[:, r, :], lambda r: top_iu[:, r, :], lambda r: sco[:, tt, r, :], 16)
                step(dve.tensor_copy(i16, top_iu))
                for hd in range(8):
                    step(dve.tensor_tensor(cand4[:, hd], top_v[:, hd, 0, :].unsqueeze(2).broadcast_to([P, TOPK, TOPK]),
                                           top_v[:, hd, 1, :].unsqueeze(1).broadcast_to([P, TOPK, TOPK]), ALU.add))
                settle()
                top16(lambda r: best_v[:, r, :], lambda r: bu[:, r, :], lambda r: cand[:, r, :], 8)
                for c, (op, by) in enumerate(((ALU.logical_shift_right, 4), (ALU.bitwise_and, 15))):
                    step(dve.tensor_scalar(pick_u, best_u, by, None, op))
                    settle()
                    step(dve.tensor_copy(pick, pick_u))
                    settle()
                    step(dve.tensor_tensor(hot, pick.unsqueeze(2).broadcast_to([P, P, TOPK]),
                                           spread(const("iota16", TOPK), P), ALU.is_equal))
                    settle()
                    for hd in range(8):
                        step(dve.tensor_tensor(hot4[:, hd], hot4[:, hd], spread(top_i[:, hd, c, :], TOPK), ALU.mult))
                    settle()
                    step(dve.tensor_reduce(found[tt][:, c, :], hot, AX_X, ALU.add))
                    settle()
                gates = found[tt][:, 2, :].rearrange("p (h k) -> p h k", h=8)
                step(dve.tensor_tensor(gates, best_v, best_v[:, :, 0:1].broadcast_to([P, 8, TOPK]), ALU.subtract))
            settle()
            dve.sem_inc(topk_done, 1)
            for tt in range(2):
                gates = found[tt][:, 2, :].rearrange("p (h k) -> p h k", h=8)
                dve.wait_ge(gate_exp, 2 + tt + 1)
                step(dve.tensor_reduce(exps, gates, AX_X, ALU.add))
                settle()
                step(dve.reciprocal(exps, exps))
                settle()
                dve.tensor_tensor(gates, gates, exps.unsqueeze(2).broadcast_to([P, 8, TOPK]),
                                  ALU.mult).then_inc(half_found, 1)
                dve.wait_ge(half_found, tt + 1)
            for a, dst in enumerate((i1_t, i2_t, gate_t)):
                filled(6 + a % 2)
                m = dve.tensor_copy(dst, ps[:, 6 + a % 2, 0:T])
                m.then_inc(emptied[6 + a % 2], 1)
            for b in (6, 7):
                dve.wait_ge(emptied[b], reads[b].n)
            dve.sem_inc(topk_done, 1)

            def one_hots(b, t0):
                k = POOL_TOKENS[b]
                dve.tensor_tensor(hot2[:, b, k:4, :], spread(const("iota"), 4 - k),
                                  i2_t[:, bass.ds(t0 + k, 4 - k)].unsqueeze(2).broadcast_to([P, 4 - k, P]), ALU.is_equal)
                dve.tensor_tensor(hot1[:, b], spread(const("iota"), 4),
                                  i1_t[:, bass.ds(t0, 4)].unsqueeze(2).broadcast_to([P, 4, P]),
                                  ALU.is_equal).then_inc(plain_ready, 1)

            def gate(b, t0):
                filled(b)
                a = act_e[:, :, bass.ds(t0, 4)]
                dve.tensor_tensor(a, a, ps[:, b, :].rearrange("p (t e) -> p e t", t=4), ALU.mult).then_inc(emptied[b], 1)

            dve.wait_ge(emptied[4], mark["peer_u"][0])
            dve.wait_ge(emptied[5], mark["peer_u"][1])
            for b in range(3):
                one_hots(b, 4 * b)
            with rolled(dve, T // 16 - 1, [(reads[b], 1) for b in range(4)]) as i:
                for b in range(4):
                    one_hots((b + 3) % 4, i * 16 + 4 * (b + 3))
                    gate(b, i * 16 + 4 * b)
            one_hots(3, T - 4)
            for b in range(4):
                gate(b, T - 16 + 4 * b)
            for b in range(4):
                dve.wait_ge(emptied[b], reads[b].n)
            dve.sem_inc(gated, 1)

            def expert_lo(e, i=None, row=None):
                dve.wait_ge(e_hi_ready, at_trip(i, TRIP, e + 1))
                dve.tensor_tensor(e_lo[:, e % 4, :], act_e[:, e if row is None else row, :], e_hi[:, e % 4, :],
                                  ALU.subtract).then_inc(e_lo_ready, 1)
                if e % 2 == 0:
                    unit_lo(dve, FIRST_UNIT["peer_v"] + e, i)

            for e in range(8):
                expert_lo(e)
            with rolled(dve, N_EXP // 8 - 1, []) as i:
                for e in range(8):
                    expert_lo(8 + e, i, i * 8 + 8 + e)
            for half in range(2):
                c = slice(4 * half, 4 * half + 4)
                for b in range(4 * half, 4 * half + 4):
                    if b in (4, 5):
                        dve.wait_ge(full[b], mark["experts"][b - 4])
                    else:
                        filled(b)
                step(dve.tensor_tensor(resid[:, c, :], resid[:, c, :], ps[:, c, 0:T], ALU.add))
                settle()
                dve.tensor_tensor(resid[:, c, :], resid[:, c, :], ps[:, c, T:2 * T], ALU.add).then_inc(final, 1)

        @block.gpsimd
        def _(pool):
            def units_lo(stage, trips, which=range(TRIP)):
                with pool.Fori(0, trips) as i:
                    for n in which:
                        unit_lo(pool, FIRST_UNIT[stage] + n, i)

            odd = range(1, TRIP, 2)
            unit_lo(pool, FIRST_UNIT["mlp0"])
            units_lo("mlp0", 8, odd)
            units_lo("conv_in", 3)
            unit_lo(pool, FIRST_UNIT["mlp1"])
            units_lo("mlp1", 8, odd)
            units_lo("in2_qk", 6)
            for n in range(20, 24):
                unit_lo(pool, FIRST_UNIT["in2_gates"] + n)
            units_lo("peer_q", 2)
            units_lo("peer_u", 16)
            pool.wait_ge(topk_done, 2)
            with pool.Fori(0, T // 16) as i:
                for b in range(4):
                    pool.wait_ge(full[b], i + mark["hot"][b])
                    pool.tensor_copy(i2_now[:, b, :], i2_t[:, bass.ds(i * 16 + 4 * b, 4)]).then_inc(pool_step, 1)
                    pool.wait_ge(pool_step, i * 4 + (1 + b))
                    pool.sem_inc(i2_copied, 1)
                    for t in range(POOL_TOKENS[b]):
                        m = pool.tensor_scalar(hot2[:, b, t, :], const("iota"), i2_now[:, b, t:t + 1], None,
                                               ALU.is_equal)
                    m.then_inc(hot2_ready, 1)
            units_lo("peer_v", 16, odd)

        @block.sync
        def _(sp):
            def load(v, s):
                sp.dma_start(ring[:, s, :], stream[v]).then_inc(landed[s], 16)

            for s in range(RING):
                load(s, s)
            with sp.Fori(1, N_UNITS // RING) as r:
                for s in range(RING):
                    sp.wait_ge(units_begun, r * RING + (s + 2 - RING))
                    load(r * RING + s, s)
            for v in range(N_UNITS // RING * RING, N_UNITS):
                sp.wait_ge(units_begun, v + 2 - RING)
                load(v, v % RING)


def _constants():
    c = np.zeros((P, N_CONST), np.float32)

    def put(name, a):
        c[:, CONST[name]:CONST[name] + a.shape[1]] = a

    put("ident", np.eye(P))
    put("mean_d", np.full((P, P), 1.0 / D))
    put("mean_64", np.kron(np.eye(2), np.full((HEAD, HEAD), 1.0 / HEAD)))
    put("mean_128", np.full((P, P), 1.0 / P))
    f = np.arange(HEAD)

    def rotation(half):
        r = np.zeros((HEAD, HEAD))
        first = f % (2 * half) < half
        r[f[first], f[first] + half] = -1.0
        r[f[~first], f[~first] - half] = 1.0
        return np.kron(np.eye(2), r).T

    put("rot_2d", rotation(HEAD // 4))
    put("rot_1d", rotation(HEAD // 2))
    put("iota", np.tile(np.arange(P), (P, 1)))
    put("iota16", np.tile(np.arange(TOPK), (P, 1)))
    t = np.arange(T)
    nf = HEAD // 4
    inv_freq = np.float32(10000.0) ** (-np.arange(nf, dtype=np.float32) / nf)
    where = np.stack([t // 64, t % 64]).astype(np.float32)
    ang = (where[f // 32] * inv_freq[f % nf][:, None]).astype(np.float32)
    put("cos_2d", np.tile(np.cos(ang), (2, 1)))
    put("sin_2d", np.tile(np.sin(ang), (2, 1)))
    half = HEAD // 2
    inv = np.float32(10000.0) ** (-np.arange(half, dtype=np.float32) / half)
    ang = (t[None].astype(np.float32) * inv[f % half][:, None]).astype(np.float32)
    put("cos_1d", np.tile(np.cos(ang), (2, 1)))
    put("sin_1d", np.tile(np.sin(ang), (2, 1)))
    return c


def _decay():
    log_g = np.log1p(-np.exp2(-5.0 - np.arange(8)))
    rel = np.arange(T)[None, :] - np.arange(P)[:, None]
    d = np.where(rel[:, None, :] >= 0, np.exp(np.maximum(rel, 0)[:, None, :] * log_g[None, :, None]), 0.0) * SCALE
    return np.concatenate([d, d[:, :, 0:P]], axis=2).astype(np.float32)


def _distances():
    import math
    dist = 255 - np.arange(DIST)
    n = np.maximum(dist, 0)
    nf = np.maximum(n, 1).astype(np.float32)
    large = 16 + (np.log(nf / np.float32(16)) / np.float32(math.log(2048 / 16)) * np.float32(16)).astype(np.int32)
    bucket = np.where(n < 16, n, np.minimum(large, 31))
    onehot = (np.arange(32)[:, None] == bucket[None]).astype(np.float32)
    mask = np.where(dist < 0, np.float32(MASKED), np.float32(0.0))
    return onehot, np.tile(mask, (8, 1)).astype(np.float32)


def _units(a):
    def tiles(w):
        return w.reshape(KC, P, -1, P).transpose(2, 1, 0, 3).reshape(-1, P, UNIT)

    def wide(w):
        return w.reshape(4, 2, P, -1, 512).transpose(3, 0, 2, 1, 4).reshape(-1, P, UNIT)

    def mlp(w1, w2):
        up, down = tiles(w1), w2.reshape(HID_TILES, P, UNIT)
        body = np.stack([up[1:], down[:-1]], axis=1).reshape(-1, P, UNIT)
        return [up[:1], body, down[-1:]]

    w = a["attn_w_in"][0]
    aq, ak, v, bq, bk, bvw = np.split(w, [512, 1024, 1536, 2048, 2176], axis=1)
    bq = bq.reshape(D, 2, 4, HEAD).transpose(0, 2, 1, 3).reshape(D, 512)
    wo = a["attn_w_out"][0]
    wo_b = wo[512:].reshape(2, 4, HEAD, D).transpose(1, 0, 2, 3).reshape(512, D)
    w2 = a["w_in_2"][0]
    rq, rk, rvw, rg, mq, mk, mvw, ga, gb = np.split(w2, np.cumsum([512, 512, 1024, 1024, 512, 512, 512, 1024]), axis=1)
    gate_b, gate_c, xv = np.split(a["conv_w_in"][0], 3, axis=1)
    keys = a["peer_sub_keys_2"][0].reshape(16, N_EXP, P)
    u = a["peer_u_2"][0].reshape(N_EXP, N_EXP, KC, P)
    return [
        wide(a["ada_w"][0])[:EARLY_ADA],
        tiles(aq), tiles(bq), tiles(ak), wide(v), tiles(bk), tiles(bvw),
        wide(a["ada_w"][0])[EARLY_ADA:], wide(a["ada_w"][1]),
        tiles(np.concatenate([wo[:512], wo_b])), *mlp(a["mlp_w1"][0], a["mlp_w2"][0]),
        tiles(gate_c), tiles(xv), tiles(gate_b), tiles(a["conv_w_out"][0]), *mlp(a["mlp_w1"][1], a["mlp_w2"][1]),
        tiles(rq), tiles(rk), tiles(mq), tiles(mk), wide(rvw), wide(mvw), tiles(rg), tiles(ga), tiles(gb),
        tiles(a["ret_w_branch_2"][0]),
        a["moba_w_branch_2"][0].reshape(4, P, 4, 2 * P).transpose(2, 1, 0, 3).reshape(-1, P, UNIT),
        tiles(a["w_out_2"][0]), tiles(a["peer_w_q_2"][0]),
        keys.transpose(2, 0, 1).reshape(P, 2, UNIT).transpose(1, 0, 2),
        u.transpose(1, 3, 2, 0).reshape(N_EXP, P, UNIT),
        a["peer_v_2"][0].reshape(N_EXP, N_EXP, UNIT).transpose(1, 0, 2),
    ]


def _params(a):
    def cols(v):
        return np.ascontiguousarray(v).reshape(-1, P).T

    twice = lambda v: np.tile(v.reshape(-1), 2).reshape(P, 1)
    c = np.stack([a["c"][0], a["c_ctx"]], axis=-1).reshape(KC, P, 2).transpose(1, 0, 2).reshape(P, 16)
    parts = [c, cols(a["ada_b"][0]), cols(a["ada_b"][1]), cols(a["ln_g"]), cols(a["ln_b"]), cols(a["mix_norm_g_2"]),
             cols(a["ffn_norm_g_2"]), cols(a["conv_w"]), cols(a["conv_b"]), a["diff_subln_g"].reshape(P, 1),
             twice(a["q_norm_g"]), twice(a["k_norm_g"]), twice(a["moba_q_gain_2"]), twice(a["moba_k_gain_2"])]
    return np.ascontiguousarray(np.concatenate(parts, axis=1))


def kernel(**inputs):
    import concourse.bacc as bacc
    from concourse.bass_utils import run_bass_kernel_spmd

    a = {k: np.asarray(v) for k, v in inputs.items()}
    parts = _units(a)
    stream = np.empty((N_UNITS, P, UNIT), np.float32)
    at = 0
    for p in parts:
        stream[at:at + len(p)] = p
        at += len(p)
    assert at == N_UNITS

    def features(v):
        return np.ascontiguousarray(v.reshape(T, KC, P).transpose(2, 1, 0))

    onehot, dist_mask = _distances()
    arrays = {
        "stream": stream, "x_t": features(a["x"]), "ctx_t": features(a["ctx"]), "params": _params(a),
        "consts": _constants(), "decay": _decay(),
        "lam_in": np.ascontiguousarray(np.broadcast_to(a["diff_lambda"], (P, 4, HEAD))),
        "rel_bias": np.ascontiguousarray(a["rel_bias_2"]), "onehot": onehot, "dist_mask": dist_mask,
    }
    nc = bacc.Bacc("TRN2", target_bir_lowering=False, num_devices=1)
    args = [nc.dram_tensor(n, v.shape, F32, kind="ExternalInput").ap() for n, v in arrays.items()]
    bias_rows = nc.dram_tensor("bias_rows", (8, P, DIST), F32).ap()
    out = nc.dram_tensor("out", (P, KC, T), F32, kind="ExternalOutput").ap()
    build(nc, *args, bias_rows, out)
    r = run_bass_kernel_spmd(nc, [arrays], core_ids=[0])
    y = r.results[0]["out"]
    return np.ascontiguousarray(y.transpose(2, 1, 0)).reshape(1, T, D)
```
